# Optimizing a Trainium2 kernel written in Bass

```python
import math
import jax
import jax.numpy as jnp
from jax import lax
import numpy as np

D_MODEL = 1024
BATCH = 1
SEQ = 256
DEPTH = 1
DEC_BATCH = 8
DEC_SEQ = 4
PAST_LEN = 2048
PAGE_SIZE = 128

SSD_HEAD_DIM = 64
SSD_D_INNER = D_MODEL
SSD_HEADS = SSD_D_INNER // SSD_HEAD_DIM
SSD_GROUPS = 2
SSD_HEADS_PER_GROUP = SSD_HEADS // SSD_GROUPS
SSD_STATE = 128
SSD_CONV = 4
SSD_CHUNK = 128
SSD_CONV_DIM = SSD_D_INNER + 2 * SSD_GROUPS * SSD_STATE
S5_WIDTH = D_MODEL // 2
S5_GROUP_CH = 16
S5_GROUPS = S5_WIDTH // S5_GROUP_CH
S5_STATE = 64
N_BRANCHES = 2
IN_Z = SSD_D_INNER
IN_XBC = SSD_CONV_DIM
IN_DT = SSD_HEADS
IN_U = S5_WIDTH
IN_GATE = N_BRANCHES * D_MODEL
IN_TOTAL = IN_Z + IN_XBC + IN_DT + IN_U + IN_GATE
IN_SPLITS = (IN_Z, IN_Z + IN_XBC, IN_Z + IN_XBC + IN_DT, IN_Z + IN_XBC + IN_DT + IN_U)
N_EXPERTS = 16
N_EXPERT_GROUPS = 4
EXPERTS_PER_GROUP = N_EXPERTS // N_EXPERT_GROUPS
TOP_K = 2
D_EXPERT = 512
EPS = 1e-6

kernel_name = 'hybrid_ssd_s5_moe_step'

def rmsnorm(x, w):
    xf = x.astype(jnp.float32)
    y = xf * lax.rsqrt(jnp.mean(xf * xf, axis=-1, keepdims=True) + EPS)
    return (y * w.astype(jnp.float32)).astype(x.dtype)

def causal_dwconv(xbc, conv_buf, w, b):
    L = xbc.shape[1]
    xp = jnp.concatenate([conv_buf.astype(xbc.dtype), xbc], axis=1)
    y = b + xp[:, 0:L] * w[0]
    for k in range(1, SSD_CONV):
        y = y + xp[:, k:k + L] * w[k]
    return y, xp[:, L:]

def segsum_exp(a_cs):
    q = a_cs.shape[-1]
    diff = a_cs[..., :, None] - a_cs[..., None, :]
    mask = jnp.tril(jnp.ones((q, q), dtype=bool))
    return jnp.where(mask, jnp.exp(jnp.where(mask, diff, 0.0)), 0.0)

def ssd_scan(x, dt, a, bm, cm, h0):
    b, L = x.shape[:2]
    Q = SSD_CHUNK if L % SSD_CHUNK == 0 else L
    nc = L // Q
    G, R, P, N = SSD_GROUPS, SSD_HEADS_PER_GROUP, SSD_HEAD_DIM, SSD_STATE
    X = (x * dt[..., None]).reshape(b, nc, Q, G, R, P)
    a_cs = jnp.cumsum(jnp.moveaxis((dt * a).reshape(b, nc, Q, G, R), 2, -1), axis=-1)
    Bc = bm.reshape(b, nc, Q, G, N)
    Cc = cm.reshape(b, nc, Q, G, N)
    CB = jnp.einsum('bcqgn,bcsgn->bcgqs', Cc, Bc)
    y_diag = jnp.einsum('bcgqs,bcgrqs,bcsgrp->bcqgrp', CB, segsum_exp(a_cs), X)
    decay_to_end = jnp.exp(a_cs[..., -1:] - a_cs)
    chunk_states = jnp.einsum('bcsgn,bcgrs,bcsgrp->bcgrpn', Bc, decay_to_end, X)
    chunk_decay = jnp.exp(a_cs[..., -1])

    def step(h, inp):
        s, d = inp
        return h * d[..., None, None] + s, h

    h_final, h_prev = lax.scan(step, h0.reshape(b, G, R, P, N),
                               (jnp.moveaxis(chunk_states, 1, 0), jnp.moveaxis(chunk_decay, 1, 0)))
    h_prev = jnp.moveaxis(h_prev, 0, 1)
    y_off = jnp.einsum('bcqgn,bcgrpn,bcgrq->bcqgrp', Cc, h_prev, jnp.exp(a_cs))
    y = (y_diag + y_off).reshape(b, L, SSD_HEADS, P)
    return y, h_final.reshape(b, SSD_HEADS, P, N)

def ssd_branch(z, xbc, dt_raw, conv_buf, ssm_h0, conv_w, conv_b, dt_bias, a_log, d_skip, norm_w, w_out_a):
    f32 = jnp.float32
    b, L = z.shape[:2]
    xbc, new_conv = causal_dwconv(xbc, conv_buf, conv_w, conv_b)
    xbc = jax.nn.silu(xbc.astype(f32))
    xs, bm, cm = jnp.split(xbc, [SSD_D_INNER, SSD_D_INNER + SSD_GROUPS * SSD_STATE], axis=-1)
    xs = xs.reshape(b, L, SSD_HEADS, SSD_HEAD_DIM)
    dt = jax.nn.softplus(dt_raw.astype(f32) + dt_bias.astype(f32))
    a = -jnp.exp(a_log.astype(f32))
    y, new_ssm = ssd_scan(xs, dt, a, bm.reshape(b, L, SSD_GROUPS, SSD_STATE),
                          cm.reshape(b, L, SSD_GROUPS, SSD_STATE), ssm_h0.astype(f32))
    y = y + d_skip.astype(f32)[:, None] * xs
    y = y.reshape(b, L, SSD_D_INNER) * jax.nn.silu(z.astype(f32))
    yg = y.reshape(b, L, SSD_GROUPS, SSD_D_INNER // SSD_GROUPS)
    yg = yg * lax.rsqrt(jnp.mean(yg * yg, axis=-1, keepdims=True) + EPS)
    y = yg.reshape(b, L, SSD_D_INNER) * norm_w.astype(f32)
    return y.astype(z.dtype) @ w_out_a, new_conv, new_ssm

def s5_branch(u, h0_re, h0_im, a_re, a_im, log_dt, b_re, b_im, c_re, c_im, d_skip, w_glu):
    f32 = jnp.float32
    b, L = u.shape[:2]
    a_re, a_im = a_re.astype(f32), a_im.astype(f32)
    dt = jnp.exp(log_dt.astype(f32))[:, None]
    mag = jnp.exp(dt * a_re)
    ab_re, ab_im = mag * jnp.cos(dt * a_im), mag * jnp.sin(dt * a_im)
    den = a_re * a_re + a_im * a_im
    f_re = ((ab_re - 1.0) * a_re + ab_im * a_im) / den
    f_im = (ab_im * a_re - (ab_re - 1.0) * a_im) / den
    b_re, b_im = b_re.astype(f32), b_im.astype(f32)
    bb_re = f_re[..., None] * b_re - f_im[..., None] * b_im
    bb_im = f_re[..., None] * b_im + f_im[..., None] * b_re
    uf = u.astype(f32)
    ug = uf.reshape(b, L, S5_GROUPS, S5_GROUP_CH)
    x_re = jnp.einsum('gsc,blgc->blgs', bb_re, ug)
    x_im = jnp.einsum('gsc,blgc->blgs', bb_im, ug)
    h0_re, h0_im = h0_re.astype(f32), h0_im.astype(f32)
    x_re = x_re.at[:, 0].add(ab_re * h0_re - ab_im * h0_im)
    x_im = x_im.at[:, 0].add(ab_re * h0_im + ab_im * h0_re)

    def combine(e1, e2):
        a1r, a1i, b1r, b1i = e1
        a2r, a2i, b2r, b2i = e2
        return (a2r * a1r - a2i * a1i, a2r * a1i + a2i * a1r,
                a2r * b1r - a2i * b1i + b2r, a2r * b1i + a2i * b1r + b2i)

    _, _, h_re, h_im = lax.associative_scan(
        combine, (jnp.broadcast_to(ab_re, x_re.shape), jnp.broadcast_to(ab_im, x_im.shape), x_re, x_im), axis=1)
    y = (jnp.einsum('gcs,blgs->blgc', c_re.astype(f32), h_re)
         - jnp.einsum('gcs,blgs->blgc', c_im.astype(f32), h_im)).reshape(b, L, S5_WIDTH)
    y = y + d_skip.astype(f32) * uf
    pre = (jax.nn.gelu(y).astype(u.dtype) @ w_glu).astype(f32)
    out = pre[..., :D_MODEL] * jax.nn.sigmoid(pre[..., D_MODEL:])
    return out.astype(u.dtype), h_re[:, -1], h_im[:, -1]

def moe_ffn(h, w_router, b_router, w1, w3, w2):
    f32 = jnp.float32
    b, L, d = h.shape
    t = h.reshape(b * L, d)
    scores = jax.nn.softmax(t.astype(f32) @ w_router.astype(f32), axis=-1)
    sel = scores + b_router.astype(f32)
    grp_score = lax.top_k(sel.reshape(-1, N_EXPERT_GROUPS, EXPERTS_PER_GROUP), TOP_K)[0].sum(-1)
    best_grp = jnp.argmax(grp_score, axis=-1)
    in_grp = (jnp.arange(N_EXPERTS) // EXPERTS_PER_GROUP)[None, :] == best_grp[:, None]
    _, idx = lax.top_k(jnp.where(in_grp, sel, -jnp.inf), TOP_K)
    wts = jnp.take_along_axis(scores, idx, axis=-1)
    wts = wts / jnp.sum(wts, axis=-1, keepdims=True)
    comb = jnp.sum(jax.nn.one_hot(idx, N_EXPERTS, dtype=f32) * wts[..., None], axis=1).astype(h.dtype)
    y = jnp.zeros_like(t)
    for e in range(N_EXPERTS):
        act = jax.nn.silu(t @ w1[e]) * (t @ w3[e])
        y = y + comb[:, e:e + 1] * (act @ w2[e])
    return y.reshape(b, L, d)

def setup_inputs(seed: int = 0) -> dict:
    key = jax.random.key(seed)
    ks = iter(jax.random.split(key, 48))
    f32 = jnp.float32

    def nrm(shape, s):
        return jax.random.normal(next(ks), shape, f32) * s

    def gain(shape):
        return 1.0 + nrm(shape, 0.02)

    x_prompt = nrm((BATCH, SEQ, D_MODEL), 1.0)
    x_sample = nrm((DEC_BATCH, DEC_SEQ, D_MODEL), 1.0)
    state_ssm = nrm((DEPTH, DEC_BATCH, SSD_HEADS, SSD_HEAD_DIM, SSD_STATE), 0.1)
    state_conv = nrm((DEPTH, DEC_BATCH, SSD_CONV - 1, SSD_CONV_DIM), 1.0)
    state_s5_re = nrm((DEPTH, DEC_BATCH, S5_GROUPS, S5_STATE), 0.5)
    state_s5_im = nrm((DEPTH, DEC_BATCH, S5_GROUPS, S5_STATE), 0.5)
    c_prompt = nrm((BATCH, D_MODEL), 1.0)
    c_sample = nrm((DEC_BATCH, D_MODEL), 1.0)

    w_in = nrm((DEPTH, D_MODEL, IN_TOTAL), D_MODEL ** -0.5)
    conv_w = nrm((DEPTH, SSD_CONV, SSD_CONV_DIM), SSD_CONV ** -0.5)
    conv_b = nrm((DEPTH, SSD_CONV_DIM), 0.01)
    dt0 = jnp.exp(jax.random.uniform(next(ks), (DEPTH, SSD_HEADS), f32, math.log(1e-3), math.log(1e-1)))
    dt_bias = dt0 + jnp.log(-jnp.expm1(-dt0))
    a_log = jnp.log(jax.random.uniform(next(ks), (DEPTH, SSD_HEADS), f32, 1.0, 16.0))
    d_ssd = gain((DEPTH, SSD_HEADS))
    ssd_norm_w = gain((DEPTH, SSD_D_INNER))
    w_out_a = nrm((DEPTH, SSD_D_INNER, D_MODEL), SSD_D_INNER ** -0.5)

    n = jnp.arange(S5_STATE, dtype=f32)
    s5_a_re = -0.5 + nrm((DEPTH, S5_GROUPS, S5_STATE), 0.01)
    s5_a_im = jnp.pi * n + nrm((DEPTH, S5_GROUPS, S5_STATE), 0.01)
    s5_log_dt = jax.random.uniform(next(ks), (DEPTH, S5_GROUPS), f32, math.log(1e-3), math.log(1e-1))
    s5_b_re = nrm((DEPTH, S5_GROUPS, S5_STATE, S5_GROUP_CH), (2 * S5_GROUP_CH) ** -0.5)
    s5_b_im = nrm((DEPTH, S5_GROUPS, S5_STATE, S5_GROUP_CH), (2 * S5_GROUP_CH) ** -0.5)
    s5_c_re = nrm((DEPTH, S5_GROUPS, S5_GROUP_CH, S5_STATE), (2 * S5_STATE) ** -0.5)
    s5_c_im = nrm((DEPTH, S5_GROUPS, S5_GROUP_CH, S5_STATE), (2 * S5_STATE) ** -0.5)
    s5_d = nrm((DEPTH, S5_WIDTH), 1.0)
    w_glu = nrm((DEPTH, S5_WIDTH, 2 * D_MODEL), S5_WIDTH ** -0.5)
    w_out = nrm((DEPTH, D_MODEL, D_MODEL), D_MODEL ** -0.5)

    norm1_w = gain((DEPTH, D_MODEL))
    norm2_w = gain((DEPTH, D_MODEL))
    w_ada = nrm((DEPTH, D_MODEL, 6 * D_MODEL), 0.5 * D_MODEL ** -0.5)
    b_ada = nrm((DEPTH, 6 * D_MODEL), 0.02)
    w_router = nrm((D_MODEL, N_EXPERTS), D_MODEL ** -0.5)
    b_router = nrm((N_EXPERTS,), 0.01)
    w1 = nrm((DEPTH, N_EXPERTS, D_MODEL, D_EXPERT), D_MODEL ** -0.5)
    w3 = nrm((DEPTH, N_EXPERTS, D_MODEL, D_EXPERT), D_MODEL ** -0.5)
    w2 = nrm((DEPTH, N_EXPERTS, D_EXPERT, D_MODEL), D_EXPERT ** -0.5)
    final_norm_w = gain((D_MODEL,))
    return {'x_prompt': x_prompt, 'x_sample': x_sample,
            'state_ssm': state_ssm, 'state_conv': state_conv,
            'state_s5_re': state_s5_re, 'state_s5_im': state_s5_im,
            'c_prompt': c_prompt, 'c_sample': c_sample,
            'w_in': w_in, 'conv_w': conv_w, 'conv_b': conv_b, 'dt_bias': dt_bias, 'a_log': a_log,
            'd_ssd': d_ssd, 'ssd_norm_w': ssd_norm_w, 'w_out_a': w_out_a,
            's5_a_re': s5_a_re, 's5_a_im': s5_a_im, 's5_log_dt': s5_log_dt,
            's5_b_re': s5_b_re, 's5_b_im': s5_b_im, 's5_c_re': s5_c_re, 's5_c_im': s5_c_im,
            's5_d': s5_d, 'w_glu': w_glu, 'w_out': w_out,
            'norm1_w': norm1_w, 'norm2_w': norm2_w, 'w_ada': w_ada, 'b_ada': b_ada,
            'w_router': w_router, 'b_router': b_router, 'w1': w1, 'w3': w3, 'w2': w2,
            'final_norm_w': final_norm_w}

def reference(x_prompt, x_sample, state_ssm, state_conv, state_s5_re, state_s5_im, c_prompt, c_sample,
              w_in, conv_w, conv_b, dt_bias, a_log, d_ssd, ssd_norm_w, w_out_a,
              s5_a_re, s5_a_im, s5_log_dt, s5_b_re, s5_b_im, s5_c_re, s5_c_im, s5_d, w_glu, w_out,
              norm1_w, norm2_w, w_ada, b_ada, w_router, b_router, w1, w3, w2, final_norm_w):
    f32 = jnp.float32

    def mixer(h, l, conv0, ssm0, s5r0, s5i0):
        b, L = h.shape[:2]
        z, xbc, dt_raw, u, gate_raw = jnp.split(h @ w_in[l], IN_SPLITS, axis=-1)
        ya, new_conv, new_ssm = ssd_branch(z, xbc, dt_raw, conv0, ssm0, conv_w[l], conv_b[l], dt_bias[l],
                                           a_log[l], d_ssd[l], ssd_norm_w[l], w_out_a[l])
        yb, new_re, new_im = s5_branch(u, s5r0, s5i0, s5_a_re[l], s5_a_im[l], s5_log_dt[l], s5_b_re[l],
                                       s5_b_im[l], s5_c_re[l], s5_c_im[l], s5_d[l], w_glu[l])
        g = jax.nn.sigmoid(gate_raw.astype(f32)).reshape(b, L, N_BRANCHES, D_MODEL)
        merged = g[..., 0, :] * ya.astype(f32) + g[..., 1, :] * yb.astype(f32)
        return merged.astype(h.dtype) @ w_out[l], new_conv, new_ssm, new_re, new_im

    def trunk(x, c, conv0, ssm0, s5r0, s5i0):
        convs, ssms, res, ims = [], [], [], []
        for l in range(DEPTH):
            mod = (jax.nn.silu(c) @ w_ada[l] + b_ada[l])[:, None, :]
            sh1, sc1, g1, sh2, sc2, g2 = jnp.split(mod, 6, axis=-1)
            h = rmsnorm(x, norm1_w[l]) * (1 + sc1) + sh1
            mix, cv, sm, sr, si = mixer(h, l, conv0[l], ssm0[l], s5r0[l], s5i0[l])
            x = x + g1 * mix
            h = rmsnorm(x, norm2_w[l]) * (1 + sc2) + sh2
            x = x + g2 * moe_ffn(h, w_router, b_router, w1[l], w3[l], w2[l])
            convs.append(cv)
            ssms.append(sm)
            res.append(sr)
            ims.append(si)
        return rmsnorm(x, final_norm_w), jnp.stack(ssms), jnp.stack(convs), jnp.stack(res), jnp.stack(ims)

    zero_conv = jnp.zeros((DEPTH, x_prompt.shape[0], SSD_CONV - 1, SSD_CONV_DIM), x_prompt.dtype)
    zero_ssm = jnp.zeros((DEPTH, x_prompt.shape[0], SSD_HEADS, SSD_HEAD_DIM, SSD_STATE), f32)
    zero_s5 = jnp.zeros((DEPTH, x_prompt.shape[0], S5_GROUPS, S5_STATE), f32)
    y_prompt, ssm_p, conv_p, s5re_p, s5im_p = trunk(x_prompt, c_prompt, zero_conv, zero_ssm, zero_s5, zero_s5)
    y_sample, ssm_s, conv_s, s5re_s, s5im_s = trunk(x_sample, c_sample, state_conv, state_ssm,
                                                    state_s5_re, state_s5_im)
    return (y_prompt, y_sample,
            ssm_p.astype(state_ssm.dtype), ssm_s.astype(state_ssm.dtype),
            conv_p.astype(state_conv.dtype), conv_s.astype(state_conv.dtype),
            s5re_p.astype(state_s5_re.dtype), s5re_s.astype(state_s5_re.dtype),
            s5im_p.astype(state_s5_im.dtype), s5im_s.astype(state_s5_im.dtype))


_drawn_inputs = setup_inputs


def setup_inputs(seed=0):
    import zlib

    import numpy as np

    out = dict(_drawn_inputs(seed))
    spreads = {}
    factors = {'conv_b': 4.027,
     'd_ssd': 5.392,
     'ssd_norm_w': 3.769,
     's5_a_re': 3.981,
     'final_norm_w': 2.947}
    for name, (base, spread) in spreads.items():
        noise = np.random.default_rng([zlib.crc32(name.encode()), seed]).standard_normal(out[name].shape)
        drawn = base * np.exp(spread * noise) if base else spread * noise
        out[name] = jnp.asarray(drawn.astype(out[name].dtype))
    for name, factor in factors.items():
        out[name] = (out[name] * factor).astype(out[name].dtype)
    return out
```

```python
from contextlib import ExitStack

import concourse.bass as bass
from concourse import mybir

F32 = mybir.dt.float32
I32 = mybir.dt.int32
ALU = mybir.AluOpType
ACT = mybir.ActivationFunctionType
AX_X = mybir.AxisListType.X

P = 128
BANK = 512
D = 1024
KD = D // P
NBATCH, LSAMP = 8, 4
TP, TS = 256, NBATCH * LSAMP
T = TP + TS
CH = 128
CHUNKS = [(0, 128), (128, 128), (256, 32)]
NC = 1 + NBATCH
H, HD, NS = 16, 64, 128
G = 2
CONV = 4
XBC = D + 2 * G * NS
XT = XBC // P
S5G, S5N, S5C = 32, 64, 16
S5T = S5G * S5N // P
UT = S5G * S5C // P
NE, NG, EPG = 16, 4, 4
FE = 512
FT = FE // P
CAP = 64
PAIRS = NE // 2
MAXPASS = -(-T // CAP)
EPS = 1e-6
IN_XBC, IN_DT, IN_U, IN_GATE = D, D + XBC, D + XBC + H, D + XBC + H + S5G * S5C
TWO_PI = 6.283185307179586
TWO_PI_HI = 6.28125
ROUND = 12582912.0
PI_IN = 3.1415925
BIG = 1e30

SLOT = 4096
NR = 5
MOE_SLOTS = [3, 4, 0, 1, 2, 5]
U_ADA1, U_U, U_XBC, U_Z, U_GATE, U_GLU, U_ADA2, U_OUTA, U_OUT, N_UNITS = 0, 4, 5, 8, 10, 14, 16, 24, 26, 28


def uses(slot):
    return len([n for n in range(N_UNITS) if n % NR == slot])


def ada_unit(i):
    return U_ADA1 + i if i < 4 else U_ADA2 + i - 4


def hybrid_decoder_step(nc, a, o):
    with ExitStack() as ctx:
        def sb(name, cols, dt=F32):
            return ctx.enter_context(nc.sbuf_tensor(name, [P, cols], dt))

        def sem(name):
            return ctx.enter_context(nc.semaphore(name))

        def part(region, off, *shape):
            n = 1
            for s in shape:
                n *= s
            v = region[:, off:off + n]
            if len(shape) == 2:
                return v.rearrange("p (a b) -> p a b", b=shape[1])
            if len(shape) == 3:
                return v.rearrange("p (a b c) -> p a b c", b=shape[1], c=shape[2])
            return v

        ring = sb("ring", NR * SLOT)
        tok_r = sb("tok_region", 3 * D)
        xT = part(sb("x_features", KD * T), 0, KD, T)
        hT_r = sb("h_region", KD * T)
        hT = part(hT_r, 0, KD, T)
        u_r = sb("u_region", UT * T)
        uT = part(u_r, 0, UT, T)
        xbc_r = sb("xbc_region", XT * T)
        xbcT = part(xbc_r, 0, XT, T)
        z_r = sb("z_region", KD * T)
        zT = part(z_r, 0, KD, T)
        gate_r = sb("gate_region", 2 * KD * T)
        gates = part(gate_r, 0, 2 * KD, T)
        mix_r = sb("mixer_region", 13312)
        conv_r = sb("conv_region", 2 * 315)

        x_tok = part(tok_r, 0, 3, D)
        s5x = part(tok_r, 0, 2, S5T, TS)
        s5h = part(tok_r, 2 * S5T * TS, 2, S5T, TS)
        Xdt = part(tok_r, 0, 3, D)

        c_in = part(gate_r, 0, D)
        prow1 = part(gate_r, 1024, P)
        prow2 = part(gate_r, 1152, P)
        prow3 = part(gate_r, 1280, P)
        b_raw = part(gate_r, 1408, 2, S5T, S5C)
        c_raw = part(gate_r, 1920, 2, UT, S5N)
        st_rows = part(gate_r, 2432, 2, P)
        exp_in = part(gate_r, 2688, 4)
        conv_in = part(gate_r, 2692, XBC)
        n1v, n1y, n1t = (part(z_r, k * T, T) for k in range(3))
        nv, ny, nt = (part(u_r, k * T, T) for k in range(3))
        sq = part(conv_r, 0, 2, T)
        rows = part(conv_r, 0, 2, 315)

        rotc = part(mix_r, 0, S5T, TP)
        rots = part(mix_r, S5T * TP, S5T, TP)
        off = 2 * S5T * TP
        bT = part(mix_r, off, 2, UT, P)
        cTs5 = part(mix_r, off + 1024, 2, UT, P)
        g5 = part(mix_r, off + 2048, 4, TP)
        h5 = part(mix_r, off + 3072, 4, TP)
        pt = part(mix_r, off + 4096, 2, TP)
        bblk = part(z_r, 3 * T, 2, S5T, 2 * S5C)
        cblk = part(gate_r, 0, 2, UT, P)
        vt = part(conv_r, 0, 2, TP)
        Xs = part(mix_r, 0, 3, D)
        B_tok = part(mix_r, 3072, 3, 2 * NS)
        CBm = part(mix_r, 3840, 2, T)
        CTs = part(mix_r, 4416, 4, CH)
        h1T = part(mix_r, 4928, 2, 512)
        hfT = part(mix_r, 5952, 2, 512)
        h0 = part(mix_r, 6976, 2, NBATCH * NS)
        h0T = part(mix_r, 9024, 2, NBATCH * NS)
        Bm = part(mix_r, 11072, 2, NBATCH * NS)
        MT = part(hT_r, 0, 4, T)
        h_out = part(hT_r, 1152, 8, P)

        cT = part(sb("c_features", KD * 32), 0, KD, 32)
        ada_s = part(sb("ada_sum", 512), 0, 512)
        mod = part(sb("modulation", 48 * NC), 0, 48, NC)
        amul = part(sb("norm_scale", KD * NC), 0, KD, NC)
        ident = sb("ident", P)
        ones = sb("ones", P)
        upper = sb("upper", P)
        strict = sb("strict", P)
        same_r = sb("same_sequence", TS)
        supper_r = sb("same_upper", TS)
        blk = sb("sequence_of", NBATCH)
        sel9 = sb("fold_rows", 32)
        par8 = sb("group_rows", 8)
        par2 = sb("group_parity", 2)
        iota = sb("slot_number", CAP)
        keyg = sb("group_key", NG)
        keye = sb("expert_key", NE)
        pc1 = sb("params1", 104)
        pc2 = sb("params2", 80)
        pc3 = sb("params3", 16)
        cs_r = sb("conv_state", XT * 24)
        csT = part(cs_r, 0, XT, 24)
        tails = part(sb("conv_tails", XT * 27), 0, XT, 27)
        w_dt = part(sb("w_dt", KD * H), 0, KD, H)
        w_rt = part(sb("w_router", KD * NE), 0, KD, NE)
        dtb = sb("dt_bias_row", H)
        alog = sb("a_log_row", H)
        brt = sb("b_router_row", NE)
        dt3 = part(sb("dt", 3 * H), 0, 3, H)
        da3 = part(sb("dta", 3 * H), 0, 3, H)
        dtt = part(sb("dt_tmp", 3 * H), 0, 3, H)
        dte = part(sb("decay_to_end", 3 * H), 0, 3, H)
        acs = part(sb("a_cumsum", 3 * 2 * H), 0, 3, 2 * H)
        eft = part(u_r, 3 * T, KD, TS)
        yoff = part(cs_r, 0, KD, TS)
        s5c = part(tok_r, 2048, 24, S5T)
        st5_flat = tok_r[:, 2432:2432 + 2 * P]
        st5 = part(tok_r, 2432, 2, NBATCH, S5T)
        fin5 = part(tok_r, 2688, 2, S5T)
        npf = sb("passes_f", 8)
        npi = sb("passes_i", 1, I32)

        ps = ctx.enter_context(nc.psum_tensor("psum", [P, 8, BANK], F32))

        nw1, nw2, ssdw = pc1[:, 0:8], pc1[:, 8:16], pc1[:, 16:24]
        convw = pc1[:, 24:72].rearrange("p (k j) -> p k j", j=XT)
        convb, s5d, fnw, dskip = pc1[:, 72:84], pc1[:, 84:88], pc1[:, 88:96], pc1[:, 96:104]
        b_ada, a_re, a_im = pc2[:, 0:48], pc2[:, 48:64], pc2[:, 64:80]

        ld_x, ld_c, ld_par, ld_exp, ld_state5, ld_conv, ld_bc, ld_rows, ld_wdt, ld_wrt = (
            sem(n) for n in ("ld_x", "ld_c", "ld_par", "ld_exp", "ld_state5", "ld_conv", "ld_bc", "ld_rows", "ld_wdt", "ld_wrt"))
        ld_h0 = [sem("ld_h0_even"), sem("ld_h0_odd")]
        landed = [sem(f"ring_landed{i}") for i in range(NR + 1)]
        unit_used = sem("unit_used")
        consts = sem("consts")
        vconsts = sem("vector_consts")
        dte_pre, q_msk, sm_in, sm_exp = sem("dte_pre"), sem("q_masked"), sem("softmax_in"), sem("softmax_exp")
        pos_dn, yo_done = sem("positions_down"), sem("yo_done")
        expd = sem("expanded")
        c_silu, cT_ps, cT_ok = sem("c_silu"), sem("cT_ps"), sem("cT_ok")
        par_ps, par_ok = sem("par_ps"), sem("par_ok")
        x_ps, x_ok, xt_free = sem("x_ps"), sem("x_ok"), sem("x_tok_free")
        sq_ok, sq_used = sem("sq_ok"), sem("sq_used")
        var_ok, rs_ok = sem("var_ok"), sem("rs_ok")
        ada_cp, adaT_ps, mod_ok = sem("ada_cp"), sem("adaT_ps"), sem("mod_ok")
        xn_ok, amul_ok, hm_ok = sem("x_normed"), sem("norm_scale_ok"), sem("h_sample_scaled")
        h_ok, hp_ok = sem("h_sample_ok"), sem("h_prompt_ok")
        tile_ps, tile_ev = sem("tile_ps"), sem("tile_ev")
        conv_acc, conv_ok = sem("conv_acc"), sem("conv_ok")
        dt_ps, dt_pre, dt_exp, da_ok = sem("dt_ps"), sem("dt_pre"), sem("dt_exp"), sem("da_ok")
        tail_ps, tail_cp = sem("tail_ps"), sem("tail_cp")
        dsc, trig, rot_u, rot_ok = sem("s5_discrete"), sem("s5_trig"), sem("rot_u"), sem("rot_ok")
        blk5, s5w_ps, s5w_ok = sem("s5_blocks"), sem("s5w_ps"), sem("s5w_ok")
        s5_x, s5_xused, s5_g, s5_h, s5_hused = sem("s5_x"), sem("s5_x_used"), sem("s5_g"), sem("s5_h"), sem("s5_h_used")
        s5_y, s5_yev, s5_hs = sem("s5_y"), sem("s5_y_ev"), sem("s5_hs")
        gelu_ok = sem("gelu_ok")
        s5f_ps, s5f_cp = sem("s5f_ps"), sem("s5f_cp")
        glu_ps, glu_sig, glu_ev = sem("glu_ps"), sem("glu_sig"), sem("glu_ev")
        cb_ps, cb_ok, acs_ps, acs_ok, dte_ok = sem("cb_ps"), sem("cb_ok"), sem("acs_ps"), sem("acs_ok"), sem("dte_ok")
        xt_ps, xdt_ok, xs_ok, bt_ok = sem("xt_ps"), sem("xdt_ok"), sem("xs_ok"), sem("bt_ok")
        st_ps, h1_ok, hf_ok, hf_ps, hf_cp = sem("st_ps"), sem("h1_ok"), sem("hf_ok"), sem("hf_ps"), sem("hf_cp")
        h0_ps, h0_cp, yo_ps, ss_ps, ss_ok, ss_out = sem("h0_ps"), sem("h0_cp"), sem("yo_ps"), sem("ss_ps"), sem("ss_ok"), sem("ss_out")
        q_ps, q_diff, q_exp, q_mt, q_y, q_yev = sem("q_ps"), sem("q_diff"), sem("q_exp"), sem("q_mt"), sem("q_y"), sem("q_yev")
        bm_ok, ca_ps, yn_ok = sem("bm_ok"), sem("ca_ps"), sem("yn_ok")
        outa_ps, mrg_ok = sem("outa_ps"), sem("merged_ok")
        mix_ps, x1_ok = sem("mix_ps"), sem("x1_ok")
        h2t_ps, h2t_ok = sem("h2t_ps"), sem("h2t_ok")
        lg_ps, top_ok, pos_ps, route_ok = sem("logits_ps"), sem("top_ok"), sem("pos_ps"), sem("route_ok")
        selo_ok, selw_ok, xe_ok = sem("chosen"), sem("weights_chosen"), sem("xe_ok")
        xg_ps = [sem("gathered_first_half"), sem("gathered_second_half")]
        act_s, act_ok = sem("act_silu"), sem("act_ok")
        aT_ps, aT_ok, pT_ps, pT_ok = sem("aT_ps"), sem("aT_ok"), sem("pT_ps"), sem("pT_ok")
        w2_ps, ye_ok, cmb_ps, cmb_ok = sem("w2_ps"), sem("ye_ok"), sem("combine_ps"), sem("combine_ok")
        x2_ok, fin_ok, fin_ps, fin_cp = sem("x2_ok"), sem("fin_ok"), sem("fin_ps"), sem("fin_cp")
        st_conv, st_s5, st_hp, st_y = sem("st_conv"), sem("st_s5"), sem("st_ssm_prompt"), sem("st_y")
        st_hs = [sem("st_ssm_even"), sem("st_ssm_odd")]
        dve_chain, act_chain, pool_chain = sem("dve_chain"), sem("act_chain"), sem("pool_chain")

        def linker(eng, chain):
            n = [0]

            def link(ins):
                n[0] += 1
                ins.then_inc(chain, 1)
                eng.wait_ge(chain, n[0])
            return link

        def ring_tile(slot, k):
            base = ring[:, slot * SLOT:(slot + 1) * SLOT] if slot < NR else mix_r[:, 0:SLOT]
            return base.rearrange("p (k n) -> p k n", k=k)

        def unit_tile(n, k):
            return ring_tile(n % NR, k)

        def turned(i, c0, c1):
            bank, at = (6, 0) if i < 4 else (1, P)
            return ps[:, bank, at + c0 * NC:at + c1 * NC]

        def sample(v):
            return v.rearrange("p (b l) -> p b l", l=LSAMP)

        h2_tok = part(tok_r, 0, 3, D)
        y_tok = part(tok_r, 0, 3, D)
        yacc = part(xbc_r, 0, KD, T)
        selw = part(xbc_r, KD * T, 3, 2, CAP)
        selw2 = selw.rearrange("p c e s -> p c (e s)")
        selo = part(xbc_r, KD * T + 384, 3, 2, CAP)
        selo2 = selo.rearrange("p c e s -> p c (e s)")
        Xe = part(gate_r, 0, KD, P)
        hs_ = part(gate_r, 1024, FE)
        act_e = part(gate_r, 1536, FE)
        actT = part(gate_r, 2048, FT, P)
        y_e = part(gate_r, 2560, D)
        pT = part(gate_r, 3584, T)
        r_ = part(z_r, 0, 40, 3 * NE)
        score, sel, comb, posm, s_all = (r_[:, k, :].rearrange("p (c e) -> p c e", e=NE) for k in range(5))

        tiles = ([("u", j) for j in range(UT)] + [("x", j) for j in range(XT)]
                 + [("z", j) for j in range(KD)] + [("g", j) for j in range(2 * KD)])
        T_XBC, T_Z, NT = UT, UT + XT, len(tiles)

        def s5_steps(n):
            return [i for i in range(S5T) if (3 * i) // 2 == n]

        block = ctx.enter_context(nc.Block())

        @block.sync
        def _(sp):
            def weights(n):
                if n < 4:
                    return a["w_ada"][0, :, n * 512:(n + 1) * 512], KD
                if n < U_XBC:
                    return a["w_in"][0, :, IN_U:IN_U + 512], KD
                if n < U_Z:
                    return a["w_in"][0, :, IN_XBC + (n - U_XBC) * 512:IN_XBC + (n - U_XBC + 1) * 512], KD
                if n < U_GATE:
                    return a["w_in"][0, :, (n - U_Z) * 512:(n - U_Z + 1) * 512], KD
                if n < U_GLU:
                    return a["w_in"][0, :, IN_GATE + (n - U_GATE) * 512:IN_GATE + (n - U_GATE + 1) * 512], KD
                if n < U_ADA2:
                    return a["w_glu"][0, :, (n - U_GLU) * D:(n - U_GLU + 1) * D], UT
                if n < U_OUTA:
                    i = n - U_ADA2 + 4
                    return a["w_ada"][0, :, i * 512:(i + 1) * 512], KD
                if n < U_OUT:
                    return a["w_out_a"][0, :, (n - U_OUTA) * 512:(n - U_OUTA + 1) * 512], KD
                return a["w_out"][0, :, (n - U_OUT) * 512:(n - U_OUT + 1) * 512], KD

            for n in range(N_UNITS):
                if n >= NR:
                    sp.wait_ge(unit_used, n - NR + 1)
                if n == 0:
                    sp.wait_ge(ld_c, 32)
                elif n == 1:
                    sp.wait_ge(ld_par, 16 * 10)
                src, k = weights(n)
                sp.dma_start(unit_tile(n, k), src.rearrange("(k p) n -> p k n", p=P)).then_inc(landed[n % NR], 16)

            def pair_weights(pair, used):
                for r, (w, k) in enumerate((("w1", KD), ("w1", KD), ("w3", KD), ("w3", KD), ("w2", FT), ("w2", FT))):
                    s = MOE_SLOTS[r]
                    sp.wait_ge(unit_used, used(r))
                    src = a[w][0, bass.ds(2 * pair + r % 2, 1), :, :].rearrange("e (k p) n -> p (e k) n", p=P)
                    sp.dma_start(ring_tile(s, k), src).then_inc(landed[s], 16)

            def first_used(r):
                if r == 5:
                    sp.wait_ge(st_hp, 16)
                    for q in range(2):
                        sp.wait_ge(st_hs[q], 16 * KD // 2)
                    return U_OUT
                return max(n for n in range(N_UNITS) if n % NR == MOE_SLOTS[r]) + 1

            pair_weights(0, first_used)
            with sp.Fori(1, PAIRS) as q:
                pair_weights(q, lambda r: N_UNITS + 6 * (q - 1) + r + 1)
            sp.wait_ge(route_ok, 1)
            passes = sp.value_load(npi[0:1, 0:1], min_val=1, max_val=MAXPASS)
            with sp.If(passes > 1):
                with sp.Fori(1, passes) as n:
                    with sp.Fori(0, PAIRS) as q:
                        pair_weights(q, lambda r: N_UNITS + 6 * ((n * PAIRS - 1) + q) + r + 1)

            sp.wait_ge(fin_cp, 3)
            for i, (t0, n) in enumerate(CHUNKS[:2]):
                sp.dma_start(o["y_prompt"][0, t0:t0 + n, :], y_tok[0:n, i, :]).then_inc(st_y, 16)
            sp.dma_start(o["y_sample"].rearrange("b l d -> (b l) d"), y_tok[0:TS, 2, :]).then_inc(st_y, 16)
            sp.wait_ge(st_y, 48)
            sp.wait_ge(st_conv, 32)
            sp.wait_ge(st_s5, 64)

        @block.gpsimd
        def _(pool):
            link = linker(pool, pool_chain)
            g = nc.gpsimd

            def keep(out, in_, pattern, mult, base, op=ALU.is_ge):
                return g.affine_select(out=out, in_=in_, compare_op=op, fill=0.0, base=base,
                                       pattern=pattern, channel_multiplier=mult)

            link(g.memset(par8[:], 1.0))
            link(g.memset(strict[:], 1.0))
            link(g.memset(same_r[0:TS, :], 1.0))
            link(g.memset(blk[0:TS, :], 1.0))
            link(g.memset(ident[:], 0.0))
            g.affine_select(out=ident[:], in_=ident[:], compare_op=ALU.not_equal, fill=1.0, base=0,
                            pattern=[[-1, P]], channel_multiplier=1).then_inc(consts, 1)
            link(g.memset(upper[:], 1.0))
            keep(upper[:], upper[:], [[1, P]], -1, 0).then_inc(consts, 1)
            keep(strict[:], strict[:], [[1, P]], -1, -1).then_inc(consts, 1)
            same3 = sample(same_r[0:TS, :])
            link(keep(same3, same3, [[-LSAMP, NBATCH], [0, LSAMP]], 1, 0))
            link(keep(same3, same3, [[LSAMP, NBATCH], [0, LSAMP]], -1, LSAMP - 1))
            keep(supper_r[0:TS, :], same_r[0:TS, :], [[1, TS]], -1, 0).then_inc(consts, 1)
            link(keep(blk[0:TS, :], blk[0:TS, :], [[-LSAMP, NBATCH]], 1, 0))
            keep(blk[0:TS, :], blk[0:TS, :], [[LSAMP, NBATCH]], -1, LSAMP - 1).then_inc(consts, 1)
            p8 = par8[:].rearrange("p (q h) -> p q h", q=2)
            link(keep(p8, p8, [[-S5C, 2], [-2 * S5C, 4]], 1, 0))
            keep(p8, p8, [[S5C, 2], [2 * S5C, 4]], -1, S5C - 1).then_inc(consts, 1)
            g.iota(iota[:], [[1, CAP]], base=0, channel_multiplier=0,
                   allow_small_or_imprecise_dtypes=True).then_inc(consts, 1)
            g.iota(keyg[:], [[-1, NG]], base=NG, channel_multiplier=0,
                   allow_small_or_imprecise_dtypes=True).then_inc(consts, 1)
            g.iota(keye[:], [[-1, NE]], base=NE, channel_multiplier=0,
                   allow_small_or_imprecise_dtypes=True).then_inc(consts, 1)

            pool.wait_ge(rot_u, 1)
            wc, ws = [s5c[:, 0, :], s5c[:, 2, :]], [s5c[:, 1, :], s5c[:, 3, :]]
            link(g.memset(rotc[:, :, 0:1], 1.0))
            link(g.memset(rots[:, :, 0:1], 0.0))
            k, lv = 1, 0
            J = 64
            ta, tb = part(mix_r, off + 2048, S5T, J), part(mix_r, off + 3072, S5T, J)
            while k < TP:
                wcb = wc[lv % 2].unsqueeze(2)
                wsb = ws[lv % 2].unsqueeze(2)
                for j0 in range(0, k, J):
                    kk = min(k, J)
                    lo, hi = slice(j0, j0 + kk), slice(k + j0, k + j0 + kk)
                    bc = [P, S5T, kk]
                    A, B = ta[:, :, 0:kk], tb[:, :, 0:kk]
                    link(g.tensor_tensor(A, rotc[:, :, lo], wcb.to_broadcast(bc), ALU.mult))
                    link(g.tensor_tensor(B, rots[:, :, lo], wsb.to_broadcast(bc), ALU.mult))
                    link(g.tensor_tensor(rotc[:, :, hi], A, B, ALU.subtract))
                    link(g.tensor_tensor(A, rotc[:, :, lo], wsb.to_broadcast(bc), ALU.mult))
                    link(g.tensor_tensor(B, rots[:, :, lo], wcb.to_broadcast(bc), ALU.mult))
                    link(g.tensor_tensor(rots[:, :, hi], A, B, ALU.add))
                if 2 * k < TP:
                    c0, s0, c1, s1 = wc[lv % 2], ws[lv % 2], wc[(lv + 1) % 2], ws[(lv + 1) % 2]
                    t4 = s5c[:, 4, :]
                    link(g.tensor_tensor(c1, c0, c0, ALU.mult))
                    link(g.tensor_tensor(t4, s0, s0, ALU.mult))
                    link(g.tensor_tensor(c1, c1, t4, ALU.subtract))
                    link(g.tensor_tensor(s1, c0, s0, ALU.mult))
                    link(g.tensor_tensor(s1, s1, s1, ALU.add))
                k, lv = 2 * k, lv + 1
            g.tensor_copy(rotc[:, 0, 0:1], rotc[:, 0, 0:1]).then_inc(rot_ok, 1)

            for i in range(S5T):
                q = i % 2
                gr, gi, hr, hi = g5[:, 2 * q, :], g5[:, 2 * q + 1, :], h5[:, 2 * q, :], h5[:, 2 * q + 1, :]
                c_, s_ = rotc[:, i, :], rots[:, i, :]
                pool.wait_ge(s5_g, i + 1)
                if i >= 2:
                    pool.wait_ge(s5_hused, i - 1)
                link(g.tensor_tensor(pt[:, 0, :], gr, c_, ALU.mult))
                link(g.tensor_tensor(pt[:, 1, :], gi, s_, ALU.mult))
                link(g.tensor_tensor(hr, pt[:, 0, :], pt[:, 1, :], ALU.subtract))
                link(g.tensor_tensor(pt[:, 0, :], gr, s_, ALU.mult))
                link(g.tensor_tensor(pt[:, 1, :], gi, c_, ALU.mult))
                link(g.tensor_tensor(hi, pt[:, 0, :], pt[:, 1, :], ALU.add))
                link(g.tensor_copy(fin5[:, 0, i:i + 1], hr[:, TP - 1:TP]))
                g.tensor_copy(fin5[:, 1, i:i + 1], hi[:, TP - 1:TP]).then_inc(s5_h, 1)

            pool.wait_ge(dte_ok, 1)
            for i, (t0, n) in enumerate(CHUNKS):
                pool.wait_ge(xdt_ok, 2 * i + 2)
                g.tensor_tensor(Xs[0:n, i, :].rearrange("p (h d) -> p h d", d=HD),
                                Xdt[0:n, i, :].rearrange("p (h d) -> p h d", d=HD),
                                dte[0:n, i, :].unsqueeze(2).to_broadcast([n, H, HD]), ALU.mult).then_inc(xs_ok, 1)
            pool.wait_ge(bt_ok, 3)
            for gr in range(G):
                g.tensor_tensor(Bm[0:TS, gr, :].rearrange("p (b n) -> p b n", n=NS),
                                B_tok[0:TS, 2, gr * NS:(gr + 1) * NS].unsqueeze(1).to_broadcast([TS, NBATCH, NS]),
                                blk[0:TS, :].unsqueeze(2).to_broadcast([TS, NBATCH, NS]), ALU.mult).then_inc(bm_ok, 1)

        @block.tensor
        def _(pe):
            def mm(out, lhsT, rhs, first, last):
                return nc.tensor.matmul(out, lhsT, rhs, start=first, stop=last, skip_group_check=True)

            def tr(out, in_):
                return nc.tensor.transpose(out, in_, ident[0:in_.shape[0], 0:in_.shape[0]])

            def wait_unit(n):
                pe.wait_ge(landed[n % NR], 16 * (n // NR + 1))

            pe.wait_ge(consts, 9)
            pe.wait_ge(vconsts, 3)
            pe.wait_ge(c_silu, 1)
            for j in range(KD):
                last = tr(ps[:, 6, j * NC:(j + 1) * NC], c_in[0:NC, j * P:(j + 1) * P])
            last.then_inc(cT_ps, 1)

            def square_sum(bank, n, first, last):
                pe.wait_ge(sq_ok, n + 1)
                mm(ps[:, bank, 0:T], ones[:], sq[:, n % 2, :], first, last).then_inc(sq_used, 1)

            def square_sums(bank, tiles_, base):
                for j in range(tiles_):
                    square_sum(bank, base + j, j == 0, j == tiles_ - 1)

            pe.wait_ge(ld_x, 32)
            for j in range(KD):
                if j >= 2:
                    pe.wait_ge(x_ok, j - 1)
                for i, (t0, n) in enumerate(CHUNKS):
                    last = tr(ps[:, j % 2, t0:t0 + n], x_tok[0:n, i, j * P:(j + 1) * P])
                last.then_inc(x_ps, 1)
                if j:
                    square_sum(4, j - 1, j == 1, False)
            square_sum(4, KD - 1, False, True)

            pe.wait_ge(ld_par, 16 * 10)
            pe.wait_ge(expd, 2)
            tr(ps[:, 7, 0:104], prow1[0:104, :])
            tr(ps[:, 7, 128:208], prow2[0:80, :])
            tr(ps[:, 7, 256:272], prow3[0:16, :]).then_inc(par_ps, 1)

            def ada(i):
                n = ada_unit(i)
                w = unit_tile(n, KD)
                wait_unit(n)
                pe.wait_ge(cT_ok, 1)
                if i >= 1:
                    pe.wait_ge(ada_cp, i)
                for r in range(2):
                    for c in range(4):
                        last = mm(ps[32 * c:32 * c + 32, 5, :], cT[:, 4 * r + c, :], w[:, 4 * r + c, :], r == 0, r == 1)
                last.then_inc(unit_used, 1)

            def ada_turn(i):
                pe.wait_ge(ada_cp, i + 1)
                if i >= 1:
                    pe.wait_ge(mod_ok, i)
                if i >= 4:
                    pe.wait_ge(q_diff, 3 * (i // 2 - 1))
                for c in range(4):
                    last = mm(turned(i, c, c + 1), ada_s[:, c * P:(c + 1) * P], sel9[:, 0:NC], c == 0, c == 3)
                last.then_inc(adaT_ps, 1)

            for i in range(4):
                ada(i)
                ada_turn(i)

            def state_columns():
                pe.wait_ge(ld_state5, 32)
                for q in range(2):
                    tr(ps[:, 2, q * P:(q + 1) * P], st_rows[:, q, :])
                pe.wait_ge(ld_conv, 16)
                for j in range(XT):
                    last = tr(ps[:, 3, j * 24:(j + 1) * 24], conv_in[0:24, j * P:(j + 1) * P])
                last.then_inc(cT_ps, 1)

            def tile(t):
                n = U_U + t // 4
                w = unit_tile(n, KD)
                wait_unit(n)
                if t >= 2:
                    pe.wait_ge(tile_ev, t - 1)
                for k in range(KD):
                    if t == 0:
                        pe.wait_ge(hp_ok, k + 1)
                        pe.wait_ge(h_ok, k + 1)
                    last = mm(ps[:, t % 2, 0:T], w[:, k, (t % 4) * P:(t % 4 + 1) * P], hT[:, k, :], k == 0, k == KD - 1)
                last.then_inc(tile_ps, 1)
                if t % 4 == 3:
                    pe.wait_ge(tile_ps, t + 1)
                    pe.nop().then_inc(unit_used, 1)

            for t in range(T_Z):
                if t == T_XBC:
                    state_columns()
                tile(t)
            pe.wait_ge(ld_wdt, 16)
            pe.wait_ge(par_ok, 2)
            for i, (t0, n) in enumerate(CHUNKS):
                for k in range(KD):
                    last = mm(ps[0:n, 2, i * H:(i + 1) * H], hT[:, k, t0:t0 + n], w_dt[:, k, :], k == 0, k == KD - 1)
            last.then_inc(dt_ps, 1)

            pe.wait_ge(blk5, 2)
            for q in range(2):
                for j in range(UT):
                    last = tr(ps[:, 3 + q, j * P:(j + 1) * P],
                              bblk[:, q, 4 * j:4 * j + 4, :].rearrange("p i c -> p (i c)"))
                last.then_inc(s5w_ps, 1)
            for q in range(2):
                for j in range(UT):
                    last = tr(ps[:, 5 + q, j * P:(j + 1) * P], cblk[:, q, j, :])
                last.then_inc(s5w_ps, 1)
            pe.wait_ge(s5w_ok, 2)
            pe.wait_ge(da_ok, 1)
            pe.wait_ge(conv_acc, XT)
            for j in range(XT):
                last = tr(ps[0:27, 2 + j // 4, (j % 4) * P:(j % 4 + 1) * P], tails[:, j, :])
            last.then_inc(tail_ps, 1)

            def s5_in(i):
                a_, r = i // 4, 32 * (i % 4)
                if i < 2:
                    pe.wait_ge(s5w_ok, 4)
                    pe.wait_ge(tail_cp, 1)
                    pe.wait_ge(tile_ev, UT)
                else:
                    pe.wait_ge(s5_xused, i - 1)
                for q in range(2):
                    last = mm(ps[:, 2 + 2 * (i % 2) + q, 0:T], bT[r:r + 32, q, a_, :], uT[r:r + 32, a_, :], True, True)
                last.then_inc(s5_x, 1)

            def s5_out(i):
                a_, r = i // 4, 32 * (i % 4)
                pe.wait_ge(s5_h, i + 1)
                if r == 0 and a_ >= 2:
                    pe.wait_ge(s5_yev, a_ - 1)
                for q in range(2):
                    last = mm(ps[r:r + 32, 6 + a_ % 2, 0:TP], cTs5[:, q, a_, r:r + 32], h5[:, 2 * (i % 2) + q, :], q == 0, q == 1)
                last.then_inc(s5_hused, 1)

            for t in range(T_Z, NT):
                for i in s5_steps(t - T_Z):
                    if i >= 2:
                        s5_out(i - 2)
                    s5_in(i)
                tile(t)
            s5_out(S5T - 2)
            s5_out(S5T - 1)
            pe.wait_ge(s5_hs, 1)
            for i in range(S5T):
                a_, r = i // 4, 32 * (i % 4)
                for q in range(2):
                    last = mm(ps[r:r + 32, 2, a_ * TS:(a_ + 1) * TS], cTs5[:, q, a_, r:r + 32], s5h[:, q, i, :], q == 0, q == 1)
            last.then_inc(s5_y, 1)
            for q in range(2):
                tr(ps[:, 3, q * P:(q + 1) * P], st5[:, q].rearrange("p b i -> p (b i)"))
                last = tr(ps[0:S5T, 3, 256 + q * P:256 + (q + 1) * P], fin5[:, q, :])
            last.then_inc(s5f_ps, 1)

            pe.wait_ge(gelu_ok, UT)
            wait_unit(U_GLU)
            wait_unit(U_GLU + 1)
            wa, wb = unit_tile(U_GLU, UT), unit_tile(U_GLU + 1, UT)
            pe.wait_ge(s5f_cp, 1)
            pe.wait_ge(s5_yev, 5)
            pe.wait_ge(tile_ev, NT)
            for j in range(KD):
                if j >= 2:
                    pe.wait_ge(glu_ev, j - 1)
                for w, q in ((wa, 0), (wb, 1)):
                    for k in range(UT):
                        last = mm(ps[:, 2 * (j % 2) + q, 0:T], w[:, k, j * P:(j + 1) * P], uT[:, k, :], k == 0, k == UT - 1)
                last.then_inc(glu_ps, 1)
            for _ in range(2):
                pe.wait_ge(glu_ps, KD)
                pe.nop().then_inc(unit_used, 1)

            pe.wait_ge(conv_ok, 2 * XT)
            for i, (t0, n) in enumerate(CHUNKS):
                for gr in range(G):
                    o_ = (i % 2) * 256 + gr * n
                    last = mm(ps[0:n, 4 + i // 2, o_:o_ + n], xbcT[:, KD + gr, t0:t0 + n], xbcT[:, KD + G + gr, t0:t0 + n], True, True)
            last.then_inc(cb_ps, 1)
            for i, (t0, n) in enumerate(CHUNKS):
                up, on = (upper, ones) if i < 2 else (supper_r, same_r)
                mm(ps[0:n, 5, 128 + 32 * i:144 + 32 * i], up[0:n, 0:n], da3[0:n, i, :], True, True)
                mm(ps[0:n, 5, 144 + 32 * i:160 + 32 * i], on[0:n, 0:n], da3[0:n, i, :], True, True)
            for hp in range(KD):
                for q in range(2):
                    last = mm(ps[64 * q:64 * q + HD, 5, 256 + hp * TS:256 + (hp + 1) * TS],
                              da3[0:TS, 2, 2 * hp + q:2 * hp + q + 1].to_broadcast([TS, HD]), supper_r[0:TS, :], True, True)
            last.then_inc(acs_ps, 1)
            pe.wait_ge(glu_ev, KD)
            for i, (t0, n) in enumerate(CHUNKS):
                if i >= 1:
                    pe.wait_ge(xdt_ok, 2 * i)
                    pe.wait_ge(bt_ok, i)
                for j in range(KD):
                    last = tr(ps[0:n, 6 + j // 4, (j % 4) * P:(j % 4 + 1) * P], xbcT[:, j, t0:t0 + n])
                for gr in range(G):
                    last = tr(ps[0:n, 2, gr * P:(gr + 1) * P], xbcT[:, KD + gr, t0:t0 + n])
                last.then_inc(xt_ps, 1)
            pe.wait_ge(bt_ok, 3)
            for i in range(2):
                pe.wait_ge(xs_ok, i + 1)
                if i:
                    pe.wait_ge(h1_ok, G)
                for gr in range(G):
                    last = mm(ps[:, 2 + gr, :], B_tok[:, i, gr * NS:(gr + 1) * NS], Xs[:, i, gr * 512:(gr + 1) * 512], True, True)
                last.then_inc(st_ps, 1)

            for hp in range(KD):
                gr = hp // (KD // G)
                pe.wait_ge(ld_h0[hp % 2], 16 * (hp // 2 + 1))
                if hp:
                    pe.wait_ge(h0_cp, 2 * hp)
                for b in range(NBATCH):
                    last = tr(ps[:, b // 4, (b % 4) * P:(b % 4 + 1) * P], h0[:, hp % 2, b * NS:(b + 1) * NS])
                    if b % 4 == 3:
                        last.then_inc(h0_ps, 1)
                if hp == 0:
                    pe.wait_ge(xdt_ok, 6)
                    pe.wait_ge(hf_ok, G)
                    pe.wait_ge(acs_ok, 3)
                    pe.wait_ge(cb_ok, 3)
                    pe.wait_ge(bm_ok, 2)
                    pe.wait_ge(xs_ok, 3)
                if hp >= 2:
                    pe.wait_ge(ss_ok, hp - 1)
                for q in range(2):
                    last = mm(ps[:, 2 + 2 * (hp % 2) + q, :], Xs[0:TS, 2, hp * P:(hp + 1) * P], Bm[0:TS, gr, q * 512:(q + 1) * 512], True, True)
                last.then_inc(ss_ps, 1)
                pe.wait_ge(h0_cp, 2 * hp + 2)
                for b in range(NBATCH):
                    last = mm(ps[:, 7, hp * TS + b * LSAMP:hp * TS + (b + 1) * LSAMP], h0T[:, hp % 2, b * NS:(b + 1) * NS],
                              xbcT[:, KD + G + gr, TP + b * LSAMP:TP + (b + 1) * LSAMP], True, True)
                last.then_inc(yo_ps, 1)
            pe.wait_ge(ss_ok, KD)
            for j in range(KD):
                last = tr(ps[:, 2 + j // 4, (j % 4) * P:(j % 4 + 1) * P], hfT[:, j // 4, (j % 4) * P:(j % 4 + 1) * P])
            last.then_inc(hf_ps, 1)

            pe.wait_ge(hf_cp, 1)
            for qd in range(4):
                if qd:
                    pe.wait_ge(q_diff, 3 * qd)
                    pe.wait_ge(q_exp, 3 * qd)
                    pe.wait_ge(mod_ok, 4 + 2 * qd)
                for i, (t0, n) in enumerate(CHUNKS):
                    for h4 in range(4):
                        h = 4 * qd + h4
                        up = upper if i < 2 else supper_r
                        last = mm(ps[0:(P if i < 2 else TS), (2, 3, 1)[i], h4 * n:(h4 + 1) * n],
                                  da3[0:n, i, h:h + 1].to_broadcast([n, P if i < 2 else TS]), up[0:n, 0:n], True, True)
                last.then_inc(q_ps, 1)
                for i in (4 + 2 * qd, 5 + 2 * qd):
                    ada(i)
                    ada_turn(i)
                pe.wait_ge(q_mt, 3 * (qd + 1))
                for h4 in range(4):
                    h = 4 * qd + h4
                    gr, j = h // (H // G), h // 2
                    if h4 % 2 == 0 and j >= 2:
                        pe.wait_ge(q_yev, j - 1)
                    bank = (0, 4)[j % 2]
                    out = ps[64 * (h % 2):64 * (h % 2) + HD, bank, :]
                    xh = slice(h * HD, (h + 1) * HD)
                    mm(out[:, 0:CH], Xdt[:, 0, xh], MT[:, h4, 0:CH], True, True)
                    mm(out[:, CH:TP], Xdt[:, 1, xh], MT[:, h4, CH:TP], True, False)
                    mm(out[:, CH:TP], h1T[:, gr, (h % 8) * HD:(h % 8 + 1) * HD], CTs[:, h4, :], False, True)
                    last = mm(out[:, TP:T], Xdt[0:TS, 2, xh], MT[0:TS, h4, TP:T], True, True)
                    if h4 % 2 == 1:
                        last.then_inc(q_y, 1)
                if qd:
                    square_sum(6 + qd // 3, 6 + 2 * qd, qd != 2, False)
                    square_sum(6 + qd // 3, 7 + 2 * qd, False, qd == 2)
            square_sum(7, 14, False, False)
            square_sum(7, 15, False, True)

            def project(unit0, bank, src, banks_ps, freed, src_ok):
                for j in range(KD):
                    n = unit0 + j // 4
                    wait_unit(n)
                    w = unit_tile(n, KD)
                    if j >= 2:
                        pe.wait_ge(freed, j - 1)
                    for k in range(KD):
                        if j == 0:
                            pe.wait_ge(src_ok, k + 1)
                        last = mm(ps[:, bank + j % 2, 0:T], w[:, k, (j % 4) * P:(j % 4 + 1) * P], src[:, k, :], k == 0, k == KD - 1)
                    last.then_inc(banks_ps, 1)
                    if j % 4 == 3:
                        pe.wait_ge(banks_ps, j + 1)
                        pe.nop().then_inc(unit_used, 1)

            project(U_OUTA, 2, zT, outa_ps, mrg_ok, yn_ok)
            project(U_OUT, 0, gates, mix_ps, x1_ok, mrg_ok)
            square_sums(4, KD, 16)
            pe.wait_ge(hp_ok, 2 * KD)
            pe.wait_ge(h_ok, 2 * KD)
            pe.wait_ge(ld_wrt, 16)
            for i, (t0, n) in enumerate(CHUNKS):
                for k in range(KD):
                    last = mm(ps[0:n, 6, i * NE:(i + 1) * NE], hT[:, k, t0:t0 + n], w_rt[:, k, :], k == 0, k == KD - 1)
            last.then_inc(lg_ps, 1)
            for i, (t0, n) in enumerate(CHUNKS):
                if i:
                    pe.wait_ge(h2t_ok, 2 * i)
                for j in range(KD):
                    last = tr(ps[0:n, j // 4, (j % 4) * P:(j % 4 + 1) * P], hT[:, j, t0:t0 + n])
                    if j % 4 == 3:
                        last.then_inc(h2t_ps, 1)
            pe.wait_ge(top_ok, 1)
            for i, (t0, n) in enumerate(CHUNKS):
                for i2 in range(i + 1):
                    m = CHUNKS[i2][1]
                    mm(ps[0:n, 7, i * NE:(i + 1) * NE], (strict if i2 == i else ones)[0:m, 0:n], s_all[0:m, i2, :], i2 == 0, i2 == i)
            for i, (t0, n) in enumerate(CHUNKS):
                last = mm(ps[:, 7, 48:64], ones[0:n, :], s_all[0:n, i, :], i == 0, i == 2)
            last.then_inc(pos_ps, 1)

            def ring_wait(v, r):
                s = MOE_SLOTS[r]
                pe.wait_ge(landed[s], (v + uses(s) + 1) * 16 if s < NR else (v + 1) * 16)

            def gather(v, half):
                if half == 0:
                    pe.wait_ge(selo_ok, v + 1)
                for j in range(4 * half, 4 * half + 4):
                    for i, (t0, n) in enumerate(CHUNKS):
                        last = mm(ps[:, half, (j % 4) * P:(j % 4 + 1) * P], h2_tok[0:n, i, j * P:(j + 1) * P], selo2[0:n, i, :], i == 0, i == 2)
                last.then_inc(xg_ps[half], 1)

            def combine(v):
                pe.wait_ge(ye_ok, 2 * v + 2)
                pe.wait_ge(pT_ok, v + 1)
                for j in range(KD):
                    if j >= 2:
                        pe.wait_ge(cmb_ok, 8 * v + 8 + j - 1)
                    mm(ps[:, (7, 4)[j % 2], 0:T], y_e[:, j * P:(j + 1) * P], pT[:, :], True, True).then_inc(cmb_ps, 1)

            def up(v, wi):
                ring_wait(v, 2 * wi)
                ring_wait(v, 2 * wi + 1)
                for k in range(KD):
                    for e in range(2):
                        w = ring_tile(MOE_SLOTS[2 * wi + e], KD)
                        last = mm(ps[64 * e:64 * e + 64, 2 + wi, :], Xe[:, k, 64 * e:64 * e + 64], w[:, k, :], k == 0, k == KD - 1)
                        if k == KD - 1:
                            last.then_inc(unit_used, 1)

            def experts(v, prev, following):
                pe.wait_ge(xe_ok, 2 * v + 2)
                up(v, 0)
                if prev:
                    combine(v - 1)
                up(v, 1)
                if following:
                    gather(v + 1, 0)
                pe.wait_ge(selw_ok, v + 1)
                if prev:
                    pe.wait_ge(cmb_ok, 8 * v + 8)
                for i, (t0, n) in enumerate(CHUNKS):
                    last = tr(ps[:, 7, t0:t0 + n], selw2[0:n, i, :])
                last.then_inc(pT_ps, 1)
                pe.wait_ge(act_ok, v + 1)
                for f in range(FT):
                    last = tr(ps[:, 4, f * P:(f + 1) * P], act_e[:, f * P:(f + 1) * P])
                last.then_inc(aT_ps, 1)
                if following:
                    gather(v + 1, 1)
                pe.wait_ge(aT_ok, v + 1)
                ring_wait(v, 4)
                ring_wait(v, 5)
                for nh in range(2):
                    for f in range(FT):
                        for e in range(2):
                            w = ring_tile(MOE_SLOTS[4 + e], FT)
                            last = mm(ps[64 * e:64 * e + 64, 5 + nh, :], actT[:, f, 64 * e:64 * e + 64], w[:, f, nh * 512:(nh + 1) * 512], f == 0, f == FT - 1)
                            if nh == 1 and f == FT - 1:
                                last.then_inc(unit_used, 1)
                    if nh == 0:
                        last.then_inc(w2_ps, 1)

            pe.wait_ge(h2t_ok, 6)
            gather(0, 0)
            gather(0, 1)
            experts(0, False, True)
            with pe.Fori(1, PAIRS - 1) as q:
                experts(q, True, True)
            experts(PAIRS - 1, True, False)
            combine(PAIRS - 1)
            pe.wait_ge(route_ok, 1)
            passes = pe.value_load(npi[0:1, 0:1], min_val=1, max_val=MAXPASS)
            with pe.If(passes > 1):
                with pe.Fori(1, passes) as n:
                    v0 = n * PAIRS
                    gather(v0, 0)
                    gather(v0, 1)
                    experts(v0, False, True)
                    with pe.Fori(1, PAIRS - 1) as q:
                        experts(n * PAIRS + q, True, True)
                    experts(v0 + (PAIRS - 1), True, False)
                    combine(v0 + (PAIRS - 1))

            square_sums(5, KD, 24)
            pe.wait_ge(fin_ok, KD)
            for i, (t0, n) in enumerate(CHUNKS):
                if i:
                    pe.wait_ge(fin_cp, i)
                for j in range(KD):
                    last = tr(ps[0:n, j // 4, (j % 4) * P:(j % 4 + 1) * P], hT[:, j, t0:t0 + n])
                last.then_inc(fin_ps, 1)

        @block.scalar
        def _(act):
            link = linker(act, act_chain)

            def f(out, in_, func=ACT.Copy, **kw):
                return nc.scalar.activation(out, in_, func, **kw)

            def load(out, in_, s):
                act.dma_start(out, in_).then_inc(s, 16)

            load(c_in[0:1, :], a["c_prompt"], ld_c)
            load(c_in[1:NC, :], a["c_sample"], ld_c)
            load(x_tok[:, 0:2, :], a["x_prompt"][0].rearrange("(i p) d -> p i d", p=P), ld_x)
            load(x_tok[0:TS, 2, :], a["x_sample"].rearrange("b l d -> (b l) d"), ld_x)
            with nc.allow_non_contiguous_dma(reason="a value or a short run per descriptor, a few KiB in all"):
                load(exp_in[96:104, 0:2], a["d_ssd"][0].rearrange("(j q) -> j q", q=2), ld_exp)
                load(exp_in[0:S5T, 2:4], a["s5_log_dt"][0].rearrange("(j q) -> j q", q=2), ld_exp)
            r0 = 0
            for name, n in (("norm1_w", 8), ("norm2_w", 8), ("ssd_norm_w", 8), ("conv_w", 48), ("conv_b", 12), ("s5_d", 4)):
                v = a[name][0]
                v = v.rearrange("k (j p) -> (k j) p", p=P) if name == "conv_w" else v.rearrange("(j p) -> j p", p=P)
                load(prow1[r0:r0 + n, :], v, ld_par)
                r0 += n
            load(prow1[r0:r0 + 8, :], a["final_norm_w"].rearrange("(j p) -> j p", p=P), ld_par)
            load(prow2[0:48, :], a["b_ada"][0].rearrange("(j p) -> j p", p=P), ld_par)
            load(prow2[48:64, :], a["s5_a_re"][0].rearrange("(i q) s -> i (q s)", q=2), ld_par)
            load(prow2[64:80, :], a["s5_a_im"][0].rearrange("(i q) s -> i (q s)", q=2), ld_par)
            act.wait_ge(ld_c, 32)
            f(c_in[0:NC, :], c_in[0:NC, :], ACT.Silu).then_inc(c_silu, 1)

            n_sq = [0]

            def square(src):
                q = n_sq[0]
                if q >= 2:
                    act.wait_ge(sq_used, q - 1)
                f(sq[:, q % 2, :], src, ACT.Square).then_inc(sq_ok, 1)
                n_sq[0] += 1

            for j in range(KD):
                act.wait_ge(x_ps, j + 1)
                f(xT[:, j, :], ps[:, j % 2, 0:T]).then_inc(x_ok, 1)
                act.wait_ge(x_ok, j + 1)
                square(xT[:, j, :])

            for q, name in enumerate(("state_s5_re", "state_s5_im")):
                load(st_rows[:, q, :], a[name][0].rearrange("b (i q) s -> (b i) (q s)", q=2), ld_state5)
            load(conv_in[0:24, :], a["state_conv"][0].rearrange("b k f -> (b k) f"), ld_conv)
            for name, t_ in (("dt_bias", dtb), ("a_log", alog)):
                load(t_[:, :], a[name].to_broadcast([P, H]), ld_bc)
            load(brt[:, :], a["b_router"].unsqueeze(0).to_broadcast([P, NE]), ld_bc)
            for q, name in enumerate(("s5_b_re", "s5_b_im")):
                for gg in range(2):
                    load(b_raw[64 * gg:64 * gg + 64, q, :, :],
                         a[name][0].rearrange("(i q) s c -> q s i c", q=2)[gg], ld_rows)
            for q, name in enumerate(("s5_c_re", "s5_c_im")):
                load(c_raw[:, q, :, :], a[name][0].rearrange("(j g) c s -> (g c) j s", j=UT), ld_rows)
            load(w_dt[:, :, :], a["w_in"][0, :, IN_DT:IN_DT + H].rearrange("(k p) n -> p k n", p=P), ld_wdt)
            load(w_rt[:, :, :], a["w_router"].rearrange("(k p) n -> p k n", p=P), ld_wrt)

            n_rs = [0]

            def rsqrt(v, y):
                n_rs[0] += 1
                act.wait_ge(var_ok, n_rs[0])
                link(f(y, v, ACT.Ln))
                f(y, y, ACT.Exp, scale=-0.5).then_inc(rs_ok, 1)

            rsqrt(n1v, n1y)

            n_mod = [0]

            def modulate(sh):
                n_mod[0] += 1
                act.wait_ge(amul_ok, n_mod[0])
                for j in range(KD):
                    act.wait_ge(xn_ok, (n_mod[0] - 1) * KD + j + 1)
                    f(hT[:, j, 0:TP], hT[:, j, 0:TP], ACT.Identity, scale=amul[:, j, 0:1], bias=mod[:, sh + j, 0:1]).then_inc(hp_ok, 1)

            modulate(0)
            act.wait_ge(par_ok, 1)
            f(s5c[:, 5, :], pc3[:, :], ACT.Exp).then_inc(trig, 1)
            act.wait_ge(dsc, 1)
            f(s5c[:, 6, :], s5c[:, 6, :], ACT.Exp).then_inc(trig, 1)
            f(s5c[:, 11, :], s5c[:, 8, :], ACT.Sin).then_inc(trig, 1)
            f(s5c[:, 10, :], s5c[:, 9, :], ACT.Sin).then_inc(trig, 1)

            def conv_silu(j):
                act.wait_ge(conv_acc, j + 1)
                acc = part(z_r, (j % 2) * 312, 312)
                f(xbcT[:, j, 0:TP], acc[:, 0:TP], ACT.Silu).then_inc(conv_ok, 1)
                f(sample(xbcT[:, j, TP:T]), rows_sample(acc)[:, :, 0:LSAMP], ACT.Silu).then_inc(conv_ok, 1)

            def rows_sample(v):
                n = v.shape[-1] - 259
                if n == 56:
                    return v[:, 259:315].rearrange("p (b l) -> p b l", l=7)
                return bass.AP(v.tensor, v.offset + 259, [list(v.ap[0]), [7, NBATCH], [1, LSAMP]])

            for t, (kind, j) in enumerate(tiles[:T_Z]):
                if kind == "x" and j >= 2:
                    conv_silu(j - 2)
                act.wait_ge(tile_ps, t + 1)
                if kind == "u":
                    f(uT[:, j, :], ps[:, t % 2, 0:T]).then_inc(tile_ev, 1)
                else:
                    if j == 0:
                        act.wait_ge(sq_used, KD)
                    row = rows[:, j % 2, :]
                    link(f(row[:, 3:3 + TP], ps[:, t % 2, 0:TP]))
                    f(rows_sample(row)[:, :, 3:7], sample(ps[:, t % 2, TP:T])).then_inc(tile_ev, 1)
            conv_silu(XT - 2)
            conv_silu(XT - 1)
            act.wait_ge(ld_bc, 48)
            link(f(alog[:, :], alog[:, :], ACT.Exp))
            act.wait_ge(dt_pre, 1)
            link(f(dtt[:, :, :], dt3[:, :, :], ACT.Abs))
            link(f(dtt[:, :, :], dtt[:, :, :], ACT.Exp, scale=-1.0))
            f(dtt[:, :, :], dtt[:, :, :], ACT.Ln, bias=1.0).then_inc(dt_exp, 1)
            act.wait_ge(tail_ps, 1)
            ctail = part(gate_r, 8 * T, XBC)
            f(ctail[0:27, :].rearrange("p (a b) -> p a b", b=512), ps[0:27, 2:5, :]).then_inc(tail_cp, 1)
            act.wait_ge(tail_cp, 1)
            act.dma_start(o["conv_prompt"][0, 0], ctail[0:3, :]).then_inc(st_conv, 16)
            act.dma_start(o["conv_sample"][0].rearrange("b k f -> (b k) f"), ctail[3:27, :]).then_inc(st_conv, 16)

            for t, (kind, j) in enumerate(tiles):
                if t < T_Z:
                    continue
                act.wait_ge(tile_ps, t + 1)
                if kind == "z":
                    f(zT[:, j, :], ps[:, t % 2, 0:T], ACT.Silu).then_inc(tile_ev, 1)
                else:
                    if j == KD:
                        act.wait_ge(st_conv, 32)
                    f(gates[:, j, :], ps[:, t % 2, 0:T], ACT.Sigmoid).then_inc(tile_ev, 1)

            act.wait_ge(s5_yev, 5)
            for j in range(UT):
                f(uT[:, j, :], uT[:, j, :], ACT.Gelu_apprx_tanh).then_inc(gelu_ok, 1)
            act.wait_ge(s5f_ps, 1)
            link(f(ada_s[:, 0:256], ps[:, 3, 0:256]))
            f(ada_s[0:S5T, 256:512], ps[0:S5T, 3, 256:512]).then_inc(s5f_cp, 1)
            act.wait_ge(s5f_cp, 1)
            for q, (ns, npr) in enumerate((("s5_re_sample", "s5_re_prompt"), ("s5_im_sample", "s5_im_prompt"))):
                act.dma_start(o[ns][0].rearrange("b (i q) s -> (b i) (q s)", q=2), ada_s[:, q * P:(q + 1) * P]).then_inc(st_s5, 16)
                act.dma_start(o[npr][0, 0].rearrange("(i q) s -> i (q s)", q=2),
                              ada_s[0:S5T, 256 + q * P:256 + (q + 1) * P]).then_inc(st_s5, 16)
            h0_src = a["state_ssm"][0].rearrange("b (j q) p n -> j (q p) b n", q=2)
            h0_dst = o["ssm_sample"][0].rearrange("b (j q) p n -> j (q p) b n", q=2)

            def h0v(j):
                return h0[:, j % 2, :].rearrange("p (b n) -> p b n", n=NS)

            for j in range(2):
                act.dma_start(h0v(j), h0_src[j]).then_inc(ld_h0[j], 16)
            for j in range(KD):
                act.wait_ge(glu_ps, j + 1)
                if j >= 2:
                    act.wait_ge(glu_ev, j - 1)
                f(sq[:, j % 2, :], ps[:, 2 * (j % 2) + 1, 0:T], ACT.Sigmoid).then_inc(glu_sig, 1)

            act.wait_ge(acs_ok, 2)
            f(eft[:, :, :].rearrange("p j t -> p (j t)"), ps[:, 5, 256:512], ACT.Exp).then_inc(acs_ok, 1)
            act.wait_ge(dte_pre, 1)
            link(f(dte[:, 0:2, :], dte[:, 0:2, :], ACT.Exp))
            link(f(dte[0:TS, 2, :], dte[0:TS, 2, :], ACT.Exp))
            f(acs[:, 1, H:2 * H], acs[:, 1, H:2 * H], ACT.Exp).then_inc(dte_ok, 1)
            for i, (t0, n) in enumerate(CHUNKS):
                act.wait_ge(xt_ps, i + 1)
                f(B_tok[0:n, i, :], ps[0:n, 2, 0:2 * NS]).then_inc(bt_ok, 1)
            act.wait_ge(st_ps, 1)
            for gr in range(G):
                f(h1T[:, gr, :], ps[:, 2 + gr, :]).then_inc(h1_ok, 1)
            for hp in range(KD):
                for q in range(2):
                    act.wait_ge(h0_ps, 2 * hp + q + 1)
                    if hp >= 2:
                        act.wait_ge(yo_ps, hp - 1)
                    f(h0T[:, hp % 2, q * 512:(q + 1) * 512], ps[:, q, :]).then_inc(h0_cp, 1)
                if hp >= 1:
                    act.wait_ge(ss_ok, hp)
                    act.dma_start(h0_dst[hp - 1], h0v(hp - 1)).then_inc(st_hs[(hp - 1) % 2], 16)
                if 1 <= hp < KD - 1:
                    act.wait_ge(st_hs[(hp - 1) % 2], 16 * ((hp - 1) // 2 + 1))
                    act.dma_start(h0v(hp + 1), h0_src[hp + 1]).then_inc(ld_h0[(hp + 1) % 2], 16)
            act.wait_ge(ss_ok, KD)
            act.dma_start(h0_dst[KD - 1], h0v(KD - 1)).then_inc(st_hs[1], 16)
            act.wait_ge(hf_ps, 1)
            f(h_out[:, :, :].rearrange("p (a j) n -> p a (j n)", a=2), ps[:, 2:4, :]).then_inc(hf_cp, 1)
            act.wait_ge(hf_cp, 1)
            act.dma_start(o["ssm_prompt"][0, 0].rearrange("(j q) p n -> (q p) j n", q=2), h_out).then_inc(st_hp, 16)

            for qd in range(4):
                act.wait_ge(q_diff, 3 * qd + 3)
                if qd:
                    act.wait_ge(q_y, 2 * qd)
                f(CTs[:, :, :].rearrange("p h q -> p (h q)"), ps[:, 3, :], ACT.Exp).then_inc(q_exp, 1)
                act.wait_ge(q_msk, 2 * qd + 2)
                f(MT[:, :, 0:TP], MT[:, :, 0:TP], ACT.Exp).then_inc(q_exp, 1)
                f(MT[0:TS, :, TP:T], MT[0:TS, :, TP:T], ACT.Exp).then_inc(q_exp, 1)
                for j in range(2 * qd - 2, 2 * qd):
                    if qd:
                        act.wait_ge(q_yev, j + 1)
                        square(zT[:, j, :])
            rsqrt(nv, ny)
            for j in (6, 7):
                act.wait_ge(q_yev, j + 1)
                square(zT[:, j, :])
            rsqrt(nv, ny)
            for j in range(KD):
                act.wait_ge(x1_ok, j + 1)
                square(xT[:, j, :])
            rsqrt(nv, ny)
            modulate(24)
            for i, (t0, n) in enumerate(CHUNKS):
                for q in range(2):
                    act.wait_ge(h2t_ps, 2 * i + q + 1)
                    f(h2_tok[0:n, i, q * 512:(q + 1) * 512], ps[0:n, q, :]).then_inc(h2t_ok, 1)
            act.wait_ge(sm_in, 1)
            f(score, score, ACT.Exp).then_inc(sm_exp, 1)

            def tokens_in(v, half):
                act.wait_ge(xg_ps[half], v + 1)
                f(Xe[:, 4 * half:4 * half + 4, :].rearrange("p j s -> p (j s)"), ps[:, half, :]).then_inc(xe_ok, 1)

            def experts(v, prev, following):
                act.wait_ge(unit_used, N_UNITS + 6 * v + 2)
                if prev:
                    act.wait_ge(act_ok, v)
                f(hs_[:, :], ps[:, 2, :], ACT.Silu).then_inc(act_s, 1)
                if following:
                    tokens_in(v + 1, 0)
                act.wait_ge(aT_ps, v + 1)
                f(actT[:, :, :].rearrange("p f s -> p (f s)"), ps[:, 4, :]).then_inc(aT_ok, 1)
                if following:
                    tokens_in(v + 1, 1)
                act.wait_ge(w2_ps, v + 1)
                f(y_e[:, 0:512], ps[:, 5, :]).then_inc(ye_ok, 1)
                act.wait_ge(unit_used, N_UNITS + 6 * v + 6)
                f(y_e[:, 512:D], ps[:, 6, :]).then_inc(ye_ok, 1)

            tokens_in(0, 0)
            tokens_in(0, 1)
            experts(0, False, True)
            with act.Fori(1, PAIRS - 1) as q:
                experts(q, True, True)
            experts(PAIRS - 1, True, False)
            act.wait_ge(route_ok, 1)
            passes = act.value_load(npi[0:1, 0:1], min_val=1, max_val=MAXPASS)
            with act.If(passes > 1):
                with act.Fori(1, passes) as n:
                    v0 = n * PAIRS
                    tokens_in(v0, 0)
                    tokens_in(v0, 1)
                    experts(v0, True, True)
                    with act.Fori(1, PAIRS - 1) as q:
                        experts(n * PAIRS + q, True, True)
                    experts(v0 + (PAIRS - 1), True, False)
            for j in range(KD):
                act.wait_ge(x2_ok, j + 1)
                square(xT[:, j, :])
            rsqrt(nv, ny)
            for i, (t0, n) in enumerate(CHUNKS):
                act.wait_ge(fin_ps, i + 1)
                f(y_tok[0:n, i, :].rearrange("p (a n) -> p a n", a=2), ps[0:n, 0:2, :]).then_inc(fin_cp, 1)

        @block.vector
        def _(dve):
            link = linker(dve, dve_chain)
            v = nc.vector

            def tt(out, x, y, op):
                return v.tensor_tensor(out, x, y, op)

            def ts(out, x, s1, s2, op0, op1=None):
                return v.tensor_scalar(out, x, s1, s2, op0, op1) if op1 is not None else v.tensor_scalar(out, x, s1, s2, op0)

            def stt(out, x, s, y, op0, op1):
                return v.scalar_tensor_tensor(out=out, in0=x, scalar=s, in1=y, op0=op0, op1=op1)

            v.memset(ones[:], 1.0).then_inc(vconsts, 1)
            link(v.memset(cT, 0.0))
            link(v.memset(bblk, 0.0))
            dve.wait_ge(consts, 9)
            for c in range(4):
                last = v.tensor_copy(sel9[32 * c:32 * c + 32, :], ident[32 * c:32 * c + 32, 32 * c:32 * c + 32])
            last.then_inc(vconsts, 1)
            v.tensor_reduce(par2[:], par8[:].rearrange("p (q h) -> p q h", q=2), AX_X, ALU.add).then_inc(vconsts, 1)
            dve.wait_ge(vconsts, 3)
            dve.wait_ge(cT_ps, 1)
            v.tensor_copy(cT[:, :, 0:NC], ps[:, 6, 0:KD * NC].rearrange("p (k c) -> p k c", c=NC)).then_inc(cT_ok, 1)
            dve.wait_ge(ld_exp, 32)
            v.tensor_copy(prow1[96:104, :].rearrange("p (q s) -> p q s", q=2),
                          exp_in[96:104, 0:2].unsqueeze(2).to_broadcast([8, 2, 64])).then_inc(expd, 1)
            v.tensor_copy(prow3[0:S5T, :].rearrange("p (q s) -> p q s", q=2),
                          exp_in[0:S5T, 2:4].unsqueeze(2).to_broadcast([S5T, 2, 64])).then_inc(expd, 1)
            dve.wait_ge(par_ps, 1)
            link(v.tensor_copy(pc1[:, :], ps[:, 7, 0:104]))
            link(v.tensor_copy(pc2[:, :], ps[:, 7, 128:208]))
            v.tensor_copy(pc3[:, :], ps[:, 7, 256:272]).then_inc(par_ok, 1)
            def norm_scale(bank, count, width, vv, y, t, n):
                dve.wait_ge(sq_used, count)
                ts(vv, ps[:, bank, 0:T], 1.0 / width, EPS, ALU.mult, ALU.add).then_inc(var_ok, 1)
                dve.wait_ge(rs_ok, n)
                link(tt(t, vv, y, ALU.mult))
                link(tt(t, t, y, ALU.mult))
                link(ts(t, t, -0.5, 1.5, ALU.mult, ALU.add))
                link(tt(y, y, t, ALU.mult))

            def ada(i):
                dve.wait_ge(unit_used, ada_unit(i) + 1)
                if i >= 1:
                    dve.wait_ge(adaT_ps, i)
                if i == 4:
                    dve.wait_ge(st_s5, 64)
                v.tensor_copy(ada_s[:, :], ps[:, 5, :]).then_inc(ada_cp, 1)
                dve.wait_ge(adaT_ps, i + 1)
                tt(mod[:, 4 * i:4 * i + 4, :], turned(i, 0, 4).rearrange("p (k c) -> p k c", c=NC),
                   b_ada[:, 4 * i:4 * i + 4].unsqueeze(2).to_broadcast([P, 4, NC]), ALU.add).then_inc(mod_ok, 1)

            def per_sequence(col):
                return col.unsqueeze(2).to_broadcast([P, NBATCH, LSAMP])

            def normalize(y):
                for j in range(KD):
                    tt(hT[:, j, :], xT[:, j, :], y, ALU.mult).then_inc(xn_ok, 1)

            def modulate(nw, sh, sc, n):
                stt(amul, mod[:, sc:sc + KD, :], 1.0, nw.unsqueeze(2).to_broadcast([P, KD, NC]), ALU.add, ALU.mult).then_inc(amul_ok, 1)
                dve.wait_ge(amul_ok, n)
                dve.wait_ge(xn_ok, n * KD)
                hs = [sample(hT[:, j, TP:T]) for j in range(KD)]
                for j in range(KD):
                    tt(hs[j], hs[j], per_sequence(amul[:, j, 1:NC]), ALU.mult).then_inc(hm_ok, 1)
                for j in range(KD):
                    dve.wait_ge(hm_ok, (n - 1) * KD + j + 1)
                    tt(hs[j], hs[j], per_sequence(mod[:, sh + j, 1:NC]), ALU.add).then_inc(h_ok, 1)

            norm_scale(4, KD, D, n1v, n1y, n1t, 1)
            ada(0)
            normalize(n1y)
            for i in range(1, 4):
                ada(i)
            dve.wait_ge(mod_ok, 4)
            modulate(nw1, 0, 8, 1)

            C = [s5c[:, k, :] for k in range(24)]
            dt_, mag, th, r, r2, co, si, abr, abi, den, fre, fim = C[5], C[6], C[7], C[8], C[9], C[10], C[11], C[12], C[13], C[14], C[15], C[16]
            t0_, t1_, am1 = C[17], C[18], C[21]
            dve.wait_ge(trig, 1)
            link(tt(mag, dt_, a_re, ALU.mult))
            link(tt(th, dt_, a_im, ALU.mult))
            link(ts(t0_, th, 1.0 / TWO_PI, ROUND, ALU.mult, ALU.add))
            link(ts(t0_, t0_, -ROUND, None, ALU.add))
            link(stt(r, t0_, -TWO_PI_HI, th, ALU.mult, ALU.add))
            link(stt(r, t0_, -(TWO_PI - TWO_PI_HI), r, ALU.mult, ALU.add))
            link(ts(r, r, PI_IN, -PI_IN, ALU.min, ALU.max))
            link(ts(t1_, r, TWO_PI / 4, -TWO_PI, ALU.is_gt, ALU.mult))
            link(stt(r2, r, TWO_PI / 4, t1_, ALU.add, ALU.add))
            ts(r2, r2, PI_IN, -PI_IN, ALU.min, ALU.max).then_inc(dsc, 1)
            dve.wait_ge(trig, 4)
            link(v.tensor_copy(C[0], co))
            v.tensor_copy(C[1], si).then_inc(rot_u, 1)
            link(tt(abr, mag, co, ALU.mult))
            link(tt(abi, mag, si, ALU.mult))
            link(ts(am1, abr, -1.0, None, ALU.add))
            link(tt(den, a_re, a_re, ALU.mult))
            link(tt(t0_, a_im, a_im, ALU.mult))
            link(tt(den, den, t0_, ALU.add))
            link(v.reciprocal(den, den))
            link(tt(fre, am1, a_re, ALU.mult))
            link(tt(t0_, abi, a_im, ALU.mult))
            link(tt(fre, fre, t0_, ALU.add))
            link(tt(fre, fre, den, ALU.mult))
            link(tt(fim, abi, a_re, ALU.mult))
            link(tt(t0_, am1, a_im, ALU.mult))
            link(tt(fim, fim, t0_, ALU.subtract))
            link(tt(fim, fim, den, ALU.mult))
            dve.wait_ge(cT_ps, 2)
            link(v.tensor_copy(csT.rearrange("p j k -> p (j k)"), ps[:, 3, 0:XT * 24]))
            dve.wait_ge(x_ps, KD)
            v.tensor_copy(st5_flat, ps[:, 2, 0:256]).then_inc(par_ok, 1)

            dve.wait_ge(ld_rows, 16 * 6)
            b3 = [P // 2, S5T, S5C]
            btmp = part(gate_r, 4228, S5T, S5C)
            for gg in range(2):
                rr = slice(64 * gg, 64 * gg + 64)
                cc = slice(S5C * gg, S5C * gg + S5C)
                fr, fi = fre[rr].unsqueeze(2).to_broadcast(b3), fim[rr].unsqueeze(2).to_broadcast(b3)
                for q, (x, y, op) in enumerate(((0, 1, ALU.subtract), (1, 0, ALU.add))):
                    link(tt(btmp[rr], b_raw[rr, y], fi, ALU.mult))
                    link(tt(bblk[rr, q, :, cc], b_raw[rr, x], fr, ALU.mult))
                    link(tt(bblk[rr, q, :, cc], bblk[rr, q, :, cc], btmp[rr], op))
            dve.wait_ge(cT_ps, 1)
            for q, sign in enumerate((1.0, -1.0)):
                for hh in range(2):
                    link(ts(cblk[:, q, :, 64 * hh:64 * hh + 64], c_raw[:, q], par2[:, hh:hh + 1], sign, ALU.mult, ALU.mult))
            v.memset(npf[:, 0:1], 0.0).then_inc(blk5, 2)


            dve.wait_ge(sq_used, KD)
            link(v.memset(rows[:, :, 0:3], 0.0))
            for j in range(XT):
                row = rows[:, j % 2, :]
                acc = part(z_r, (j % 2) * 312, 312)
                srow = row[:, 259:315].rearrange("p (b l) -> p b l", l=7)
                link(v.tensor_copy(srow[:, :, 0:3], csT[:, j, :].rearrange("p (b k) -> p b k", k=3)))
                dve.wait_ge(tile_ev, T_XBC + j + 1)
                if j >= 2:
                    dve.wait_ge(conv_ok, 2 * (j - 1))
                elif j == 0:
                    dve.wait_ge(xn_ok, KD)
                link(ts(acc, row[:, 0:312], convw[:, 0, j:j + 1], convb[:, j:j + 1], ALU.mult, ALU.add))
                for k in range(1, CONV):
                    link(stt(acc, row[:, k:k + 312], convw[:, k, j:j + 1], acc, ALU.mult, ALU.add))
                link(v.tensor_copy(tails[:, j, 0:3], row[:, TP:TP + 3]))
                v.tensor_copy(tails[:, j, 3:27].rearrange("p (b k) -> p b k", k=3), srow[:, :, 4:7]).then_inc(conv_acc, 1)

            link(v.memset(dt3, 0.0))
            dve.wait_ge(dt_ps, 1)
            dve.wait_ge(ld_bc, 48)
            link(tt(dt3[:, 0:2, :], ps[:, 2, 0:2 * H].rearrange("p (i h) -> p i h", h=H),
                    dtb[:, :].unsqueeze(1).to_broadcast([P, 2, H]), ALU.add))
            tt(dt3[0:TS, 2, :], ps[0:TS, 2, 2 * H:3 * H], dtb[0:TS, :], ALU.add).then_inc(dt_pre, 1)
            dve.wait_ge(dt_exp, 1)
            link(stt(dt3, dt3, 0.0, dtt, ALU.max, ALU.add))
            stt(da3, dt3, -1.0, alog[:, :].unsqueeze(1).to_broadcast([P, 3, H]), ALU.mult, ALU.mult).then_inc(da_ok, 1)
            for q in range(4):
                dve.wait_ge(s5w_ps, q + 1)
                dst = (bT if q < 2 else cTs5)[:, q % 2]
                v.tensor_copy(dst.rearrange("p j m -> p (j m)"), ps[:, 3 + q, :]).then_inc(s5w_ok, 1)

            dve.wait_ge(rot_ok, 1)
            dve.wait_ge(conv_acc, XT)

            def s5_y_out(j):
                dve.wait_ge(s5_hused, 4 * j + 4)
                stt(uT[:, j, 0:TP], uT[:, j, 0:TP], s5d[:, j:j + 1], ps[:, 6 + j % 2, 0:TP], ALU.mult, ALU.add).then_inc(s5_yev, 1)

            for i in range(S5T):
                q = i % 2
                xr, xi = ps[:, 2 + 2 * q, :], ps[:, 3 + 2 * q, :]
                c_, s_ = rotc[:, i, :], rots[:, i, :]
                gr, gi = g5[:, 2 * q, :], g5[:, 2 * q + 1, :]
                dve.wait_ge(s5_x, i + 1)
                if i >= 2:
                    dve.wait_ge(s5_h, i - 1)
                link(tt(vt[:, 0, :], xr[:, 0:TP], c_, ALU.mult))
                link(tt(vt[:, 1, :], xi[:, 0:TP], s_, ALU.mult))
                link(tt(gr, vt[:, 0, :], vt[:, 1, :], ALU.add))
                link(tt(vt[:, 0, :], xi[:, 0:TP], c_, ALU.mult))
                link(tt(vt[:, 1, :], xr[:, 0:TP], s_, ALU.mult))
                link(tt(gi, vt[:, 0, :], vt[:, 1, :], ALU.subtract))
                link(v.tensor_copy(s5x[:, 0, i, :], xr[:, TP:T]))
                v.tensor_copy(s5x[:, 1, i, :], xi[:, TP:T]).then_inc(s5_xused, 1)
                m_ = mag[:, i:i + 1].to_broadcast([P, TP])
                link(v.tensor_tensor_scan(gr, m_, gr, 0.0, ALU.mult, ALU.add))
                v.tensor_tensor_scan(gi, m_, gi, 0.0, ALU.mult, ALU.add).then_inc(s5_g, 1)
                if i % 4 == 1 and i > 1:
                    s5_y_out(i // 4 - 1)
            dve.wait_ge(s5_xused, S5T)
            dve.wait_ge(s5_g, S5T)
            sh = [P, S5T, NBATCH]
            ar, ai = abr.unsqueeze(2).to_broadcast(sh), abi.unsqueeze(2).to_broadcast(sh)
            w0, w1_ = part(conv_r, 0, S5T, NBATCH), part(conv_r, P, S5T, NBATCH)
            xl = [s5x[:, q].rearrange("p i (b l) -> p i b l", l=LSAMP) for q in range(2)]
            hl = [s5h[:, q].rearrange("p i (b l) -> p i b l", l=LSAMP) for q in range(2)]
            prev = [st5[:, q].rearrange("p b i -> p i b") for q in range(2)]
            for l in range(LSAMP):
                for q, (x, y, op) in enumerate(((0, 1, ALU.subtract), (1, 0, ALU.add))):
                    link(tt(w0, prev[x], ar, ALU.mult))
                    link(tt(w1_, prev[y], ai, ALU.mult))
                    link(tt(w0, w0, w1_, op))
                    link(tt(hl[q][:, :, :, l], w0, xl[q][:, :, :, l], ALU.add))
                prev = [hl[q][:, :, :, l] for q in range(2)]
            link(v.tensor_copy(st5[:, 0].rearrange("p b i -> p i b"), prev[0]))
            dve.wait_ge(s5_h, S5T)
            v.tensor_copy(st5[:, 1].rearrange("p b i -> p i b"), prev[1]).then_inc(s5_hs, 1)
            s5_y_out(UT - 1)
            dve.wait_ge(s5_y, 1)
            for j in range(UT):
                last = stt(uT[:, j, TP:T], uT[:, j, TP:T], s5d[:, j:j + 1], ps[:, 2, j * TS:(j + 1) * TS], ALU.mult, ALU.add)
            last.then_inc(s5_yev, 1)

            for j in range(KD):
                dve.wait_ge(glu_sig, j + 1)
                link(tt(sq[:, j % 2, :], ps[:, 2 * (j % 2), 0:T], sq[:, j % 2, :], ALU.mult))
                tt(gates[:, KD + j, :], gates[:, KD + j, :], sq[:, j % 2, :], ALU.mult).then_inc(glu_ev, 1)

            dve.wait_ge(cb_ps, 1)
            for i, (c0, n) in enumerate(CHUNKS):
                if i == 2:
                    dve.wait_ge(acs_ps, 1)
                o_ = (i % 2) * 256
                mask = upper[:, :] if i < 2 else supper_r[0:TS, :]
                tt(CBm[0:n, :, c0:c0 + n], ps[0:n, 4 + i // 2, o_:o_ + 2 * n].rearrange("p (g q) -> p g q", g=G),
                   mask.unsqueeze(1).to_broadcast([n, G, n]), ALU.mult).then_inc(cb_ok, 1)
            dve.wait_ge(acs_ps, 1)
            p5 = ps[:, 5, 128:224].rearrange("p (i h) -> p i h", i=3)
            v.tensor_copy(acs[:, 0:2, :], p5[:, 0:2, :]).then_inc(acs_ok, 1)
            v.tensor_copy(acs[0:TS, 2, :], p5[0:TS, 2, :]).then_inc(acs_ok, 1)
            dve.wait_ge(acs_ok, 3)
            link(tt(dte[:, 0:2, :], acs[:, 0:2, H:2 * H], acs[:, 0:2, 0:H], ALU.subtract))
            tt(dte[0:TS, 2, :], acs[0:TS, 2, H:2 * H], acs[0:TS, 2, 0:H], ALU.subtract).then_inc(dte_pre, 1)
            for i, (c0, n) in enumerate(CHUNKS):
                dve.wait_ge(xt_ps, i + 1)
                for q in range(2):
                    tt(Xdt[0:n, i, q * 512:(q + 1) * 512].rearrange("p (h d) -> p h d", d=HD),
                       ps[0:n, 6 + q, :].rearrange("p (h d) -> p h d", d=HD),
                       dt3[0:n, i, 8 * q:8 * q + 8].unsqueeze(2).to_broadcast([n, 8, HD]), ALU.mult).then_inc(xdt_ok, 1)
            dve.wait_ge(st_ps, 2)
            dve.wait_ge(dte_ok, 1)
            for gr in range(G):
                hf3 = hfT[:, gr, :].rearrange("p (h d) -> p h d", d=HD)
                link(tt(hf3, h1T[:, gr, :].rearrange("p (h d) -> p h d", d=HD),
                        acs[:, 1, H + 8 * gr:H + 8 * gr + 8].unsqueeze(2).to_broadcast([P, 8, HD]), ALU.mult))
                tt(hfT[:, gr, :], hfT[:, gr, :], ps[:, 2 + gr, :], ALU.add).then_inc(hf_ok, 1)
            for hp in range(KD):
                hv = h0[:, hp % 2, :].rearrange("p (b n) -> p b n", n=NS)
                dve.wait_ge(h0_ps, 2 * hp + 2)
                link(tt(hv, hv, sample(eft[:, hp, :])[:, :, LSAMP - 1:LSAMP].to_broadcast([P, NBATCH, NS]), ALU.mult))
                dve.wait_ge(ss_ps, hp + 1)
                b0 = 2 + 2 * (hp % 2)
                h2v = h0[:, hp % 2, :].rearrange("p (a n) -> p a n", a=2)
                tt(h2v, h2v, ps[:, b0:b0 + 2, :], ALU.add).then_inc(ss_ok, 1)
            dve.wait_ge(yo_ps, KD)
            tt(yoff.rearrange("p j t -> p (j t)"), ps[:, 7, 0:256], eft.rearrange("p j t -> p (j t)"), ALU.mult).then_inc(yo_done, 1)
            dve.wait_ge(yo_done, 1)

            def y_out(j):
                dve.wait_ge(q_y, j + 1)
                if j:
                    dve.wait_ge(q_yev, j)
                link(stt(nt, xbcT[:, j, :], dskip[:, j:j + 1], ps[:, (0, 4)[j % 2], 0:T], ALU.mult, ALU.add))
                link(tt(nt[:, TP:T], nt[:, TP:T], yoff[:, j, :], ALU.add))
                tt(zT[:, j, :], zT[:, j, :], nt, ALU.mult).then_inc(q_yev, 1)

            def group_norm(gr):
                dve.wait_ge(q_yev, 6 + 2 * gr)
                norm_scale(6 + gr, 12 + 4 * gr, D // G, nv, ny, nt, 2 + gr)
                for j in range(4 * gr, 4 * gr + 4):
                    stt(zT[:, j, :], zT[:, j, :], ssdw[:, j:j + 1], ny, ALU.mult, ALU.mult).then_inc(yn_ok, 1)
                dve.wait_ge(yn_ok, 4 * gr + 4)

            dve.wait_ge(tile_ev, NT)
            for qd in range(4):
                dve.wait_ge(q_ps, qd + 1)
                if qd:
                    dve.wait_ge(q_y, 2 * qd)
                for i, (c0, n) in enumerate(CHUNKS):
                    tt(MT[0:n, :, c0:c0 + n], ps[0:n, (2, 3, 1)[i], 0:4 * n].rearrange("p (h q) -> p h q", h=4),
                       acs[0:n, i, 4 * qd:4 * qd + 4].unsqueeze(2).to_broadcast([n, 4, n]), ALU.subtract).then_inc(q_diff, 1)
                dve.wait_ge(q_diff, 3 * qd + 3)
                m3 = MT[:, :, 0:TP].rearrange("p h (i q) -> p h i q", i=2)
                tt(m3, m3, upper[:, :].unsqueeze(1).unsqueeze(1).to_broadcast([P, 4, 2, CH]), ALU.mult).then_inc(q_msk, 1)
                ms = MT[0:TS, :, TP:T]
                tt(ms, ms, supper_r[0:TS, :].unsqueeze(1).to_broadcast([TS, 4, TS]), ALU.mult).then_inc(q_msk, 1)
                ada(4 + 2 * qd)
                gr = qd // 2
                dve.wait_ge(q_exp, 3 * qd + 3)
                tt(CTs, CTs, xbcT[:, KD + G + gr, CH:TP].unsqueeze(1).to_broadcast([P, 4, CH]), ALU.mult).then_inc(q_mt, 1)
                tt(MT[:, :, 0:TP], MT[:, :, 0:TP], CBm[:, gr, 0:TP].unsqueeze(1).to_broadcast([P, 4, TP]), ALU.mult).then_inc(q_mt, 1)
                tt(ms, ms, CBm[0:TS, gr, TP:T].unsqueeze(1).to_broadcast([TS, 4, TS]), ALU.mult).then_inc(q_mt, 1)
                ada(5 + 2 * qd)
                if qd == 3:
                    group_norm(0)
                y_out(2 * qd)
                y_out(2 * qd + 1)
            group_norm(1)
            for j in range(KD):
                dve.wait_ge(outa_ps, j + 1)
                link(tt(gates[:, j, :], gates[:, j, :], ps[:, 2 + j % 2, 0:T], ALU.mult))
                tt(gates[:, j, :], gates[:, j, :], gates[:, KD + j, :], ALU.add).then_inc(mrg_ok, 1)

            def residual(j, src, gate, done):
                link(stt(xT[:, j, 0:TP], src[:, 0:TP], mod[:, gate + j, 0:1], xT[:, j, 0:TP], ALU.mult, ALU.add))
                link(tt(sample(nt[:, 0:TS]), sample(src[:, TP:T]), per_sequence(mod[:, gate + j, 1:NC]), ALU.mult))
                tt(xT[:, j, TP:T], xT[:, j, TP:T], nt[:, 0:TS], ALU.add).then_inc(done, 1)

            for j in range(KD):
                dve.wait_ge(mix_ps, j + 1)
                residual(j, ps[:, j % 2, 0:T], 16, x1_ok)
            norm_scale(4, 24, D, nv, ny, nt, 4)
            dve.wait_ge(st_hp, 16)
            normalize(ny)
            modulate(nw2, 24, 32, 2)

            S = [r_[:, k, :].rearrange("p (c e) -> p c e", e=NE) for k in range(40)]
            m3_, g12 = [P, 3, NE], [P, 3 * NG, EPG]

            def col(k):
                return r_[:, k, 0:3]

            def wide(c3):
                return c3.unsqueeze(2).to_broadcast(m3_)

            link(v.memset(score, 0.0))
            link(v.memset(posm, -1.0))
            v.memset(yacc, 0.0).then_inc(cmb_ok, 8)
            dve.wait_ge(lg_ps, 1)
            link(v.tensor_copy(score[:, 0:2, :], ps[:, 6, 0:2 * NE].rearrange("p (c e) -> p c e", e=NE)))
            link(v.tensor_copy(score[0:TS, 2, :], ps[0:TS, 6, 2 * NE:3 * NE]))
            link(v.tensor_reduce(col(5), score, AX_X, ALU.max))
            tt(score, score, wide(col(5)), ALU.subtract).then_inc(sm_in, 1)
            dve.wait_ge(sm_exp, 1)
            link(v.tensor_reduce(col(5), score, AX_X, ALU.add))
            link(v.reciprocal(col(5), col(5)))
            link(tt(score, score, wide(col(5)), ALU.mult))
            link(tt(sel, score, brt[:, :].unsqueeze(1).to_broadcast(m3_), ALU.add))
            s4 = r_[:, 1, :].rearrange("p (c e) -> p c e", e=EPG)
            e4 = [s4[:, :, k] for k in range(4)]
            q = [r_[:, 6 + k, 0:3 * NG] for k in range(8)]
            link(tt(q[0], e4[0], e4[1], ALU.max))
            link(tt(q[1], e4[0], e4[1], ALU.min))
            link(tt(q[2], e4[2], e4[3], ALU.max))
            link(tt(q[3], e4[2], e4[3], ALU.min))
            link(tt(q[4], q[0], q[2], ALU.max))
            link(tt(q[5], q[0], q[2], ALU.min))
            link(tt(q[6], q[1], q[3], ALU.max))
            link(tt(q[5], q[5], q[6], ALU.max))
            link(tt(q[4], q[4], q[5], ALU.add))

            def first_max(vals, key, m, one):
                n = vals.shape[-1]
                bc = [P, 3, n]
                link(v.tensor_reduce(m, vals, AX_X, ALU.max))
                link(tt(one, vals, m.unsqueeze(2).to_broadcast(bc), ALU.is_equal))
                link(tt(one, one, key.unsqueeze(1).to_broadcast(bc), ALU.mult))
                link(v.tensor_reduce(m, one, AX_X, ALU.max))
                link(tt(one, one, m.unsqueeze(2).to_broadcast(bc), ALU.is_equal))

            best = q[7]
            first_max(q[4].rearrange("p (c g) -> p c g", g=NG), keyg[:, :], col(5), best.rearrange("p (c g) -> p c g", g=NG))
            msk, one1, one2 = S[14], S[15], S[16]
            msk4 = r_[:, 14, :].rearrange("p (c e) -> p c e", e=EPG)
            link(tt(msk4, s4, best.unsqueeze(2).to_broadcast(g12), ALU.mult))
            link(ts(q[0], best, -1.0, BIG, ALU.add, ALU.mult))
            link(tt(msk4, msk4, q[0].unsqueeze(2).to_broadcast(g12), ALU.add))
            first_max(msk, keye[:, :], col(5), one1)
            link(stt(msk, one1, -BIG, msk, ALU.mult, ALU.add))
            first_max(msk, keye[:, :], col(5), one2)
            tt(s_all, one1, one2, ALU.add).then_inc(top_ok, 1)
            dve.wait_ge(top_ok, 1)
            link(tt(comb, score, s_all, ALU.mult))
            link(v.tensor_reduce(col(5), comb, AX_X, ALU.add))
            link(v.reciprocal(col(5), col(5)))
            link(tt(comb, comb, wide(col(5)), ALU.mult))
            dve.wait_ge(pos_ps, 1)
            for rr, cc in ((P, slice(0, 2)), (TS, slice(2, 3))):
                pp = ps[0:rr, 7, 0:3 * NE].rearrange("p (c e) -> p c e", e=NE)[:, cc, :]
                link(stt(posm[0:rr, cc, :], pp, 1.0, s_all[0:rr, cc, :], ALU.add, ALU.mult))
            link(ts(posm, posm, -1.0, None, ALU.add))
            link(v.tensor_reduce(npf[:, 1:2], ps[:, 7, 48:64], AX_X, ALU.max))
            link(v.memset(npf[:, 2:3], 1.0))
            for k in range(1, MAXPASS):
                link(stt(npf[:, 2:3], npf[:, 1:2], float(CAP * k), npf[:, 2:3], ALU.is_gt, ALU.add))
            v.tensor_copy(npi[:, :], npf[:, 2:3]).then_inc(route_ok, 1)
            dve.wait_ge(route_ok, 1)

            b4 = [P, 3, 2, CAP]

            def choose(q, v_, first, after=None):
                if not first:
                    dve.wait_ge(xg_ps[1], v_)
                    dve.wait_ge(selw_ok, v_)
                if after is not None:
                    dve.wait_ge(pos_dn, after)
                tt(selo, iota[:, :].unsqueeze(1).unsqueeze(1).to_broadcast(b4),
                   posm[:, :, bass.ds(2 * q, 2)].unsqueeze(3).to_broadcast(b4), ALU.is_equal).then_inc(selo_ok, 1)

            def add_up(v_):
                dve.wait_ge(cmb_ok, 8 * v_ + 8)
                for j in range(KD):
                    dve.wait_ge(cmb_ps, 8 * v_ + j + 1)
                    tt(yacc[:, j, :], yacc[:, j, :], ps[:, (7, 4)[j % 2], 0:T], ALU.add).then_inc(cmb_ok, 1)

            def experts(q, v_, first, prev, following):
                dve.wait_ge(selo_ok, v_ + 1)
                if not first:
                    dve.wait_ge(pT_ps, v_)
                tt(selw, selo, comb[:, :, bass.ds(2 * q, 2)].unsqueeze(3).to_broadcast(b4), ALU.mult).then_inc(selw_ok, 1)
                if following:
                    choose(q + 1, v_ + 1, False)
                if prev:
                    add_up(v_ - 1)
                dve.wait_ge(act_s, v_ + 1)
                dve.wait_ge(unit_used, N_UNITS + 6 * v_ + 4)
                if not first:
                    dve.wait_ge(aT_ps, v_)
                tt(act_e[:, :], hs_[:, :], ps[:, 3, :], ALU.mult).then_inc(act_ok, 1)
                dve.wait_ge(pT_ps, v_ + 1)
                v.tensor_copy(pT[:, :], ps[:, 7, 0:T]).then_inc(pT_ok, 1)

            choose(0, 0, True)
            experts(0, 0, True, False, True)
            with dve.Fori(1, PAIRS - 1) as q_:
                experts(q_, q_, False, True, True)
            experts(PAIRS - 1, PAIRS - 1, False, True, False)
            add_up(PAIRS - 1)
            passes = dve.value_load(npi[0:1, 0:1], min_val=1, max_val=MAXPASS)
            with dve.If(passes > 1):
                with dve.Fori(1, passes) as n_:
                    v0 = n_ * PAIRS
                    dve.wait_ge(selo_ok, v0)
                    ts(posm, posm, -float(CAP), None, ALU.add).then_inc(pos_dn, 1)
                    choose(0, v0, False, n_)
                    experts(0, v0, False, False, True)
                    with dve.Fori(1, PAIRS - 1) as q_:
                        experts(q_, n_ * PAIRS + q_, False, True, True)
                    experts(PAIRS - 1, v0 + (PAIRS - 1), False, True, False)
                    add_up(v0 + (PAIRS - 1))

            dve.wait_ge(cmb_ok, 8 * PAIRS * passes + 8)
            for j in range(KD):
                residual(j, yacc[:, j, :], 40, x2_ok)
            norm_scale(5, 32, D, nv, ny, nt, 5)
            for j in range(KD):
                stt(hT[:, j, :], xT[:, j, :], fnw[:, j:j + 1], ny, ALU.mult, ALU.mult).then_inc(fin_ok, 1)


_OUTS = [("y_prompt", (1, TP, D)), ("y_sample", (NBATCH, LSAMP, D)),
         ("ssm_prompt", (1, 1, H, HD, NS)), ("ssm_sample", (1, NBATCH, H, HD, NS)),
         ("conv_prompt", (1, 1, CONV - 1, XBC)), ("conv_sample", (1, NBATCH, CONV - 1, XBC)),
         ("s5_re_prompt", (1, 1, S5G, S5N)), ("s5_re_sample", (1, NBATCH, S5G, S5N)),
         ("s5_im_prompt", (1, 1, S5G, S5N)), ("s5_im_sample", (1, NBATCH, S5G, S5N))]


def kernel(**inputs):
    import numpy as _np
    import concourse.bacc as _bacc
    from concourse import mybir as _mybir
    from concourse.bass_utils import run_bass_kernel_spmd as _run

    nc = _bacc.Bacc("TRN2", target_bir_lowering=False, num_devices=1, dynamic_dma_scratch_size=1024)
    arrays, a, o = {}, {}, {}
    for name, x in inputs.items():
        x = _np.ascontiguousarray(x)
        arrays[f"in_{name}"] = x
        a[name] = nc.dram_tensor(f"in_{name}", x.shape, _mybir.dt.from_np(x.dtype), kind="ExternalInput").ap()
    for name, shape in _OUTS:
        o[name] = nc.dram_tensor(f"out_{name}", shape, _mybir.dt.float32, kind="ExternalOutput").ap()
    hybrid_decoder_step(nc, a, o)
    r = _run(nc, [arrays], core_ids=[0])
    return tuple(r.results[0][f"out_{name}"] for name, _ in _OUTS)
```

```python
from contextlib import ExitStack

import concourse.bass as bass
from concourse import mybir

F32 = mybir.dt.float32
I32 = mybir.dt.int32
ALU = mybir.AluOpType
ACT = mybir.ActivationFunctionType
AX_X = mybir.AxisListType.X

P = 128
BANK = 512
D = 1024
KD = D // P
NBATCH, LSAMP = 8, 4
TP, TS = 256, NBATCH * LSAMP
T = TP + TS
CH = 128
CHUNKS = [(0, 128), (128, 128), (256, 32)]
NC = 1 + NBATCH
H, HD, NS = 16, 64, 128
G = 2
CONV = 4
XBC = D + 2 * G * NS
XT = XBC // P
S5G, S5N, S5C = 32, 64, 16
S5T = S5G * S5N // P
UT = S5G * S5C // P
NE, NG, EPG = 16, 4, 4
FE = 512
FT = FE // P
CAP = 64
PAIRS = NE // 2
MAXPASS = -(-T // CAP)
NH0 = 4
EPS = 1e-6
IN_XBC, IN_DT, IN_U, IN_GATE = D, D + XBC, D + XBC + H, D + XBC + H + S5G * S5C
TWO_PI = 6.283185307179586
TWO_PI_HI = 6.28125
ROUND = 12582912.0
PI_IN = 3.1415925
BIG = 1e30

SLOT = 4096
NR = 5
MOE_SLOTS = [3, 4, 0, 1, 2, 5]
U_ADA1, U_U, U_XBC, U_Z, U_GATE, U_GLU, U_ADA2, U_OUTA, U_OUT, N_UNITS = 0, 4, 5, 8, 10, 14, 16, 24, 26, 28


def uses(slot):
    return len([n for n in range(N_UNITS) if n % NR == slot])


def ada_unit(i):
    return U_ADA1 + i if i < 4 else U_ADA2 + i - 4


def hybrid_decoder_step(nc, a, o):
    with ExitStack() as ctx:
        def sb(name, cols, dt=F32):
            return ctx.enter_context(nc.sbuf_tensor(name, [P, cols], dt))

        def sem(name):
            return ctx.enter_context(nc.semaphore(name))

        def part(region, off, *shape):
            n = 1
            for s in shape:
                n *= s
            v = region[:, off:off + n]
            if len(shape) == 2:
                return v.rearrange("p (a b) -> p a b", b=shape[1])
            if len(shape) == 3:
                return v.rearrange("p (a b c) -> p a b c", b=shape[1], c=shape[2])
            return v

        ring = sb("ring", NR * SLOT)
        tok_r = sb("tok_region", 3 * D)
        xT = part(sb("x_features", KD * T), 0, KD, T)
        hT_r = sb("h_region", KD * T)
        hT = part(hT_r, 0, KD, T)
        u_r = sb("u_region", UT * T)
        uT = part(u_r, 0, UT, T)
        xbc_r = sb("xbc_region", XT * T)
        xbcT = part(xbc_r, 0, XT, T)
        z_r = sb("z_region", KD * T)
        zT = part(z_r, 0, KD, T)
        gate_r = sb("gate_region", 2 * KD * T)
        gates = part(gate_r, 0, 2 * KD, T)
        mix_r = sb("mixer_region", 13312)
        conv_r = sb("conv_region", 2 * 315)

        x_tok = part(tok_r, 0, 3, D)
        s5x = part(tok_r, 0, 2, S5T, TS)
        s5h = part(tok_r, 2 * S5T * TS, 2, S5T, TS)
        Xdt = part(tok_r, 0, 3, D)

        c_in = part(gate_r, 0, D)
        prow1 = part(gate_r, 1024, P)
        prow2 = part(gate_r, 1152, P)
        prow3 = part(gate_r, 1280, P)
        b_raw = part(gate_r, 1408, 2, S5T, S5C)
        c_raw = part(gate_r, 1920, 2, UT, S5N)
        st_rows = part(gate_r, 2432, 2, P)
        exp_in = part(gate_r, 2688, 4)
        conv_in = part(gate_r, 2692, XBC)
        n1v, n1y, n1t = (part(z_r, k * T, T) for k in range(3))
        nv, ny, nt = (part(u_r, k * T, T) for k in range(3))
        sq = part(conv_r, 0, 2, T)
        rows = part(conv_r, 0, 2, 315)

        rotc = part(mix_r, 0, S5T, TP)
        rots = part(mix_r, S5T * TP, S5T, TP)
        off = 2 * S5T * TP
        bT = part(mix_r, off, 2, UT, P)
        cTs5 = part(mix_r, off + 1024, 2, UT, P)
        g5 = part(mix_r, off + 2048, 4, TP)
        h5 = part(mix_r, off + 3072, 4, TP)
        pt = part(mix_r, off + 4096, 2, TP)
        bblk = part(z_r, 3 * T, 2, S5T, 2 * S5C)
        cblk = part(gate_r, 0, 2, UT, P)
        vt = part(conv_r, 0, 2, TP)
        Xs = part(mix_r, 0, 3, D)
        B_tok = part(mix_r, 3072, 3, 2 * NS)
        CBm = part(mix_r, 3840, 2, T)
        CTs = part(mix_r, 4416, 4, CH)
        h1T = part(mix_r, 4928, 2, 512)
        hfT = part(mix_r, 5952, 2, 512)
        h0 = [part(mix_r, 6976, NBATCH, NS), part(mix_r, 8000, NBATCH, NS), part(hT_r, 1024, NBATCH, NS),
              part(mix_r, 10048, NBATCH, NS)]
        h0T = part(mix_r, 9024, NBATCH * NS)
        yraw = part(hT_r, 2048, 2, P)
        Bm = part(mix_r, 11072, 2, NBATCH * NS)
        h_out = part(mix_r, 9024, 8, P)
        MTs = part(mix_r, 3072, H, TS)
        MT = part(hT_r, 0, 4, TP)

        cT = part(sb("c_features", KD * 32), 0, KD, 32)
        ada_s = part(sb("ada_sum", 512), 0, 512)
        mod = part(sb("modulation", 48 * NC), 0, 48, NC)
        amul = part(sb("norm_scale", KD * NC), 0, KD, NC)
        ident = sb("ident", P)
        ones = sb("ones", P)
        upper = sb("upper", P)
        strict = sb("strict", P)
        same_r = sb("same_sequence", TS)
        supper_r = sb("same_upper", TS)
        blk = sb("sequence_of", NBATCH)
        sel9 = sb("fold_rows", 32)
        par8 = sb("group_rows", 8)
        par2 = sb("group_parity", 2)
        iota = sb("slot_number", CAP)
        keyg = sb("group_key", NG)
        keye = sb("expert_key", NE)
        pc1 = sb("params1", 104)
        pc2 = sb("params2", 80)
        pc3 = sb("params3", 16)
        cs_r = sb("conv_state", XT * 24)
        csT = part(cs_r, 0, XT, 24)
        tails_r = sb("conv_tails", XT * 27)
        tails = part(tails_r, 0, XT, 27)
        w_dt = part(sb("w_dt", KD * H), 0, KD, H)
        w_rt = part(sb("w_router", KD * NE), 0, KD, NE)
        dtb = sb("dt_bias_row", H)
        alog = sb("a_log_row", H)
        brt = sb("b_router_row", NE)
        dt3 = part(sb("dt", 3 * H), 0, 3, H)
        da3 = part(sb("dta", 3 * H), 0, 3, H)
        dtt = part(sb("dt_tmp", 3 * H), 0, 3, H)
        dte = part(sb("decay_to_end", 3 * H), 0, 3, H)
        acs = part(sb("a_cumsum", 3 * 2 * H), 0, 3, 2 * H)
        eft = part(tails_r, 0, KD, TS)
        yoff = part(cs_r, 0, KD, TS)
        s5c = part(tok_r, 2048, 24, S5T)
        st5_flat = tok_r[:, 2432:2432 + 2 * P]
        st5 = part(tok_r, 2432, 2, NBATCH, S5T)
        fin5 = part(tok_r, 2688, 2, S5T)
        npf = sb("passes_f", 8)
        npi = sb("passes_i", 1, I32)

        ps = ctx.enter_context(nc.psum_tensor("psum", [P, 8, BANK], F32))

        nw1, nw2, ssdw = pc1[:, 0:8], pc1[:, 8:16], pc1[:, 16:24]
        convw = pc1[:, 24:72].rearrange("p (k j) -> p k j", j=XT)
        convb, s5d, fnw, dskip = pc1[:, 72:84], pc1[:, 84:88], pc1[:, 88:96], pc1[:, 96:104]
        b_ada, a_re, a_im = pc2[:, 0:48], pc2[:, 48:64], pc2[:, 64:80]

        ld_x, ld_c, ld_par, ld_exp, ld_state5, ld_conv, ld_bc, ld_rows, ld_wdt, ld_wrt = (
            sem(n) for n in ("ld_x", "ld_c", "ld_par", "ld_exp", "ld_state5", "ld_conv", "ld_bc", "ld_rows", "ld_wdt", "ld_wrt"))
        ld_h0 = [sem(f"ld_h0_{i}") for i in range(NH0)]
        landed = [sem(f"ring_landed{i}") for i in range(NR + 1)]
        unit_used = sem("unit_used")
        consts = sem("consts")
        vconsts = sem("vector_consts")
        dte_pre, q_msk, sm_in, sm_exp = sem("dte_pre"), sem("q_masked"), sem("softmax_in"), sem("softmax_exp")
        pos_dn = sem("positions_down")
        expd = sem("expanded")
        c_silu, cT_ps, cT_ok = sem("c_silu"), sem("cT_ps"), sem("cT_ok")
        par_ps, par_ok = sem("par_ps"), sem("par_ok")
        x_ps, x_ok = sem("x_ps"), sem("x_ok")
        sq_ok, sq_used = sem("sq_ok"), sem("sq_used")
        var_ok, rs_ok = sem("var_ok"), sem("rs_ok")
        ada_cp, adaT_ps, mod_ok = sem("ada_cp"), sem("adaT_ps"), sem("mod_ok")
        xn_ok, amul_ok, hm_ok = sem("x_normed"), sem("norm_scale_ok"), sem("h_sample_scaled")
        h_ok, hp_ok = sem("h_sample_ok"), sem("h_prompt_ok")
        tile_ps, tile_ev = sem("tile_ps"), sem("tile_ev")
        conv_acc, conv_ok = sem("conv_acc"), sem("conv_ok")
        dt_ps, dt_pre, dt_exp, da_ok = sem("dt_ps"), sem("dt_pre"), sem("dt_exp"), sem("da_ok")
        tail_ps, tail_cp = sem("tail_ps"), sem("tail_cp")
        dsc, trig, rot_u, rot_ok = sem("s5_discrete"), sem("s5_trig"), sem("rot_u"), sem("rot_ok")
        blk5, s5w_ps, s5w_ok = sem("s5_blocks"), sem("s5w_ps"), sem("s5w_ok")
        s5_x, s5_xused, s5_g, s5_h, s5_hused = sem("s5_x"), sem("s5_x_used"), sem("s5_g"), sem("s5_h"), sem("s5_h_used")
        s5_y, s5_yev, s5_hs = sem("s5_y"), sem("s5_y_ev"), sem("s5_hs")
        gelu_ok = sem("gelu_ok")
        s5f_ps, s5f_cp = sem("s5f_ps"), sem("s5f_cp")
        glu_ps, glu_sig, glu_ev = sem("glu_ps"), sem("glu_sig"), sem("glu_ev")
        cb_ps, cb_ok, acs_ps, acs_ok, dte_ok = sem("cb_ps"), sem("cb_ok"), sem("acs_ps"), sem("acs_ok"), sem("dte_ok")
        xt_ps, xdt_ok, xs_ok, bt_ok = sem("xt_ps"), sem("xdt_ok"), sem("xs_ok"), sem("bt_ok")
        st_ps, h1_ok, hf_ok, hf_ps, hf_cp = sem("st_ps"), sem("h1_ok"), sem("hf_ok"), sem("hf_ps"), sem("hf_cp")
        h0_ps, h0_cp, yo_ps, ss_ps, ss_ok = sem("h0_ps"), sem("h0_cp"), sem("yo_ps"), sem("ss_ps"), sem("ss_ok")
        qs_ps, qs_diff, qs_msk, qs_exp, qs_ok = (sem(n) for n in ("qs_ps", "qs_diff", "qs_masked", "qs_exp", "qs_ok"))
        yo_cp, yoT_ps = sem("yo_copied"), sem("yoT_ps")
        h0_dec, yoff_ok = sem("h0_decayed"), sem("yoff_ok")
        q_ps, q_diff, q_exp, q_mt, q_y, q_yev = sem("q_ps"), sem("q_diff"), sem("q_exp"), sem("q_mt"), sem("q_y"), sem("q_yev")
        bm_ok, yn_ok = sem("bm_ok"), sem("yn_ok")
        outa_ps, mrg_ok = sem("outa_ps"), sem("merged_ok")
        mix_ps, x1_ok = sem("mix_ps"), sem("x1_ok")
        h2t_ps, h2t_ok = sem("h2t_ps"), sem("h2t_ok")
        lg_ps, top_ok, pos_ps, route_ok = sem("logits_ps"), sem("top_ok"), sem("pos_ps"), sem("route_ok")
        selo_ok, selw_ok, xe_ok = sem("chosen"), sem("weights_chosen"), sem("xe_ok")
        xg_ps = [sem("gathered_first_half"), sem("gathered_second_half")]
        act_s, act_ok = sem("act_silu"), sem("act_ok")
        aT_ps, aT_ok, pT_ps, pT_ok = sem("aT_ps"), sem("aT_ok"), sem("pT_ps"), sem("pT_ok")
        w2_ps, ye_ok, cmb_ps, cmb_ok = sem("w2_ps"), sem("ye_ok"), sem("combine_ps"), sem("combine_ok")
        x2_ok, fin_ok, fin_ps, fin_cp, fin_rs = sem("x2_ok"), sem("fin_ok"), sem("fin_ps"), sem("fin_cp"), sem("fin_rs")
        st_conv, st_s5, st_hp, st_y = sem("st_conv"), sem("st_s5"), sem("st_ssm_prompt"), sem("st_y")
        st_hs = [sem(f"st_ssm_{i}") for i in range(NH0)]
        dve_chain, act_chain, pool_chain = sem("dve_chain"), sem("act_chain"), sem("pool_chain")

        def linker(eng, chain):
            n = [0]

            def link(ins):
                n[0] += 1
                ins.then_inc(chain, 1)
                eng.wait_ge(chain, n[0])
            return link

        def ring_tile(slot, k):
            base = ring[:, slot * SLOT:(slot + 1) * SLOT] if slot < NR else mix_r[:, 0:SLOT]
            return base.rearrange("p (k n) -> p k n", k=k)

        def unit_tile(n, k):
            return ring_tile(n % NR, k)

        def sums_bank(i):
            return 5 if i < 4 else 6

        def turned(i, c0, c1):
            bank, at = (6, 0) if i < 4 else (7, 256)
            return ps[:, bank, at + c0 * NC:at + c1 * NC]

        def sample(v):
            return v.rearrange("p (b l) -> p b l", l=LSAMP)

        h2_tok = part(tok_r, 0, 3, D)
        y_tok = part(tok_r, 0, 3, D)
        yacc = part(xbc_r, 0, KD, T)
        selw = part(xbc_r, KD * T, 3, 2, CAP)
        selw2 = selw.rearrange("p c e s -> p c (e s)")
        selo = part(xbc_r, KD * T + 384, 3, 2, CAP)
        selo2 = selo.rearrange("p c e s -> p c (e s)")
        Xe = part(gate_r, 0, KD, P)
        hs_ = part(gate_r, 1024, FE)
        act_e = part(gate_r, 1536, FE)
        actT = part(gate_r, 2048, FT, P)
        y_e = part(gate_r, 2560, D)
        pT = part(gate_r, 3584, T)
        tok_v, tok_rs, tok_t = (part(z_r, 40 * 3 * NE + 4 * k, 3) for k in range(3))
        r_ = part(z_r, 0, 40, 3 * NE)
        score, sel, comb, posm, s_all = (r_[:, k, :].rearrange("p (c e) -> p c e", e=NE) for k in range(5))

        tiles = ([("u", j) for j in range(UT)] + [("x", j) for j in range(XT)]
                 + [("z", j) for j in range(KD)] + [("g", j) for j in range(2 * KD)])
        T_XBC, T_Z, NT = UT, UT + XT, len(tiles)

        def s5_steps(n):
            return [i for i in range(S5T) if (4 * i) // 3 == n]

        block = ctx.enter_context(nc.Block())

        @block.sync
        def _(sp):
            def weights(n):
                if n < 4:
                    return a["w_ada"][0, :, n * 512:(n + 1) * 512], KD
                if n < U_XBC:
                    return a["w_in"][0, :, IN_U:IN_U + 512], KD
                if n < U_Z:
                    return a["w_in"][0, :, IN_XBC + (n - U_XBC) * 512:IN_XBC + (n - U_XBC + 1) * 512], KD
                if n < U_GATE:
                    return a["w_in"][0, :, (n - U_Z) * 512:(n - U_Z + 1) * 512], KD
                if n < U_GLU:
                    return a["w_in"][0, :, IN_GATE + (n - U_GATE) * 512:IN_GATE + (n - U_GATE + 1) * 512], KD
                if n < U_ADA2:
                    return a["w_glu"][0, :, (n - U_GLU) * D:(n - U_GLU + 1) * D], UT
                if n < U_OUTA:
                    i = n - U_ADA2 + 4
                    return a["w_ada"][0, :, i * 512:(i + 1) * 512], KD
                if n < U_OUT:
                    return a["w_out_a"][0, :, (n - U_OUTA) * 512:(n - U_OUTA + 1) * 512], KD
                return a["w_out"][0, :, (n - U_OUT) * 512:(n - U_OUT + 1) * 512], KD

            for n in range(N_UNITS):
                if n >= NR:
                    sp.wait_ge(unit_used, n - NR + 1)
                if n == 0:
                    sp.wait_ge(ld_c, 32)
                elif n == 1:
                    sp.wait_ge(ld_par, 16 * 10)
                src, k = weights(n)
                sp.dma_start(unit_tile(n, k), src.rearrange("(k p) n -> p k n", p=P)).then_inc(landed[n % NR], 16)

            def pair_weights(pair, used):
                for r, (w, k) in enumerate((("w1", KD), ("w1", KD), ("w3", KD), ("w3", KD), ("w2", FT), ("w2", FT))):
                    s = MOE_SLOTS[r]
                    sp.wait_ge(unit_used, used(r))
                    src = a[w][0, bass.ds(2 * pair + r % 2, 1), :, :].rearrange("e (k p) n -> p (e k) n", p=P)
                    sp.dma_start(ring_tile(s, k), src).then_inc(landed[s], 16)

            def first_used(r):
                if r == 5:
                    sp.wait_ge(st_hp, 16)
                    for b in range(NH0):
                        sp.wait_ge(st_hs[b], 16 * len(range(b, KD, NH0)))
                    return U_OUT
                return max(n for n in range(N_UNITS) if n % NR == MOE_SLOTS[r]) + 1

            pair_weights(0, first_used)
            with sp.Fori(1, PAIRS) as q:
                pair_weights(q, lambda r: N_UNITS + 6 * (q - 1) + r + 1)
            sp.wait_ge(route_ok, 1)
            passes = sp.value_load(npi[0:1, 0:1], min_val=1, max_val=MAXPASS)
            with sp.If(passes > 1):
                with sp.Fori(1, passes) as n:
                    with sp.Fori(0, PAIRS) as q:
                        pair_weights(q, lambda r: N_UNITS + 6 * ((n * PAIRS - 1) + q) + r + 1)

            sp.wait_ge(fin_cp, 6)
            for i, (t0, n) in enumerate(CHUNKS[:2]):
                sp.dma_start(o["y_prompt"][0, t0:t0 + n, :], y_tok[0:n, i, :]).then_inc(st_y, 16)
            sp.dma_start(o["y_sample"].rearrange("b l d -> (b l) d"), y_tok[0:TS, 2, :]).then_inc(st_y, 16)
            sp.wait_ge(st_y, 48)
            sp.wait_ge(st_conv, 32)
            sp.wait_ge(st_s5, 64)

        @block.gpsimd
        def _(pool):
            link = linker(pool, pool_chain)
            g = nc.gpsimd

            def keep(out, in_, pattern, mult, base, op=ALU.is_ge):
                return g.affine_select(out=out, in_=in_, compare_op=op, fill=0.0, base=base,
                                       pattern=pattern, channel_multiplier=mult)

            link(g.memset(par8[:], 1.0))
            link(g.memset(strict[:], 1.0))
            link(g.memset(same_r[0:TS, :], 1.0))
            link(g.memset(blk[0:TS, :], 1.0))
            link(g.memset(ident[:], 0.0))
            g.affine_select(out=ident[:], in_=ident[:], compare_op=ALU.not_equal, fill=1.0, base=0,
                            pattern=[[-1, P]], channel_multiplier=1).then_inc(consts, 1)
            link(g.memset(upper[:], 1.0))
            keep(upper[:], upper[:], [[1, P]], -1, 0).then_inc(consts, 1)
            keep(strict[:], strict[:], [[1, P]], -1, -1).then_inc(consts, 1)
            same3 = sample(same_r[0:TS, :])
            link(keep(same3, same3, [[-LSAMP, NBATCH], [0, LSAMP]], 1, 0))
            link(keep(same3, same3, [[LSAMP, NBATCH], [0, LSAMP]], -1, LSAMP - 1))
            keep(supper_r[0:TS, :], same_r[0:TS, :], [[1, TS]], -1, 0).then_inc(consts, 1)
            link(keep(blk[0:TS, :], blk[0:TS, :], [[-LSAMP, NBATCH]], 1, 0))
            keep(blk[0:TS, :], blk[0:TS, :], [[LSAMP, NBATCH]], -1, LSAMP - 1).then_inc(consts, 1)
            p8 = par8[:].rearrange("p (q h) -> p q h", q=2)
            link(keep(p8, p8, [[-S5C, 2], [-2 * S5C, 4]], 1, 0))
            keep(p8, p8, [[S5C, 2], [2 * S5C, 4]], -1, S5C - 1).then_inc(consts, 1)
            g.iota(iota[:], [[1, CAP]], base=0, channel_multiplier=0,
                   allow_small_or_imprecise_dtypes=True).then_inc(consts, 1)
            g.iota(keyg[:], [[-1, NG]], base=NG, channel_multiplier=0,
                   allow_small_or_imprecise_dtypes=True).then_inc(consts, 1)
            g.iota(keye[:], [[-1, NE]], base=NE, channel_multiplier=0,
                   allow_small_or_imprecise_dtypes=True).then_inc(consts, 1)

            pool.wait_ge(rot_u, 1)
            wc, ws = [s5c[:, 0, :], s5c[:, 2, :]], [s5c[:, 1, :], s5c[:, 3, :]]
            link(g.memset(rotc[:, :, 0:1], 1.0))
            link(g.memset(rots[:, :, 0:1], 0.0))
            k, lv = 1, 0
            J = 64
            ta, tb = part(mix_r, off + 2048, S5T, J), part(mix_r, off + 3072, S5T, J)
            while k < TP:
                wcb = wc[lv % 2].unsqueeze(2)
                wsb = ws[lv % 2].unsqueeze(2)
                for j0 in range(0, k, J):
                    kk = min(k, J)
                    lo, hi = slice(j0, j0 + kk), slice(k + j0, k + j0 + kk)
                    bc = [P, S5T, kk]
                    A, B = ta[:, :, 0:kk], tb[:, :, 0:kk]
                    link(g.tensor_tensor(A, rotc[:, :, lo], wcb.to_broadcast(bc), ALU.mult))
                    link(g.tensor_tensor(B, rots[:, :, lo], wsb.to_broadcast(bc), ALU.mult))
                    link(g.tensor_tensor(rotc[:, :, hi], A, B, ALU.subtract))
                    link(g.tensor_tensor(A, rotc[:, :, lo], wsb.to_broadcast(bc), ALU.mult))
                    link(g.tensor_tensor(B, rots[:, :, lo], wcb.to_broadcast(bc), ALU.mult))
                    link(g.tensor_tensor(rots[:, :, hi], A, B, ALU.add))
                if 2 * k < TP:
                    c0, s0, c1, s1 = wc[lv % 2], ws[lv % 2], wc[(lv + 1) % 2], ws[(lv + 1) % 2]
                    t4 = s5c[:, 4, :]
                    link(g.tensor_tensor(c1, c0, c0, ALU.mult))
                    link(g.tensor_tensor(t4, s0, s0, ALU.mult))
                    link(g.tensor_tensor(c1, c1, t4, ALU.subtract))
                    link(g.tensor_tensor(s1, c0, s0, ALU.mult))
                    link(g.tensor_tensor(s1, s1, s1, ALU.add))
                k, lv = 2 * k, lv + 1
            g.tensor_copy(rotc[:, 0, 0:1], rotc[:, 0, 0:1]).then_inc(rot_ok, 1)

            for i in range(S5T):
                q = i % 2
                gr, gi, hr, hi = g5[:, 2 * q, :], g5[:, 2 * q + 1, :], h5[:, 2 * q, :], h5[:, 2 * q + 1, :]
                c_, s_ = rotc[:, i, :], rots[:, i, :]
                pool.wait_ge(s5_g, i + 1)
                if i >= 2:
                    pool.wait_ge(s5_hused, i - 1)
                link(g.tensor_tensor(pt[:, 0, :], gr, c_, ALU.mult))
                link(g.tensor_tensor(pt[:, 1, :], gi, s_, ALU.mult))
                link(g.tensor_tensor(hr, pt[:, 0, :], pt[:, 1, :], ALU.subtract))
                link(g.tensor_tensor(pt[:, 0, :], gr, s_, ALU.mult))
                link(g.tensor_tensor(pt[:, 1, :], gi, c_, ALU.mult))
                link(g.tensor_tensor(hi, pt[:, 0, :], pt[:, 1, :], ALU.add))
                link(g.tensor_copy(fin5[:, 0, i:i + 1], hr[:, TP - 1:TP]))
                g.tensor_copy(fin5[:, 1, i:i + 1], hi[:, TP - 1:TP]).then_inc(s5_h, 1)

            pool.wait_ge(dte_ok, 1)
            for i, (t0, n) in enumerate(CHUNKS):
                pool.wait_ge(xdt_ok, 2 * i + 2)
                g.tensor_tensor(Xs[0:n, i, :].rearrange("p (h d) -> p h d", d=HD),
                                Xdt[0:n, i, :].rearrange("p (h d) -> p h d", d=HD),
                                dte[0:n, i, :].unsqueeze(2).to_broadcast([n, H, HD]), ALU.mult).then_inc(xs_ok, 1)
            pool.wait_ge(bt_ok, 3)
            for gr in range(G):
                g.tensor_tensor(Bm[0:TS, gr, :].rearrange("p (b n) -> p b n", n=NS),
                                B_tok[0:TS, 2, gr * NS:(gr + 1) * NS].unsqueeze(1).to_broadcast([TS, NBATCH, NS]),
                                blk[0:TS, :].unsqueeze(2).to_broadcast([TS, NBATCH, NS]), ALU.mult).then_inc(bm_ok, 1)

        @block.tensor
        def _(pe):
            def mm(out, lhsT, rhs, first, last):
                return nc.tensor.matmul(out, lhsT, rhs, start=first, stop=last, skip_group_check=True)

            def tr(out, in_):
                return nc.tensor.transpose(out, in_, ident[0:in_.shape[0], 0:in_.shape[0]])

            def wait_unit(n):
                pe.wait_ge(landed[n % NR], 16 * (n // NR + 1))

            pe.wait_ge(consts, 9)
            pe.wait_ge(vconsts, 3)
            pe.wait_ge(c_silu, 1)
            for j in range(KD):
                last = tr(ps[:, 6, j * NC:(j + 1) * NC], c_in[0:NC, j * P:(j + 1) * P])
            last.then_inc(cT_ps, 1)

            def square_sum(bank, n, first, last):
                pe.wait_ge(sq_ok, n + 1)
                mm(ps[:, bank, 0:T], ones[:], sq[:, n % 2, :], first, last).then_inc(sq_used, 1)

            def square_sums(bank, tiles_, base):
                for j in range(tiles_):
                    square_sum(bank, base + j, j == 0, j == tiles_ - 1)

            pe.wait_ge(ld_x, 32)
            for j in range(KD):
                if j >= 2:
                    pe.wait_ge(x_ok, j - 1)
                for i, (t0, n) in enumerate(CHUNKS):
                    last = tr(ps[:, j % 2, t0:t0 + n], x_tok[0:n, i, j * P:(j + 1) * P])
                last.then_inc(x_ps, 1)
                if j:
                    square_sum(4, j - 1, j == 1, False)
            square_sum(4, KD - 1, False, True)

            pe.wait_ge(ld_par, 16 * 10)
            pe.wait_ge(expd, 2)
            tr(ps[:, 7, 0:104], prow1[0:104, :])
            tr(ps[:, 7, 128:208], prow2[0:80, :])
            tr(ps[:, 7, 256:272], prow3[0:16, :]).then_inc(par_ps, 1)

            def ada(i):
                n = ada_unit(i)
                w = unit_tile(n, KD)
                wait_unit(n)
                pe.wait_ge(cT_ok, 1)
                if i >= 1:
                    pe.wait_ge(ada_cp, i)
                for r in range(2):
                    for c in range(4):
                        last = mm(ps[32 * c:32 * c + 32, sums_bank(i), :], cT[:, 4 * r + c, :], w[:, 4 * r + c, :], r == 0, r == 1)
                last.then_inc(unit_used, 1)

            def ada_turn(i):
                pe.wait_ge(ada_cp, i + 1)
                if i >= 1:
                    pe.wait_ge(mod_ok, i)
                if i >= 4:
                    pe.wait_ge(yoff_ok, i - 3)
                for c in range(4):
                    last = mm(turned(i, c, c + 1), ada_s[:, c * P:(c + 1) * P], sel9[:, 0:NC], c == 0, c == 3)
                last.then_inc(adaT_ps, 1)

            for i in range(4):
                ada(i)
                ada_turn(i)

            def state_columns():
                pe.wait_ge(ld_state5, 32)
                for q in range(2):
                    tr(ps[:, 2, q * P:(q + 1) * P], st_rows[:, q, :])
                pe.wait_ge(ld_conv, 16)
                for j in range(XT):
                    last = tr(ps[:, 3, j * 24:(j + 1) * 24], conv_in[0:24, j * P:(j + 1) * P])
                last.then_inc(cT_ps, 1)

            def tile(t):
                n = U_U + t // 4
                w = unit_tile(n, KD)
                wait_unit(n)
                if t >= 2:
                    pe.wait_ge(tile_ev, t - 1)
                for k in range(KD):
                    if t == 0:
                        pe.wait_ge(hp_ok, k + 1)
                        pe.wait_ge(h_ok, 1)
                    last = mm(ps[:, t % 2, 0:T], w[:, k, (t % 4) * P:(t % 4 + 1) * P], hT[:, k, :], k == 0, k == KD - 1)
                last.then_inc(tile_ps, 1)
                if t % 4 == 3:
                    pe.wait_ge(tile_ps, t + 1)
                    pe.nop().then_inc(unit_used, 1)

            for t in range(T_Z):
                if t == T_XBC:
                    state_columns()
                tile(t)
            pe.wait_ge(ld_wdt, 16)
            pe.wait_ge(par_ok, 2)
            for i, (t0, n) in enumerate(CHUNKS):
                for k in range(KD):
                    last = mm(ps[0:n, 2, i * H:(i + 1) * H], hT[:, k, t0:t0 + n], w_dt[:, k, :], k == 0, k == KD - 1)
            last.then_inc(dt_ps, 1)

            pe.wait_ge(blk5, 2)
            for q in range(2):
                for j in range(UT):
                    last = tr(ps[:, 3 + q, j * P:(j + 1) * P],
                              bblk[:, q, 4 * j:4 * j + 4, :].rearrange("p i c -> p (i c)"))
                last.then_inc(s5w_ps, 1)
            for q in range(2):
                for j in range(UT):
                    last = tr(ps[:, 5 + q, j * P:(j + 1) * P], cblk[:, q, j, :])
                last.then_inc(s5w_ps, 1)
            pe.wait_ge(s5w_ok, 2)
            pe.wait_ge(da_ok, 1)
            pe.wait_ge(conv_acc, XT)
            for j in range(XT):
                last = tr(ps[0:27, 2 + j // 4, (j % 4) * P:(j % 4 + 1) * P], tails[:, j, :])
            last.then_inc(tail_ps, 1)

            def s5_in(i):
                a_, r = i // 4, 32 * (i % 4)
                if i < 2:
                    pe.wait_ge(s5w_ok, 4)
                    pe.wait_ge(tail_cp, 1)
                    pe.wait_ge(tile_ev, UT)
                else:
                    pe.wait_ge(s5_xused, i - 1)
                for q in range(2):
                    last = mm(ps[:, 2 + 2 * (i % 2) + q, 0:T], bT[r:r + 32, q, a_, :], uT[r:r + 32, a_, :], True, True)
                last.then_inc(s5_x, 1)

            def s5_out(i):
                a_, r = i // 4, 32 * (i % 4)
                pe.wait_ge(s5_h, i + 1)
                if r == 0 and a_ >= 2:
                    pe.wait_ge(s5_yev, a_ - 1)
                for q in range(2):
                    last = mm(ps[r:r + 32, 6 + a_ % 2, 0:TP], cTs5[:, q, a_, r:r + 32], h5[:, 2 * (i % 2) + q, :], q == 0, q == 1)
                last.then_inc(s5_hused, 1)

            for t in range(T_Z, NT):
                for i in s5_steps(t - T_Z):
                    if i >= 2:
                        s5_out(i - 2)
                    s5_in(i)
                tile(t)
                if NT - 4 <= t < NT - 2:
                    s5_out(S5T - 2 + t - (NT - 4))
            pe.wait_ge(s5_hs, 1)
            for i in range(S5T):
                a_, r = i // 4, 32 * (i % 4)
                for q in range(2):
                    last = mm(ps[r:r + 32, 2, a_ * TS:(a_ + 1) * TS], cTs5[:, q, a_, r:r + 32], s5h[:, q, i, :], q == 0, q == 1)
            last.then_inc(s5_y, 1)
            for q in range(2):
                tr(ps[:, 3, q * P:(q + 1) * P], st5[:, q].rearrange("p b i -> p (b i)"))
                last = tr(ps[0:S5T, 3, 256 + q * P:256 + (q + 1) * P], fin5[:, q, :])
            last.then_inc(s5f_ps, 1)

            pe.wait_ge(gelu_ok, UT)
            wait_unit(U_GLU)
            wait_unit(U_GLU + 1)
            wa, wb = unit_tile(U_GLU, UT), unit_tile(U_GLU + 1, UT)
            pe.wait_ge(s5f_cp, 1)
            pe.wait_ge(s5_yev, 5)
            pe.wait_ge(tile_ev, NT)

            def glu(j):
                if j:
                    pe.wait_ge(glu_ev, j)
                for w, q in ((wa, 0), (wb, 1)):
                    for k in range(UT):
                        last = mm(ps[:, q, 0:T], w[:, k, j * P:(j + 1) * P], uT[:, k, :], k == 0, k == UT - 1)
                last.then_inc(glu_ps, 1)

            def cb_and_sums():
                for i, (t0, n) in enumerate(CHUNKS):
                    for gr in range(G):
                        o_ = (i % 2) * 256 + gr * n
                        last = mm(ps[0:n, 4 + i // 2, o_:o_ + n], xbcT[:, KD + gr, t0:t0 + n], xbcT[:, KD + G + gr, t0:t0 + n], True, True)
                last.then_inc(cb_ps, 1)
                for i, (t0, n) in enumerate(CHUNKS):
                    up, on = (upper, ones) if i < 2 else (supper_r, same_r)
                    mm(ps[0:n, 5, 128 + 32 * i:144 + 32 * i], up[0:n, 0:n], da3[0:n, i, :], True, True)
                    mm(ps[0:n, 5, 144 + 32 * i:160 + 32 * i], on[0:n, 0:n], da3[0:n, i, :], True, True)
                for hp in range(KD):
                    for q in range(2):
                        last = mm(ps[64 * q:64 * q + HD, 5, 256 + hp * TS:256 + (hp + 1) * TS],
                                  da3[0:TS, 2, 2 * hp + q:2 * hp + q + 1].to_broadcast([TS, HD]), supper_r[0:TS, :], True, True)
                last.then_inc(acs_ps, 1)

            def token_major(i):
                t0, n = CHUNKS[i]
                if i >= 1:
                    pe.wait_ge(xdt_ok, 2 * i)
                    pe.wait_ge(bt_ok, i)
                for j in range(KD):
                    last = tr(ps[0:n, 6 + j // 4, (j % 4) * P:(j % 4 + 1) * P], xbcT[:, j, t0:t0 + n])
                for gr in range(G):
                    last = tr(ps[0:n, 2, gr * P:(gr + 1) * P], xbcT[:, KD + gr, t0:t0 + n])
                last.then_inc(xt_ps, 1)

            def chunk_states(i):
                pe.wait_ge(bt_ok, 3)
                pe.wait_ge(xs_ok, i + 1)
                if i:
                    pe.wait_ge(h1_ok, G)
                for gr in range(G):
                    last = mm(ps[:, 2 + gr, :], B_tok[:, i, gr * NS:(gr + 1) * NS], Xs[:, i, gr * 512:(gr + 1) * 512], True, True)
                last.then_inc(st_ps, 1)

            def sample_sums():
                pe.wait_ge(cb_ok, 3)
                for h in range(H):
                    last = mm(ps[0:TS, 4, h * TS:(h + 1) * TS], da3[0:TS, 2, h:h + 1].to_broadcast([TS, TS]), supper_r[0:TS, :], True, True)
                last.then_inc(qs_ps, 1)

            pe.wait_ge(conv_ok, 2 * XT)
            for j, step in enumerate((cb_and_sums, lambda: token_major(0), lambda: token_major(1), lambda: token_major(2),
                                      lambda: chunk_states(0), lambda: chunk_states(1), sample_sums, None)):
                glu(j)
                if step is not None:
                    step()
            for _ in range(2):
                pe.wait_ge(glu_ps, KD)
                pe.nop().then_inc(unit_used, 1)

            def h0_turn(hp):
                pe.wait_ge(ld_h0[hp % NH0], 16 * (hp // NH0 + 1))
                if hp:
                    pe.wait_ge(h0_cp, 2 * hp)
                else:
                    pe.wait_ge(hf_ok, G)
                for b in range(NBATCH):
                    last = tr(ps[:, 2 + b // 4, (b % 4) * P:(b % 4 + 1) * P], h0[hp % NH0][:, b, :])
                    if b % 4 == 3:
                        last.then_inc(h0_ps, 1)

            def sample_states(hp):
                if hp:
                    pe.wait_ge(ss_ok, hp)
                else:
                    pe.wait_ge(qs_diff, 1)
                    pe.wait_ge(acs_ok, 3)
                    pe.wait_ge(bm_ok, 2)
                    pe.wait_ge(xs_ok, 3)
                gr = hp // (KD // G)
                for q in range(2):
                    last = mm(ps[:, 4 + q, :], Xs[0:TS, 2, hp * P:(hp + 1) * P], Bm[0:TS, gr, q * 512:(q + 1) * 512], True, True)
                last.then_inc(ss_ps, 1)

            def sample_off(hp):
                gr = hp // (KD // G)
                pe.wait_ge(h0_cp, 2 * hp + 2)
                if hp:
                    pe.wait_ge(yoff_ok, hp)
                    pe.wait_ge(mod_ok, 4 + hp)
                for b in range(NBATCH):
                    c, r = b % 4, b // 4
                    last = mm(ps[32 * c:32 * c + TS, 7, r * P:(r + 1) * P], xbcT[:, KD + G + gr, TP:T],
                              h0T[:, b * NS:(b + 1) * NS], True, True)
                last.then_inc(yo_ps, 1)

            def off_turn(hp):
                pe.wait_ge(yo_cp, hp + 1)
                for r in range(2):
                    last = tr(ps[:, 7, r * P:(r + 1) * P], yraw[:, r, :])
                last.then_inc(yoT_ps, 1)

            pe.wait_ge(glu_ev, KD)
            for qd in range(4):
                if qd:
                    pe.wait_ge(q_yev, 2 * qd)
                for i in range(2):
                    for h4 in range(4):
                        h = 4 * qd + h4
                        last = mm(ps[:, i, h4 * CH:(h4 + 1) * CH], da3[:, i, h:h + 1].to_broadcast([P, P]), upper[:, :], True, True)
                last.then_inc(q_ps, 1)
                h0_turn(2 * qd)
                ada(4 + 2 * qd)
                sample_off(2 * qd)
                sample_states(2 * qd)
                h0_turn(2 * qd + 1)
                off_turn(2 * qd)
                ada_turn(4 + 2 * qd)
                sample_off(2 * qd + 1)
                ada(5 + 2 * qd)
                sample_states(2 * qd + 1)
                off_turn(2 * qd + 1)
                pe.wait_ge(q_mt, 2 * (qd + 1))
                if qd == 0:
                    pe.wait_ge(qs_ok, 2)
                for h4 in range(4):
                    h = 4 * qd + h4
                    gr, j = h // (H // G), h // 2
                    out = ps[64 * (h % 2):64 * (h % 2) + HD, j % 2, :]
                    xh = slice(h * HD, (h + 1) * HD)
                    mm(out[:, 0:CH], Xdt[:, 0, xh], MT[:, h4, 0:CH], True, True)
                    mm(out[:, CH:TP], Xdt[:, 1, xh], MT[:, h4, CH:TP], True, False)
                    mm(out[:, CH:TP], h1T[:, gr, (h % 8) * HD:(h % 8 + 1) * HD], CTs[:, h4, :], False, True)
                    last = mm(out[:, TP:T], Xdt[0:TS, 2, xh], MTs[0:TS, h, :], True, True)
                    if h4 % 2 == 1:
                        last.then_inc(q_y, 1)
                ada_turn(5 + 2 * qd)
            pe.wait_ge(h0_cp, 2 * KD)
            for j in range(KD):
                last = tr(ps[:, 2 + j // 4, (j % 4) * P:(j % 4 + 1) * P], hfT[:, j // 4, (j % 4) * P:(j % 4 + 1) * P])
            last.then_inc(hf_ps, 1)
            pe.wait_ge(ss_ok, KD)
            for gr in range(G):
                square_sums(4 + gr, 4, 8 + 4 * gr)
            pe.wait_ge(hf_cp, 1)

            def project(unit0, bank, src, banks_ps, freed, src_ok, after=None):
                for j in range(KD):
                    n = unit0 + j // 4
                    wait_unit(n)
                    w = unit_tile(n, KD)
                    if j >= 2:
                        pe.wait_ge(freed, j - 1)
                    for k in range(KD):
                        if j == 0:
                            pe.wait_ge(src_ok, k + 1)
                        last = mm(ps[:, bank + j % 2, 0:T], w[:, k, (j % 4) * P:(j % 4 + 1) * P], src[:, k, :], k == 0, k == KD - 1)
                    last.then_inc(banks_ps, 1)
                    if j % 4 == 3:
                        pe.wait_ge(banks_ps, j + 1)
                        pe.nop().then_inc(unit_used, 1)
                    if after is not None:
                        after(j)

            def residual_square(j):
                if j >= 2:
                    square_sum(4, 16 + j - 2, j == 2, False)

            project(U_OUTA, 0, zT, outa_ps, mrg_ok, yn_ok)
            pe.wait_ge(hf_cp, 1)
            project(U_OUT, 2, gates, mix_ps, x1_ok, mrg_ok, residual_square)
            square_sum(4, 22, False, False)
            square_sum(4, 23, False, True)
            pe.wait_ge(h_ok, 2)
            pe.wait_ge(ld_wrt, 16)
            for k in range(KD):
                pe.wait_ge(hp_ok, KD + k + 1)
                for i, (t0, n) in enumerate(CHUNKS):
                    last = mm(ps[0:n, 6, i * NE:(i + 1) * NE], hT[:, k, t0:t0 + n], w_rt[:, k, :], k == i == 0, k == KD - 1)
                if k == KD - 1:
                    last.then_inc(lg_ps, 1)
            for q in range(2):
                for i, (t0, n) in enumerate(CHUNKS):
                    for j in range(4 * q, 4 * q + 4):
                        last = tr(ps[0:n, 3 * q + i, (j % 4) * P:(j % 4 + 1) * P], hT[:, j, t0:t0 + n])
                    last.then_inc(h2t_ps, 1)
            pe.wait_ge(top_ok, 1)
            for i, (t0, n) in enumerate(CHUNKS):
                for i2 in range(i + 1):
                    m = CHUNKS[i2][1]
                    mm(ps[0:n, 7, i * NE:(i + 1) * NE], (strict if i2 == i else ones)[0:m, 0:n], s_all[0:m, i2, :], i2 == 0, i2 == i)
            for i, (t0, n) in enumerate(CHUNKS):
                last = mm(ps[:, 7, 48:64], ones[0:n, :], s_all[0:n, i, :], i == 0, i == 2)
            last.then_inc(pos_ps, 1)

            def ring_wait(v, r):
                s = MOE_SLOTS[r]
                pe.wait_ge(landed[s], (v + uses(s) + 1) * 16 if s < NR else (v + 1) * 16)

            def gather(v, half):
                if half == 0:
                    pe.wait_ge(selo_ok, v + 1)
                for j in range(4 * half, 4 * half + 4):
                    for i, (t0, n) in enumerate(CHUNKS):
                        last = mm(ps[:, half, (j % 4) * P:(j % 4 + 1) * P], h2_tok[0:n, i, j * P:(j + 1) * P], selo2[0:n, i, :], i == 0, i == 2)
                last.then_inc(xg_ps[half], 1)

            def combine(v):
                pe.wait_ge(ye_ok, 2 * v + 2)
                pe.wait_ge(pT_ok, v + 1)
                for j in range(KD):
                    if j >= 2:
                        pe.wait_ge(cmb_ok, 8 * v + 8 + j - 1)
                    mm(ps[:, (7, 4)[j % 2], 0:T], y_e[:, j * P:(j + 1) * P], pT[:, :], True, True).then_inc(cmb_ps, 1)

            def up(v, wi):
                ring_wait(v, 2 * wi)
                ring_wait(v, 2 * wi + 1)
                for k in range(KD):
                    for e in range(2):
                        w = ring_tile(MOE_SLOTS[2 * wi + e], KD)
                        last = mm(ps[64 * e:64 * e + 64, 2 + wi, :], Xe[:, k, 64 * e:64 * e + 64], w[:, k, :], k == 0, k == KD - 1)
                        if k == KD - 1:
                            last.then_inc(unit_used, 1)

            def experts(v, prev, following):
                pe.wait_ge(xe_ok, 2 * v + 2)
                up(v, 0)
                if prev:
                    combine(v - 1)
                up(v, 1)
                if following:
                    gather(v + 1, 0)
                pe.wait_ge(selw_ok, v + 1)
                if prev:
                    pe.wait_ge(cmb_ok, 8 * v + 8)
                for i, (t0, n) in enumerate(CHUNKS):
                    last = tr(ps[:, 7, t0:t0 + n], selw2[0:n, i, :])
                last.then_inc(pT_ps, 1)
                pe.wait_ge(act_ok, v + 1)
                for f in range(FT):
                    last = tr(ps[:, 4, f * P:(f + 1) * P], act_e[:, f * P:(f + 1) * P])
                last.then_inc(aT_ps, 1)
                if following:
                    gather(v + 1, 1)
                pe.wait_ge(aT_ok, v + 1)
                ring_wait(v, 4)
                ring_wait(v, 5)
                for nh in range(2):
                    for f in range(FT):
                        for e in range(2):
                            w = ring_tile(MOE_SLOTS[4 + e], FT)
                            last = mm(ps[64 * e:64 * e + 64, 5 + nh, :], actT[:, f, 64 * e:64 * e + 64], w[:, f, nh * 512:(nh + 1) * 512], f == 0, f == FT - 1)
                            if nh == 1 and f == FT - 1:
                                last.then_inc(unit_used, 1)
                    if nh == 0:
                        last.then_inc(w2_ps, 1)

            pe.wait_ge(h2t_ok, 6)
            gather(0, 0)
            gather(0, 1)
            experts(0, False, True)
            with pe.Fori(1, PAIRS - 1) as q:
                experts(q, True, True)
            experts(PAIRS - 1, True, False)
            combine(PAIRS - 1)
            pe.wait_ge(route_ok, 1)
            passes = pe.value_load(npi[0:1, 0:1], min_val=1, max_val=MAXPASS)
            with pe.If(passes > 1):
                with pe.Fori(1, passes) as n:
                    v0 = n * PAIRS
                    gather(v0, 0)
                    gather(v0, 1)
                    experts(v0, False, True)
                    with pe.Fori(1, PAIRS - 1) as q:
                        experts(n * PAIRS + q, True, True)
                    experts(v0 + (PAIRS - 1), True, False)
                    combine(v0 + (PAIRS - 1))

            for j in range(KD):
                pe.wait_ge(fin_ok, j + 1)
                for i, (t0, n) in enumerate(CHUNKS):
                    last = tr(ps[0:n, 2 * i + j // 4, (j % 4) * P:(j % 4 + 1) * P], hT[:, j, t0:t0 + n])
                if j % 4 == 3:
                    last.then_inc(fin_ps, 1)
                pe.wait_ge(sq_ok, 24 + j + 1)
                for i, (t0, n) in enumerate(CHUNKS):
                    last = mm(ps[0:n, 6, 2 * i:2 * i + 1], sq[:, j % 2, t0:t0 + n], ones[:, 0:1], j == i == 0, j == KD - 1)
                last.then_inc(sq_used, 1)

        @block.scalar
        def _(act):
            link = linker(act, act_chain)

            def f(out, in_, func=ACT.Copy, **kw):
                return nc.scalar.activation(out, in_, func, **kw)

            def load(out, in_, s):
                act.dma_start(out, in_).then_inc(s, 16)

            load(c_in[0:1, :], a["c_prompt"], ld_c)
            load(c_in[1:NC, :], a["c_sample"], ld_c)
            load(x_tok[:, 0:2, :], a["x_prompt"][0].rearrange("(i p) d -> p i d", p=P), ld_x)
            load(x_tok[0:TS, 2, :], a["x_sample"].rearrange("b l d -> (b l) d"), ld_x)
            with nc.allow_non_contiguous_dma(reason="a value or a short run per descriptor, a few KiB in all"):
                load(exp_in[96:104, 0:2], a["d_ssd"][0].rearrange("(j q) -> j q", q=2), ld_exp)
                load(exp_in[0:S5T, 2:4], a["s5_log_dt"][0].rearrange("(j q) -> j q", q=2), ld_exp)
            r0 = 0
            for name, n in (("norm1_w", 8), ("norm2_w", 8), ("ssd_norm_w", 8), ("conv_w", 48), ("conv_b", 12), ("s5_d", 4)):
                v = a[name][0]
                v = v.rearrange("k (j p) -> (k j) p", p=P) if name == "conv_w" else v.rearrange("(j p) -> j p", p=P)
                load(prow1[r0:r0 + n, :], v, ld_par)
                r0 += n
            load(prow1[r0:r0 + 8, :], a["final_norm_w"].rearrange("(j p) -> j p", p=P), ld_par)
            load(prow2[0:48, :], a["b_ada"][0].rearrange("(j p) -> j p", p=P), ld_par)
            load(prow2[48:64, :], a["s5_a_re"][0].rearrange("(i q) s -> i (q s)", q=2), ld_par)
            load(prow2[64:80, :], a["s5_a_im"][0].rearrange("(i q) s -> i (q s)", q=2), ld_par)
            act.wait_ge(ld_c, 32)
            f(c_in[0:NC, :], c_in[0:NC, :], ACT.Silu).then_inc(c_silu, 1)

            n_sq = [0]

            def square(src):
                q = n_sq[0]
                if q >= 2:
                    act.wait_ge(sq_used, q - 1)
                f(sq[:, q % 2, :], src, ACT.Square).then_inc(sq_ok, 1)
                n_sq[0] += 1

            for j in range(KD):
                act.wait_ge(x_ps, j + 1)
                f(xT[:, j, :], ps[:, j % 2, 0:T]).then_inc(x_ok, 1)
                act.wait_ge(x_ok, j + 1)
                square(xT[:, j, :])

            for q, name in enumerate(("state_s5_re", "state_s5_im")):
                load(st_rows[:, q, :], a[name][0].rearrange("b (i q) s -> (b i) (q s)", q=2), ld_state5)
            load(conv_in[0:24, :], a["state_conv"][0].rearrange("b k f -> (b k) f"), ld_conv)
            for name, t_ in (("dt_bias", dtb), ("a_log", alog)):
                load(t_[:, :], a[name].to_broadcast([P, H]), ld_bc)
            load(brt[:, :], a["b_router"].unsqueeze(0).to_broadcast([P, NE]), ld_bc)
            for q, name in enumerate(("s5_b_re", "s5_b_im")):
                for gg in range(2):
                    load(b_raw[64 * gg:64 * gg + 64, q, :, :],
                         a[name][0].rearrange("(i q) s c -> q s i c", q=2)[gg], ld_rows)
            for q, name in enumerate(("s5_c_re", "s5_c_im")):
                load(c_raw[:, q, :, :], a[name][0].rearrange("(j g) c s -> (g c) j s", j=UT), ld_rows)
            load(w_dt[:, :, :], a["w_in"][0, :, IN_DT:IN_DT + H].rearrange("(k p) n -> p k n", p=P), ld_wdt)
            load(w_rt[:, :, :], a["w_router"].rearrange("(k p) n -> p k n", p=P), ld_wrt)

            n_rs = [0]

            def rsqrt(v, y):
                n_rs[0] += 1
                act.wait_ge(var_ok, n_rs[0])
                link(f(y, v, ACT.Ln))
                f(y, y, ACT.Exp, scale=-0.5).then_inc(rs_ok, 1)

            rsqrt(n1v, n1y)

            n_mod = [0]

            def modulate(sh):
                n_mod[0] += 1
                act.wait_ge(amul_ok, n_mod[0])
                for j in range(KD):
                    act.wait_ge(xn_ok, (n_mod[0] - 1) * KD + j + 1)
                    f(hT[:, j, 0:TP], hT[:, j, 0:TP], ACT.Identity, scale=amul[:, j, 0:1], bias=mod[:, sh + j, 0:1]).then_inc(hp_ok, 1)

            modulate(0)
            act.wait_ge(par_ok, 1)
            f(s5c[:, 5, :], pc3[:, :], ACT.Exp).then_inc(trig, 1)
            act.wait_ge(dsc, 1)
            f(s5c[:, 6, :], s5c[:, 6, :], ACT.Exp).then_inc(trig, 1)
            f(s5c[:, 11, :], s5c[:, 8, :], ACT.Sin).then_inc(trig, 1)
            f(s5c[:, 10, :], s5c[:, 9, :], ACT.Sin).then_inc(trig, 1)

            def conv_silu(j):
                act.wait_ge(conv_acc, j + 1)
                acc = part(z_r, (j % 2) * 312, 312)
                f(xbcT[:, j, 0:TP], acc[:, 0:TP], ACT.Silu).then_inc(conv_ok, 1)
                f(sample(xbcT[:, j, TP:T]), rows_sample(acc)[:, :, 0:LSAMP], ACT.Silu).then_inc(conv_ok, 1)

            def rows_sample(v):
                n = v.shape[-1] - 259
                if n == 56:
                    return v[:, 259:315].rearrange("p (b l) -> p b l", l=7)
                return bass.AP(v.tensor, v.offset + 259, [list(v.ap[0]), [7, NBATCH], [1, LSAMP]])

            for t, (kind, j) in enumerate(tiles[:T_Z]):
                if kind == "x" and j >= 2:
                    conv_silu(j - 2)
                act.wait_ge(tile_ps, t + 1)
                if kind == "u":
                    f(uT[:, j, :], ps[:, t % 2, 0:T]).then_inc(tile_ev, 1)
                else:
                    if j == 0:
                        act.wait_ge(sq_used, KD)
                    row = rows[:, j % 2, :]
                    link(f(row[:, 3:3 + TP], ps[:, t % 2, 0:TP]))
                    f(rows_sample(row)[:, :, 3:7], sample(ps[:, t % 2, TP:T])).then_inc(tile_ev, 1)
            conv_silu(XT - 2)
            conv_silu(XT - 1)
            act.wait_ge(ld_bc, 48)
            link(f(alog[:, :], alog[:, :], ACT.Exp))
            act.wait_ge(dt_pre, 1)
            link(f(dtt[:, :, :], dt3[:, :, :], ACT.Abs))
            link(f(dtt[:, :, :], dtt[:, :, :], ACT.Exp, scale=-1.0))
            f(dtt[:, :, :], dtt[:, :, :], ACT.Ln, bias=1.0).then_inc(dt_exp, 1)
            act.wait_ge(tail_ps, 1)
            ctail = part(gate_r, 8 * T, XBC)
            f(ctail[0:27, :].rearrange("p (a b) -> p a b", b=512), ps[0:27, 2:5, :]).then_inc(tail_cp, 1)
            act.wait_ge(tail_cp, 1)
            act.dma_start(o["conv_prompt"][0, 0], ctail[0:3, :]).then_inc(st_conv, 16)
            act.dma_start(o["conv_sample"][0].rearrange("b k f -> (b k) f"), ctail[3:27, :]).then_inc(st_conv, 16)

            for t, (kind, j) in enumerate(tiles):
                if t < T_Z:
                    continue
                act.wait_ge(tile_ps, t + 1)
                if kind == "z":
                    f(zT[:, j, :], ps[:, t % 2, 0:T], ACT.Silu).then_inc(tile_ev, 1)
                else:
                    if j == KD:
                        act.wait_ge(st_conv, 32)
                    f(gates[:, j, :], ps[:, t % 2, 0:T], ACT.Sigmoid).then_inc(tile_ev, 1)

            act.wait_ge(s5_yev, 5)
            for j in range(UT):
                f(uT[:, j, :], uT[:, j, :], ACT.Gelu_apprx_tanh).then_inc(gelu_ok, 1)
            act.wait_ge(s5f_ps, 1)
            link(f(ada_s[:, 0:256], ps[:, 3, 0:256]))
            f(ada_s[0:S5T, 256:512], ps[0:S5T, 3, 256:512]).then_inc(s5f_cp, 1)
            act.wait_ge(s5f_cp, 1)
            for q, (ns, npr) in enumerate((("s5_re_sample", "s5_re_prompt"), ("s5_im_sample", "s5_im_prompt"))):
                act.dma_start(o[ns][0].rearrange("b (i q) s -> (b i) (q s)", q=2), ada_s[:, q * P:(q + 1) * P]).then_inc(st_s5, 16)
                act.dma_start(o[npr][0, 0].rearrange("(i q) s -> i (q s)", q=2),
                              ada_s[0:S5T, 256 + q * P:256 + (q + 1) * P]).then_inc(st_s5, 16)
            h0_src = a["state_ssm"][0].rearrange("b (j q) p n -> j (q p) b n", q=2)
            h0_dst = o["ssm_sample"][0].rearrange("b (j q) p n -> j (q p) b n", q=2)

            for hp in range(NH0):
                act.dma_start(h0[hp], h0_src[hp]).then_inc(ld_h0[hp], 16)

            def glu_gate(j):
                act.wait_ge(glu_ps, j + 1)
                if j >= 2:
                    act.wait_ge(glu_ev, j - 1)
                f(sq[:, j % 2, :], ps[:, 1, 0:T], ACT.Sigmoid).then_inc(glu_sig, 1)

            glu_gate(0)
            glu_gate(1)
            act.wait_ge(acs_ok, 2)
            f(eft[:, :, :].rearrange("p j t -> p (j t)"), ps[:, 5, 256:512], ACT.Exp).then_inc(acs_ok, 1)
            act.wait_ge(dte_pre, 1)
            link(f(dte[:, 0:2, :], dte[:, 0:2, :], ACT.Exp))
            link(f(dte[0:TS, 2, :], dte[0:TS, 2, :], ACT.Exp))
            f(acs[:, 1, H:2 * H], acs[:, 1, H:2 * H], ACT.Exp).then_inc(dte_ok, 1)
            for i, (t0, n) in enumerate(CHUNKS):
                act.wait_ge(xt_ps, i + 1)
                f(B_tok[0:n, i, :], ps[0:n, 2, 0:2 * NS]).then_inc(bt_ok, 1)
                glu_gate(2 + i)
            act.wait_ge(st_ps, 1)
            for gr in range(G):
                f(h1T[:, gr, :], ps[:, 2 + gr, :]).then_inc(h1_ok, 1)
            for j in range(5, KD):
                glu_gate(j)

            def h0_copies(hp):
                for q in range(2):
                    act.wait_ge(h0_ps, 2 * hp + q + 1)
                    if hp:
                        act.wait_ge(yo_ps, hp)
                    f(h0T[:, q * 512:(q + 1) * 512], ps[:, 2 + q, :]).then_inc(h0_cp, 1)
                act.wait_ge(yo_ps, hp + 1)
                f(yraw[:, :, :], ps[:, 7, 0:2 * P].rearrange("p (r f) -> p r f", r=2)).then_inc(yo_cp, 1)
                if hp >= 1:
                    store_states(hp - 1)
                if 2 <= hp < KD - 2:
                    b = (hp + 2) % NH0
                    act.wait_ge(st_hs[b], 16 * ((hp + 2) // NH0))
                    act.dma_start(h0[b], h0_src[hp + 2]).then_inc(ld_h0[b], 16)

            def store_states(hp):
                act.wait_ge(ss_ok, hp + 1)
                act.dma_start(h0_dst[hp], h0[hp % NH0]).then_inc(st_hs[hp % NH0], 16)

            act.wait_ge(qs_msk, 1)
            f(MTs[0:TS], MTs[0:TS], ACT.Exp).then_inc(qs_exp, 1)
            for qd in range(4):
                act.wait_ge(q_diff, qd + 1)
                if qd:
                    act.wait_ge(q_y, 2 * qd)
                f(CTs[:, :, :].rearrange("p h q -> p (h q)"), ps[:, 1, :], ACT.Exp).then_inc(q_exp, 1)
                act.wait_ge(q_msk, qd + 1)
                f(MT, MT, ACT.Exp).then_inc(q_exp, 1)
                h0_copies(2 * qd)
                h0_copies(2 * qd + 1)
            store_states(KD - 1)
            act.wait_ge(hf_ps, 1)
            f(h_out[:, :, :].rearrange("p (a j) n -> p a (j n)", a=2), ps[:, 2:4, :]).then_inc(hf_cp, 1)
            act.wait_ge(hf_cp, 1)
            act.dma_start(o["ssm_prompt"][0, 0].rearrange("(j q) p n -> (q p) j n", q=2), h_out).then_inc(st_hp, 16)
            for gr in range(G):
                for j in range(4 * gr, 4 * gr + 4):
                    act.wait_ge(q_yev, j + 1)
                    square(zT[:, j, :])
                if gr:
                    rsqrt(nv, ny)
                    rsqrt(nv, ny)
            for j in range(KD):
                act.wait_ge(x1_ok, j + 1)
                square(xT[:, j, :])
            rsqrt(nv, ny)
            modulate(24)
            for q in range(2):
                for i, (t0, n) in enumerate(CHUNKS):
                    act.wait_ge(h2t_ps, 3 * q + i + 1)
                    f(h2_tok[0:n, i, q * 512:(q + 1) * 512], ps[0:n, 3 * q + i, :]).then_inc(h2t_ok, 1)
            act.wait_ge(sm_in, 1)
            f(score, score, ACT.Exp).then_inc(sm_exp, 1)

            def tokens_in(v, half):
                act.wait_ge(xg_ps[half], v + 1)
                f(Xe[:, 4 * half:4 * half + 4, :].rearrange("p j s -> p (j s)"), ps[:, half, :]).then_inc(xe_ok, 1)

            def experts(v, prev, following):
                act.wait_ge(unit_used, N_UNITS + 6 * v + 2)
                if prev:
                    act.wait_ge(act_ok, v)
                f(hs_[:, :], ps[:, 2, :], ACT.Silu).then_inc(act_s, 1)
                if following:
                    tokens_in(v + 1, 0)
                act.wait_ge(aT_ps, v + 1)
                f(actT[:, :, :].rearrange("p f s -> p (f s)"), ps[:, 4, :]).then_inc(aT_ok, 1)
                if following:
                    tokens_in(v + 1, 1)
                act.wait_ge(w2_ps, v + 1)
                f(y_e[:, 0:512], ps[:, 5, :]).then_inc(ye_ok, 1)
                act.wait_ge(unit_used, N_UNITS + 6 * v + 6)
                f(y_e[:, 512:D], ps[:, 6, :]).then_inc(ye_ok, 1)

            tokens_in(0, 0)
            tokens_in(0, 1)
            experts(0, False, True)
            with act.Fori(1, PAIRS - 1) as q:
                experts(q, True, True)
            experts(PAIRS - 1, True, False)
            act.wait_ge(route_ok, 1)
            passes = act.value_load(npi[0:1, 0:1], min_val=1, max_val=MAXPASS)
            with act.If(passes > 1):
                with act.Fori(1, passes) as n:
                    v0 = n * PAIRS
                    tokens_in(v0, 0)
                    tokens_in(v0, 1)
                    experts(v0, True, True)
                    with act.Fori(1, PAIRS - 1) as q:
                        experts(n * PAIRS + q, True, True)
                    experts(v0 + (PAIRS - 1), True, False)
            for j in range(KD):
                act.wait_ge(x2_ok, j + 1)
                f(hT[:, j, :], xT[:, j, :], ACT.Copy, scale=fnw[:, j:j + 1]).then_inc(fin_ok, 1)
                square(xT[:, j, :])
            rsqrt(tok_v, tok_rs)
            act.wait_ge(fin_rs, 1)
            act.wait_ge(fin_ps, 2)
            for i, (t0, n) in enumerate(CHUNKS):
                f(y_tok[0:n, i, 0:512], ps[0:n, 2 * i, :], ACT.Copy, scale=tok_rs[0:n, i:i + 1]).then_inc(fin_cp, 1)

        @block.vector
        def _(dve):
            link = linker(dve, dve_chain)
            v = nc.vector

            def tt(out, x, y, op):
                return v.tensor_tensor(out, x, y, op)

            def ts(out, x, s1, s2, op0, op1=None):
                return v.tensor_scalar(out, x, s1, s2, op0, op1) if op1 is not None else v.tensor_scalar(out, x, s1, s2, op0)

            def stt(out, x, s, y, op0, op1):
                return v.scalar_tensor_tensor(out=out, in0=x, scalar=s, in1=y, op0=op0, op1=op1)

            v.memset(ones[:], 1.0).then_inc(vconsts, 1)
            link(v.memset(cT, 0.0))
            link(v.memset(bblk, 0.0))
            dve.wait_ge(consts, 9)
            for c in range(4):
                last = v.tensor_copy(sel9[32 * c:32 * c + 32, :], ident[32 * c:32 * c + 32, 32 * c:32 * c + 32])
            last.then_inc(vconsts, 1)
            v.tensor_reduce(par2[:], par8[:].rearrange("p (q h) -> p q h", q=2), AX_X, ALU.add).then_inc(vconsts, 1)
            dve.wait_ge(vconsts, 3)
            dve.wait_ge(cT_ps, 1)
            v.tensor_copy(cT[:, :, 0:NC], ps[:, 6, 0:KD * NC].rearrange("p (k c) -> p k c", c=NC)).then_inc(cT_ok, 1)
            dve.wait_ge(ld_exp, 32)
            v.tensor_copy(prow1[96:104, :].rearrange("p (q s) -> p q s", q=2),
                          exp_in[96:104, 0:2].unsqueeze(2).to_broadcast([8, 2, 64])).then_inc(expd, 1)
            v.tensor_copy(prow3[0:S5T, :].rearrange("p (q s) -> p q s", q=2),
                          exp_in[0:S5T, 2:4].unsqueeze(2).to_broadcast([S5T, 2, 64])).then_inc(expd, 1)
            dve.wait_ge(par_ps, 1)
            link(v.tensor_copy(pc1[:, :], ps[:, 7, 0:104]))
            link(v.tensor_copy(pc2[:, :], ps[:, 7, 128:208]))
            v.tensor_copy(pc3[:, :], ps[:, 7, 256:272]).then_inc(par_ok, 1)
            def norm_scale(bank, count, width, vv, y, t, n):
                dve.wait_ge(sq_used, count)
                ts(vv, ps[:, bank, 0:T], 1.0 / width, EPS, ALU.mult, ALU.add).then_inc(var_ok, 1)
                dve.wait_ge(rs_ok, n)
                link(tt(t, vv, y, ALU.mult))
                link(tt(t, t, y, ALU.mult))
                link(ts(t, t, -0.5, 1.5, ALU.mult, ALU.add))
                link(tt(y, y, t, ALU.mult))

            def ada_copy(i):
                dve.wait_ge(unit_used, ada_unit(i) + 1)
                if i >= 1:
                    dve.wait_ge(adaT_ps, i)
                if i == 4:
                    dve.wait_ge(st_s5, 64)
                v.tensor_copy(ada_s[:, :], ps[:, sums_bank(i), :]).then_inc(ada_cp, 1)

            def ada_add(i):
                dve.wait_ge(adaT_ps, i + 1)
                tt(mod[:, 4 * i:4 * i + 4, :], turned(i, 0, 4).rearrange("p (k c) -> p k c", c=NC),
                   b_ada[:, 4 * i:4 * i + 4].unsqueeze(2).to_broadcast([P, 4, NC]), ALU.add).then_inc(mod_ok, 1)

            def ada(i):
                ada_copy(i)
                ada_add(i)

            def per_sequence(col):
                return col.unsqueeze(2).to_broadcast([P, NBATCH, LSAMP])

            def normalize(y):
                for j in range(KD):
                    tt(hT[:, j, :], xT[:, j, :], y, ALU.mult).then_inc(xn_ok, 1)

            def scales(nw, sc):
                stt(amul, mod[:, sc:sc + KD, :], 1.0, nw.unsqueeze(2).to_broadcast([P, KD, NC]), ALU.add, ALU.mult).then_inc(amul_ok, 1)

            def modulate(sh, n):
                dve.wait_ge(amul_ok, n)
                dve.wait_ge(xn_ok, n * KD)
                hs = hT[:, :, TP:T].rearrange("p j (b l) -> p j b l", l=LSAMP)
                m4 = [P, KD, NBATCH, LSAMP]
                tt(hs, hs, amul[:, :, 1:NC].unsqueeze(3).to_broadcast(m4), ALU.mult).then_inc(hm_ok, 1)
                dve.wait_ge(hm_ok, n)
                tt(hs, hs, mod[:, sh:sh + KD, 1:NC].unsqueeze(3).to_broadcast(m4), ALU.add).then_inc(h_ok, 1)

            norm_scale(4, KD, D, n1v, n1y, n1t, 1)
            ada(0)
            normalize(n1y)
            for i in range(1, 4):
                ada(i)
            dve.wait_ge(mod_ok, 4)
            scales(nw1, 8)
            modulate(0, 1)

            C = [s5c[:, k, :] for k in range(24)]
            dt_, mag, th, r, r2, co, si, abr, abi, den, fre, fim = C[5], C[6], C[7], C[8], C[9], C[10], C[11], C[12], C[13], C[14], C[15], C[16]
            t0_, t1_, am1 = C[17], C[18], C[21]
            dve.wait_ge(trig, 1)
            link(tt(mag, dt_, a_re, ALU.mult))
            link(tt(th, dt_, a_im, ALU.mult))
            link(ts(t0_, th, 1.0 / TWO_PI, ROUND, ALU.mult, ALU.add))
            link(ts(t0_, t0_, -ROUND, None, ALU.add))
            link(stt(r, t0_, -TWO_PI_HI, th, ALU.mult, ALU.add))
            link(stt(r, t0_, -(TWO_PI - TWO_PI_HI), r, ALU.mult, ALU.add))
            link(ts(r, r, PI_IN, -PI_IN, ALU.min, ALU.max))
            link(ts(t1_, r, TWO_PI / 4, -TWO_PI, ALU.is_gt, ALU.mult))
            link(stt(r2, r, TWO_PI / 4, t1_, ALU.add, ALU.add))
            ts(r2, r2, PI_IN, -PI_IN, ALU.min, ALU.max).then_inc(dsc, 1)
            dve.wait_ge(trig, 4)
            link(v.tensor_copy(C[0], co))
            v.tensor_copy(C[1], si).then_inc(rot_u, 1)
            link(tt(abr, mag, co, ALU.mult))
            link(tt(abi, mag, si, ALU.mult))
            link(ts(am1, abr, -1.0, None, ALU.add))
            link(tt(den, a_re, a_re, ALU.mult))
            link(tt(t0_, a_im, a_im, ALU.mult))
            link(tt(den, den, t0_, ALU.add))
            link(v.reciprocal(den, den))
            link(tt(fre, am1, a_re, ALU.mult))
            link(tt(t0_, abi, a_im, ALU.mult))
            link(tt(fre, fre, t0_, ALU.add))
            link(tt(fre, fre, den, ALU.mult))
            link(tt(fim, abi, a_re, ALU.mult))
            link(tt(t0_, am1, a_im, ALU.mult))
            link(tt(fim, fim, t0_, ALU.subtract))
            link(tt(fim, fim, den, ALU.mult))
            dve.wait_ge(cT_ps, 2)
            link(v.tensor_copy(csT.rearrange("p j k -> p (j k)"), ps[:, 3, 0:XT * 24]))
            dve.wait_ge(x_ps, KD)
            v.tensor_copy(st5_flat, ps[:, 2, 0:256]).then_inc(par_ok, 1)

            dve.wait_ge(ld_rows, 16 * 6)
            b3 = [P // 2, S5T, S5C]
            btmp = part(gate_r, 4228, S5T, S5C)
            for gg in range(2):
                rr = slice(64 * gg, 64 * gg + 64)
                cc = slice(S5C * gg, S5C * gg + S5C)
                fr, fi = fre[rr].unsqueeze(2).to_broadcast(b3), fim[rr].unsqueeze(2).to_broadcast(b3)
                for q, (x, y, op) in enumerate(((0, 1, ALU.subtract), (1, 0, ALU.add))):
                    link(tt(btmp[rr], b_raw[rr, y], fi, ALU.mult))
                    link(tt(bblk[rr, q, :, cc], b_raw[rr, x], fr, ALU.mult))
                    link(tt(bblk[rr, q, :, cc], bblk[rr, q, :, cc], btmp[rr], op))
            dve.wait_ge(cT_ps, 1)
            for q, sign in enumerate((1.0, -1.0)):
                for hh in range(2):
                    link(ts(cblk[:, q, :, 64 * hh:64 * hh + 64], c_raw[:, q], par2[:, hh:hh + 1], sign, ALU.mult, ALU.mult))
            v.memset(npf[:, 0:1], 0.0).then_inc(blk5, 2)


            dve.wait_ge(sq_used, KD)
            link(v.memset(rows[:, :, 0:3], 0.0))
            for j in range(XT):
                row = rows[:, j % 2, :]
                acc = part(z_r, (j % 2) * 312, 312)
                srow = row[:, 259:315].rearrange("p (b l) -> p b l", l=7)
                link(v.tensor_copy(srow[:, :, 0:3], csT[:, j, :].rearrange("p (b k) -> p b k", k=3)))
                dve.wait_ge(tile_ev, T_XBC + j + 1)
                if j >= 2:
                    dve.wait_ge(conv_ok, 2 * (j - 1))
                elif j == 0:
                    dve.wait_ge(xn_ok, KD)
                link(ts(acc, row[:, 0:312], convw[:, 0, j:j + 1], convb[:, j:j + 1], ALU.mult, ALU.add))
                for k in range(1, CONV):
                    link(stt(acc, row[:, k:k + 312], convw[:, k, j:j + 1], acc, ALU.mult, ALU.add))
                link(v.tensor_copy(tails[:, j, 0:3], row[:, TP:TP + 3]))
                v.tensor_copy(tails[:, j, 3:27].rearrange("p (b k) -> p b k", k=3), srow[:, :, 4:7]).then_inc(conv_acc, 1)

            link(v.memset(dt3, 0.0))
            dve.wait_ge(dt_ps, 1)
            dve.wait_ge(ld_bc, 48)
            link(tt(dt3[:, 0:2, :], ps[:, 2, 0:2 * H].rearrange("p (i h) -> p i h", h=H),
                    dtb[:, :].unsqueeze(1).to_broadcast([P, 2, H]), ALU.add))
            tt(dt3[0:TS, 2, :], ps[0:TS, 2, 2 * H:3 * H], dtb[0:TS, :], ALU.add).then_inc(dt_pre, 1)
            dve.wait_ge(dt_exp, 1)
            link(stt(dt3, dt3, 0.0, dtt, ALU.max, ALU.add))
            stt(da3, dt3, -1.0, alog[:, :].unsqueeze(1).to_broadcast([P, 3, H]), ALU.mult, ALU.mult).then_inc(da_ok, 1)
            for q in range(4):
                dve.wait_ge(s5w_ps, q + 1)
                dst = (bT if q < 2 else cTs5)[:, q % 2]
                v.tensor_copy(dst.rearrange("p j m -> p (j m)"), ps[:, 3 + q, :]).then_inc(s5w_ok, 1)

            dve.wait_ge(rot_ok, 1)
            dve.wait_ge(conv_acc, XT)

            def s5_y_out(j):
                dve.wait_ge(s5_hused, 4 * j + 4)
                stt(uT[:, j, 0:TP], uT[:, j, 0:TP], s5d[:, j:j + 1], ps[:, 6 + j % 2, 0:TP], ALU.mult, ALU.add).then_inc(s5_yev, 1)

            for i in range(S5T):
                q = i % 2
                xr, xi = ps[:, 2 + 2 * q, :], ps[:, 3 + 2 * q, :]
                c_, s_ = rotc[:, i, :], rots[:, i, :]
                gr, gi = g5[:, 2 * q, :], g5[:, 2 * q + 1, :]
                dve.wait_ge(s5_x, i + 1)
                if i >= 2:
                    dve.wait_ge(s5_h, i - 1)
                link(tt(vt[:, 0, :], xr[:, 0:TP], c_, ALU.mult))
                link(tt(vt[:, 1, :], xi[:, 0:TP], s_, ALU.mult))
                link(tt(gr, vt[:, 0, :], vt[:, 1, :], ALU.add))
                link(tt(vt[:, 0, :], xi[:, 0:TP], c_, ALU.mult))
                link(tt(vt[:, 1, :], xr[:, 0:TP], s_, ALU.mult))
                link(tt(gi, vt[:, 0, :], vt[:, 1, :], ALU.subtract))
                link(v.tensor_copy(s5x[:, 0, i, :], xr[:, TP:T]))
                v.tensor_copy(s5x[:, 1, i, :], xi[:, TP:T]).then_inc(s5_xused, 1)
                m_ = mag[:, i:i + 1].to_broadcast([P, TP])
                link(v.tensor_tensor_scan(gr, m_, gr, 0.0, ALU.mult, ALU.add))
                v.tensor_tensor_scan(gi, m_, gi, 0.0, ALU.mult, ALU.add).then_inc(s5_g, 1)
                if i % 4 == 1 and i > 1:
                    s5_y_out(i // 4 - 1)
            dve.wait_ge(s5_xused, S5T)
            dve.wait_ge(s5_g, S5T)
            sh = [P, S5T, NBATCH]
            ar, ai = abr.unsqueeze(2).to_broadcast(sh), abi.unsqueeze(2).to_broadcast(sh)
            w0, w1_ = part(conv_r, 0, S5T, NBATCH), part(conv_r, P, S5T, NBATCH)
            xl = [s5x[:, q].rearrange("p i (b l) -> p i b l", l=LSAMP) for q in range(2)]
            hl = [s5h[:, q].rearrange("p i (b l) -> p i b l", l=LSAMP) for q in range(2)]
            prev = [st5[:, q].rearrange("p b i -> p i b") for q in range(2)]
            for l in range(LSAMP):
                for q, (x, y, op) in enumerate(((0, 1, ALU.subtract), (1, 0, ALU.add))):
                    link(tt(w0, prev[x], ar, ALU.mult))
                    link(tt(w1_, prev[y], ai, ALU.mult))
                    link(tt(w0, w0, w1_, op))
                    link(tt(hl[q][:, :, :, l], w0, xl[q][:, :, :, l], ALU.add))
                prev = [hl[q][:, :, :, l] for q in range(2)]
            link(v.tensor_copy(st5[:, 0].rearrange("p b i -> p i b"), prev[0]))
            dve.wait_ge(s5_h, S5T)
            v.tensor_copy(st5[:, 1].rearrange("p b i -> p i b"), prev[1]).then_inc(s5_hs, 1)
            s5_y_out(UT - 1)
            dve.wait_ge(s5_y, 1)
            for j in range(UT):
                last = stt(uT[:, j, TP:T], uT[:, j, TP:T], s5d[:, j:j + 1], ps[:, 2, j * TS:(j + 1) * TS], ALU.mult, ALU.add)
            last.then_inc(s5_yev, 1)

            def gated(j):
                dve.wait_ge(glu_sig, j + 1)
                link(tt(sq[:, j % 2, :], ps[:, 0, 0:T], sq[:, j % 2, :], ALU.mult))
                tt(gates[:, KD + j, :], gates[:, KD + j, :], sq[:, j % 2, :], ALU.mult).then_inc(glu_ev, 1)

            gated(0)
            dve.wait_ge(cb_ps, 1)
            for i, (c0, n) in enumerate(CHUNKS):
                if i == 2:
                    dve.wait_ge(acs_ps, 1)
                o_ = (i % 2) * 256
                mask = upper[:, :] if i < 2 else supper_r[0:TS, :]
                tt(CBm[0:n, :, c0:c0 + n], ps[0:n, 4 + i // 2, o_:o_ + 2 * n].rearrange("p (g q) -> p g q", g=G),
                   mask.unsqueeze(1).to_broadcast([n, G, n]), ALU.mult).then_inc(cb_ok, 1)
            dve.wait_ge(acs_ps, 1)
            p5 = ps[:, 5, 128:224].rearrange("p (i h) -> p i h", i=3)
            v.tensor_copy(acs[:, 0:2, :], p5[:, 0:2, :]).then_inc(acs_ok, 1)
            v.tensor_copy(acs[0:TS, 2, :], p5[0:TS, 2, :]).then_inc(acs_ok, 1)
            gated(1)
            dve.wait_ge(acs_ok, 3)
            link(tt(dte[:, 0:2, :], acs[:, 0:2, H:2 * H], acs[:, 0:2, 0:H], ALU.subtract))
            tt(dte[0:TS, 2, :], acs[0:TS, 2, H:2 * H], acs[0:TS, 2, 0:H], ALU.subtract).then_inc(dte_pre, 1)
            for i, (c0, n) in enumerate(CHUNKS):
                dve.wait_ge(xt_ps, i + 1)
                for q in range(2):
                    tt(Xdt[0:n, i, q * 512:(q + 1) * 512].rearrange("p (h d) -> p h d", d=HD),
                       ps[0:n, 6 + q, :].rearrange("p (h d) -> p h d", d=HD),
                       dt3[0:n, i, 8 * q:8 * q + 8].unsqueeze(2).to_broadcast([n, 8, HD]), ALU.mult).then_inc(xdt_ok, 1)
                gated(2 + i)
            gated(5)
            dve.wait_ge(st_ps, 2)
            dve.wait_ge(dte_ok, 1)
            for gr in range(G):
                hf3 = hfT[:, gr, :].rearrange("p (h d) -> p h d", d=HD)
                link(tt(hf3, h1T[:, gr, :].rearrange("p (h d) -> p h d", d=HD),
                        acs[:, 1, H + 8 * gr:H + 8 * gr + 8].unsqueeze(2).to_broadcast([P, 8, HD]), ALU.mult))
                tt(hfT[:, gr, :], hfT[:, gr, :], ps[:, 2 + gr, :], ALU.add).then_inc(hf_ok, 1)
            gated(6)
            dve.wait_ge(qs_ps, 1)
            dve.wait_ge(bm_ok, 2)
            tt(MTs[0:TS], ps[0:TS, 4, :].rearrange("p (h q) -> p h q", h=H),
               acs[0:TS, 2, 0:H].unsqueeze(2).to_broadcast([TS, H, TS]), ALU.subtract).then_inc(qs_diff, 1)
            dve.wait_ge(qs_diff, 1)
            tt(MTs[0:TS], MTs[0:TS], supper_r[0:TS, :].unsqueeze(1).to_broadcast([TS, H, TS]), ALU.mult).then_inc(qs_msk, 1)
            gated(7)
            dve.wait_ge(qs_exp, 1)
            for gr in range(G):
                ms = MTs[0:TS, gr * (H // G):(gr + 1) * (H // G), :]
                tt(ms, ms, CBm[0:TS, gr, TP:T].unsqueeze(1).to_broadcast([TS, H // G, TS]), ALU.mult).then_inc(qs_ok, 1)

            def decayed(hp):
                dve.wait_ge(h0_ps, 2 * hp + 2)
                hv = h0[hp % NH0]
                tt(hv, hv, sample(eft[:, hp, :])[:, :, LSAMP - 1:LSAMP].to_broadcast([P, NBATCH, NS]), ALU.mult).then_inc(h0_dec, 1)

            def renewed(hp):
                dve.wait_ge(ss_ps, hp + 1)
                dve.wait_ge(h0_dec, hp + 1)
                h2v = h0[hp % NH0].rearrange("p (a b) n -> p a (b n)", a=2)
                tt(h2v, h2v, ps[:, 4:6, :], ALU.add).then_inc(ss_ok, 1)

            def y_out(j):
                dve.wait_ge(q_y, j + 1)
                if j:
                    dve.wait_ge(q_yev, j)
                link(stt(nt, xbcT[:, j, :], dskip[:, j:j + 1], ps[:, j % 2, 0:T], ALU.mult, ALU.add))
                link(tt(nt[:, TP:T], nt[:, TP:T], yoff[:, j, :], ALU.add))
                tt(zT[:, j, :], zT[:, j, :], nt, ALU.mult).then_inc(q_yev, 1)

            def group_norm(gr):
                dve.wait_ge(q_yev, KD)
                norm_scale(4 + gr, 12 + 4 * gr, D // G, nv, ny, nt, 2 + gr)
                for j in range(4 * gr, 4 * gr + 4):
                    stt(zT[:, j, :], zT[:, j, :], ssdw[:, j:j + 1], ny, ALU.mult, ALU.mult).then_inc(yn_ok, 1)
                dve.wait_ge(yn_ok, 4 * gr + 4)

            dve.wait_ge(tile_ev, NT)

            def off_decayed(hp):
                dve.wait_ge(yoT_ps, hp + 1)
                raw = ps[:, 7, 0:1]
                own = bass.AP(raw.tensor, raw.offset, [list(raw.ap[0]), [P + 4 * LSAMP, 2], [32 + LSAMP, 4], [1, LSAMP]])
                v4 = [t[:, hp, :].rearrange("p (r c l) -> p r c l", r=2, c=4) for t in (yoff, eft)]
                tt(v4[0], own, v4[1], ALU.mult).then_inc(yoff_ok, 1)

            for qd in range(4):
                dve.wait_ge(q_ps, qd + 1)
                if qd:
                    dve.wait_ge(q_y, 2 * qd)
                tt(MT.rearrange("p h (i q) -> p i h q", i=2), ps[:, 0:2, :].rearrange("p i (h q) -> p i h q", h=4),
                   acs[:, 0:2, 4 * qd:4 * qd + 4].unsqueeze(3).to_broadcast([P, 2, 4, CH]), ALU.subtract).then_inc(q_diff, 1)
                dve.wait_ge(q_diff, qd + 1)
                m3 = MT.rearrange("p h (i q) -> p h i q", i=2)
                tt(m3, m3, upper[:, :].unsqueeze(1).unsqueeze(1).to_broadcast([P, 4, 2, CH]), ALU.mult).then_inc(q_msk, 1)
                decayed(2 * qd)
                ada_copy(4 + 2 * qd)
                gr = qd // 2
                dve.wait_ge(q_exp, 2 * qd + 1)
                tt(CTs, CTs, xbcT[:, KD + G + gr, CH:TP].unsqueeze(1).to_broadcast([P, 4, CH]), ALU.mult).then_inc(q_mt, 1)
                renewed(2 * qd)
                off_decayed(2 * qd)
                ada_add(4 + 2 * qd)
                dve.wait_ge(q_exp, 2 * qd + 2)
                tt(MT, MT, CBm[:, gr, 0:TP].unsqueeze(1).to_broadcast([P, 4, TP]), ALU.mult).then_inc(q_mt, 1)
                decayed(2 * qd + 1)
                ada_copy(5 + 2 * qd)
                renewed(2 * qd + 1)
                off_decayed(2 * qd + 1)
                dve.wait_ge(yoff_ok, 2 * qd + 2)
                y_out(2 * qd)
                y_out(2 * qd + 1)
                ada_add(5 + 2 * qd)
            group_norm(0)
            group_norm(1)
            dve.wait_ge(mod_ok, 12)
            scales(nw2, 32)
            for j in range(KD):
                dve.wait_ge(outa_ps, j + 1)
                link(tt(gates[:, j, :], gates[:, j, :], ps[:, j % 2, 0:T], ALU.mult))
                tt(gates[:, j, :], gates[:, j, :], gates[:, KD + j, :], ALU.add).then_inc(mrg_ok, 1)

            def residual(j, src, gate, done):
                link(stt(xT[:, j, 0:TP], src[:, 0:TP], mod[:, gate + j, 0:1], xT[:, j, 0:TP], ALU.mult, ALU.add))
                link(tt(sample(nt[:, 0:TS]), sample(src[:, TP:T]), per_sequence(mod[:, gate + j, 1:NC]), ALU.mult))
                tt(xT[:, j, TP:T], xT[:, j, TP:T], nt[:, 0:TS], ALU.add).then_inc(done, 1)

            for j in range(KD):
                dve.wait_ge(mix_ps, j + 1)
                residual(j, ps[:, 2 + j % 2, 0:T], 16, x1_ok)
            norm_scale(4, 24, D, nv, ny, nt, 4)
            dve.wait_ge(st_hp, 16)
            normalize(ny)
            modulate(24, 2)

            S = [r_[:, k, :].rearrange("p (c e) -> p c e", e=NE) for k in range(40)]
            m3_, g12 = [P, 3, NE], [P, 3 * NG, EPG]

            def col(k):
                return r_[:, k, 0:3]

            def wide(c3):
                return c3.unsqueeze(2).to_broadcast(m3_)

            link(v.memset(score, 0.0))
            link(v.memset(posm, -1.0))
            v.memset(yacc, 0.0).then_inc(cmb_ok, 8)
            dve.wait_ge(lg_ps, 1)
            link(v.tensor_copy(score[:, 0:2, :], ps[:, 6, 0:2 * NE].rearrange("p (c e) -> p c e", e=NE)))
            link(v.tensor_copy(score[0:TS, 2, :], ps[0:TS, 6, 2 * NE:3 * NE]))
            link(v.tensor_reduce(col(5), score, AX_X, ALU.max))
            tt(score, score, wide(col(5)), ALU.subtract).then_inc(sm_in, 1)
            dve.wait_ge(sm_exp, 1)
            link(v.tensor_reduce(col(5), score, AX_X, ALU.add))
            link(v.reciprocal(col(5), col(5)))
            link(tt(score, score, wide(col(5)), ALU.mult))
            link(tt(sel, score, brt[:, :].unsqueeze(1).to_broadcast(m3_), ALU.add))
            s4 = r_[:, 1, :].rearrange("p (c e) -> p c e", e=EPG)
            e4 = [s4[:, :, k] for k in range(4)]
            q = [r_[:, 6 + k, 0:3 * NG] for k in range(8)]
            link(tt(q[0], e4[0], e4[1], ALU.max))
            link(tt(q[1], e4[0], e4[1], ALU.min))
            link(tt(q[2], e4[2], e4[3], ALU.max))
            link(tt(q[3], e4[2], e4[3], ALU.min))
            link(tt(q[4], q[0], q[2], ALU.max))
            link(tt(q[5], q[0], q[2], ALU.min))
            link(tt(q[6], q[1], q[3], ALU.max))
            link(tt(q[5], q[5], q[6], ALU.max))
            link(tt(q[4], q[4], q[5], ALU.add))

            def first_max(vals, key, m, one):
                n = vals.shape[-1]
                bc = [P, 3, n]
                link(v.tensor_reduce(m, vals, AX_X, ALU.max))
                link(tt(one, vals, m.unsqueeze(2).to_broadcast(bc), ALU.is_equal))
                link(tt(one, one, key.unsqueeze(1).to_broadcast(bc), ALU.mult))
                link(v.tensor_reduce(m, one, AX_X, ALU.max))
                link(tt(one, one, m.unsqueeze(2).to_broadcast(bc), ALU.is_equal))

            best = q[7]
            first_max(q[4].rearrange("p (c g) -> p c g", g=NG), keyg[:, :], col(5), best.rearrange("p (c g) -> p c g", g=NG))
            msk, one1, one2 = S[14], S[15], S[16]
            msk4 = r_[:, 14, :].rearrange("p (c e) -> p c e", e=EPG)
            link(tt(msk4, s4, best.unsqueeze(2).to_broadcast(g12), ALU.mult))
            link(ts(q[0], best, -1.0, BIG, ALU.add, ALU.mult))
            link(tt(msk4, msk4, q[0].unsqueeze(2).to_broadcast(g12), ALU.add))
            first_max(msk, keye[:, :], col(5), one1)
            link(stt(msk, one1, -BIG, msk, ALU.mult, ALU.add))
            first_max(msk, keye[:, :], col(5), one2)
            tt(s_all, one1, one2, ALU.add).then_inc(top_ok, 1)
            dve.wait_ge(top_ok, 1)
            link(tt(comb, score, s_all, ALU.mult))
            link(v.tensor_reduce(col(5), comb, AX_X, ALU.add))
            link(v.reciprocal(col(5), col(5)))
            link(tt(comb, comb, wide(col(5)), ALU.mult))
            dve.wait_ge(pos_ps, 1)
            for rr, cc in ((P, slice(0, 2)), (TS, slice(2, 3))):
                pp = ps[0:rr, 7, 0:3 * NE].rearrange("p (c e) -> p c e", e=NE)[:, cc, :]
                link(stt(posm[0:rr, cc, :], pp, 1.0, s_all[0:rr, cc, :], ALU.add, ALU.mult))
            link(ts(posm, posm, -1.0, None, ALU.add))
            link(v.tensor_reduce(npf[:, 1:2], ps[:, 7, 48:64], AX_X, ALU.max))
            link(v.memset(npf[:, 2:3], 1.0))
            for k in range(1, MAXPASS):
                link(stt(npf[:, 2:3], npf[:, 1:2], float(CAP * k), npf[:, 2:3], ALU.is_gt, ALU.add))
            v.tensor_copy(npi[:, :], npf[:, 2:3]).then_inc(route_ok, 1)
            dve.wait_ge(route_ok, 1)

            b4 = [P, 3, 2, CAP]

            def choose(q, v_, first, after=None):
                if not first:
                    dve.wait_ge(xg_ps[1], v_)
                    dve.wait_ge(selw_ok, v_)
                if after is not None:
                    dve.wait_ge(pos_dn, after)
                tt(selo, iota[:, :].unsqueeze(1).unsqueeze(1).to_broadcast(b4),
                   posm[:, :, bass.ds(2 * q, 2)].unsqueeze(3).to_broadcast(b4), ALU.is_equal).then_inc(selo_ok, 1)

            def add_up(v_):
                dve.wait_ge(cmb_ok, 8 * v_ + 8)
                for j in range(KD):
                    dve.wait_ge(cmb_ps, 8 * v_ + j + 1)
                    tt(yacc[:, j, :], yacc[:, j, :], ps[:, (7, 4)[j % 2], 0:T], ALU.add).then_inc(cmb_ok, 1)

            def experts(q, v_, first, prev, following):
                dve.wait_ge(selo_ok, v_ + 1)
                if not first:
                    dve.wait_ge(pT_ps, v_)
                tt(selw, selo, comb[:, :, bass.ds(2 * q, 2)].unsqueeze(3).to_broadcast(b4), ALU.mult).then_inc(selw_ok, 1)
                if following:
                    choose(q + 1, v_ + 1, False)
                if prev:
                    add_up(v_ - 1)
                dve.wait_ge(act_s, v_ + 1)
                dve.wait_ge(unit_used, N_UNITS + 6 * v_ + 4)
                if not first:
                    dve.wait_ge(aT_ps, v_)
                tt(act_e[:, :], hs_[:, :], ps[:, 3, :], ALU.mult).then_inc(act_ok, 1)
                dve.wait_ge(pT_ps, v_ + 1)
                v.tensor_copy(pT[:, :], ps[:, 7, 0:T]).then_inc(pT_ok, 1)

            choose(0, 0, True)
            experts(0, 0, True, False, True)
            with dve.Fori(1, PAIRS - 1) as q_:
                experts(q_, q_, False, True, True)
            experts(PAIRS - 1, PAIRS - 1, False, True, False)
            add_up(PAIRS - 1)
            passes = dve.value_load(npi[0:1, 0:1], min_val=1, max_val=MAXPASS)
            with dve.If(passes > 1):
                with dve.Fori(1, passes) as n_:
                    v0 = n_ * PAIRS
                    dve.wait_ge(selo_ok, v0)
                    ts(posm, posm, -float(CAP), None, ALU.add).then_inc(pos_dn, 1)
                    choose(0, v0, False, n_)
                    experts(0, v0, False, False, True)
                    with dve.Fori(1, PAIRS - 1) as q_:
                        experts(q_, n_ * PAIRS + q_, False, True, True)
                    experts(PAIRS - 1, v0 + (PAIRS - 1), False, True, False)
                    add_up(v0 + (PAIRS - 1))

            dve.wait_ge(cmb_ok, 8 * PAIRS * passes + 8)
            ys = yacc[:, :, TP:T].rearrange("p j (b l) -> p j b l", l=LSAMP)
            link(tt(ys, ys, mod[:, 40:48, 1:NC].unsqueeze(3).to_broadcast([P, KD, NBATCH, LSAMP]), ALU.mult))
            link(tt(xT[:, :, TP:T], xT[:, :, TP:T], yacc[:, :, TP:T], ALU.add))
            for j in range(KD):
                stt(xT[:, j, 0:TP], yacc[:, j, 0:TP], mod[:, 40 + j, 0:1], xT[:, j, 0:TP], ALU.mult, ALU.add).then_inc(x2_ok, 1)
            link(v.memset(tok_v, 1.0))
            dve.wait_ge(sq_used, 32)
            for rr, cc in ((P, slice(0, 2)), (TS, slice(2, 3))):
                link(ts(tok_v[0:rr, cc], ps[0:rr, 6, 0:6].rearrange("p (i k) -> p i k", k=2)[:, cc, 0], 1.0 / D, EPS, ALU.mult, ALU.add))
            v.tensor_copy(tok_v, tok_v).then_inc(var_ok, 1)
            dve.wait_ge(rs_ok, 5)
            link(tt(tok_t, tok_v, tok_rs, ALU.mult))
            link(tt(tok_t, tok_t, tok_rs, ALU.mult))
            link(ts(tok_t, tok_t, -0.5, 1.5, ALU.mult, ALU.add))
            tt(tok_rs, tok_rs, tok_t, ALU.mult).then_inc(fin_rs, 1)
            dve.wait_ge(fin_rs, 1)
            dve.wait_ge(fin_ps, 2)
            for i, (t0, n) in enumerate(CHUNKS):
                ts(y_tok[0:n, i, 512:D], ps[0:n, 2 * i + 1, :], tok_rs[0:n, i:i + 1], None, ALU.mult).then_inc(fin_cp, 1)


_OUTS = [("y_prompt", (1, TP, D)), ("y_sample", (NBATCH, LSAMP, D)),
         ("ssm_prompt", (1, 1, H, HD, NS)), ("ssm_sample", (1, NBATCH, H, HD, NS)),
         ("conv_prompt", (1, 1, CONV - 1, XBC)), ("conv_sample", (1, NBATCH, CONV - 1, XBC)),
         ("s5_re_prompt", (1, 1, S5G, S5N)), ("s5_re_sample", (1, NBATCH, S5G, S5N)),
         ("s5_im_prompt", (1, 1, S5G, S5N)), ("s5_im_sample", (1, NBATCH, S5G, S5N))]


def kernel(**inputs):
    import numpy as _np
    import concourse.bacc as _bacc
    from concourse import mybir as _mybir
    from concourse.bass_utils import run_bass_kernel_spmd as _run

    nc = _bacc.Bacc("TRN2", target_bir_lowering=False, num_devices=1, dynamic_dma_scratch_size=1024)
    arrays, a, o = {}, {}, {}
    for name, x in inputs.items():
        x = _np.ascontiguousarray(x)
        arrays[f"in_{name}"] = x
        a[name] = nc.dram_tensor(f"in_{name}", x.shape, _mybir.dt.from_np(x.dtype), kind="ExternalInput").ap()
    for name, shape in _OUTS:
        o[name] = nc.dram_tensor(f"out_{name}", shape, _mybir.dt.float32, kind="ExternalOutput").ap()
    hybrid_decoder_step(nc, a, o)
    r = _run(nc, [arrays], core_ids=[0])
    return tuple(r.results[0][f"out_{name}"] for name, _ in _OUTS)
```

```python
from contextlib import ExitStack

import concourse.bass as bass
from concourse import mybir

F32 = mybir.dt.float32
I32 = mybir.dt.int32
ALU = mybir.AluOpType
ACT = mybir.ActivationFunctionType
AX_X = mybir.AxisListType.X

P = 128
BANK = 512
D = 1024
KD = D // P
NBATCH, LSAMP = 8, 4
TP, TS = 256, NBATCH * LSAMP
T = TP + TS
CH = 128
CHUNKS = [(0, 128), (128, 128), (256, 32)]
NC = 1 + NBATCH
H, HD, NS = 16, 64, 128
G = 2
CONV = 4
XBC = D + 2 * G * NS
XT = XBC // P
S5G, S5N, S5C = 32, 64, 16
S5T = S5G * S5N // P
UT = S5G * S5C // P
NE, NG, EPG = 16, 4, 4
FE = 512
FT = FE // P
CAP = 64
PAIRS = NE // 2
MAXPASS = -(-T // CAP)
UNITS_OF = ((4, 5), (6, 7), (8,), (9,))
CMB_BANKS = (7, 4, 0, 1)
NH0 = 4
EPS = 1e-6
IN_XBC, IN_DT, IN_U, IN_GATE = D, D + XBC, D + XBC + H, D + XBC + H + S5G * S5C
TWO_PI = 6.283185307179586
TWO_PI_HI = 6.28125
ROUND = 12582912.0
PI_IN = 3.1415925
BIG = 1e30

SLOT = 4096
NR = 5
MOE_SLOTS = ([3, 4, 0, 1, 2, 5], [6, 7, 8, 1, 2, 5])
ALTERNATE = 3
U_ADA1, U_U, U_XBC, U_Z, U_GATE, U_GLU, U_ADA2, U_OUTA, U_OUT, U_ADA3, N_UNITS = 0, 4, 5, 8, 10, 14, 16, 23, 25, 27, 28


def uses(slot):
    return len([n for n in range(N_UNITS) if n % NR == slot])


def ada_unit(i):
    return U_ADA1 + i if i < 4 else U_ADA2 + i - 4 if i < 11 else U_ADA3


def hybrid_decoder_step(nc, a, o):
    with ExitStack() as ctx:
        def sb(name, cols, dt=F32):
            return ctx.enter_context(nc.sbuf_tensor(name, [P, cols], dt))

        def sem(name):
            return ctx.enter_context(nc.semaphore(name))

        def part(region, off, *shape):
            n = 1
            for s in shape:
                n *= s
            v = region[:, off:off + n]
            if len(shape) == 2:
                return v.rearrange("p (a b) -> p a b", b=shape[1])
            if len(shape) == 3:
                return v.rearrange("p (a b c) -> p a b c", b=shape[1], c=shape[2])
            return v

        ring = sb("ring", NR * SLOT)
        tok_r = sb("tok_region", 3 * D)
        xT = part(sb("x_features", KD * T), 0, KD, T)
        proj_r = sb("projection_region", SLOT)
        hT_r = proj_r[:, 0:KD * T]
        hT = part(hT_r, 0, KD, T)
        u_r = proj_r[:, KD * T:(KD + UT) * T]
        uT = part(u_r, 0, UT, T)
        xbc_r = sb("xbc_region", XT * T)
        xbcT = part(xbc_r, 0, XT, T)
        z_r = sb("z_region", KD * T)
        zT = part(z_r, 0, KD, T)
        gate_r = sb("gate_region", 2 * KD * T)
        gates = part(gate_r, 0, 2 * KD, T)
        mix_r = sb("mixer_region", 13312)
        conv_r = proj_r[:, (KD + UT) * T:SLOT]

        x_tok = part(tok_r, 0, 3, D)
        s5x = part(tok_r, 0, 2, S5T, TS)
        s5h = part(tok_r, 2 * S5T * TS, 2, S5T, TS)
        Xdt = part(tok_r, 0, 3, D)

        c_in = part(gate_r, 0, D)
        prow1 = part(gate_r, 1024, P)
        prow2 = part(gate_r, 1152, P)
        prow3 = part(gate_r, 1280, P)
        b_raw = part(gate_r, 1408, 2, S5T, S5C)
        c_raw = part(gate_r, 1920, 2, UT, S5N)
        st_rows = part(gate_r, 2432, 2, P)
        exp_in = part(gate_r, 2688, 4)
        conv_in = part(gate_r, 2692, XBC)
        n1v, n1y, n1t = (part(z_r, k * T, T) for k in range(3))
        nv, ny, nt, sq_acc = (part(u_r, k * T, T) for k in range(4))
        sq = part(conv_r, 0, 2, T)
        rows = part(conv_r, 0, 2, 315)

        rotc = part(mix_r, 0, S5T, TP)
        rots = part(mix_r, S5T * TP, S5T, TP)
        off = 2 * S5T * TP
        bT = part(mix_r, off, 2, UT, P)
        cTs5 = part(mix_r, off + 1024, 2, UT, P)
        g5 = part(mix_r, off + 2048, 4, TP)
        h5 = part(mix_r, off + 3072, 4, TP)
        pt = part(mix_r, off + 4096, 2, TP)
        bblk = part(z_r, 3 * T, 2, S5T, 2 * S5C)
        cblk = part(gate_r, 0, 2, UT, P)
        vt = part(conv_r, 0, 2, TP)
        Xs = part(mix_r, 0, 3, D)
        B_tok = part(mix_r, 3072, 3, 2 * NS)
        CBm = part(mix_r, 3840, 2, T)
        CTs = part(mix_r, 4416, 4, CH)
        h1T = part(mix_r, 4928, 2, 512)
        hfT = part(mix_r, 5952, 2, 512)
        h0 = [part(mix_r, 6976, NBATCH, NS), part(mix_r, 8000, NBATCH, NS), part(hT_r, 1024, NBATCH, NS),
              part(mix_r, 10048, NBATCH, NS)]
        h0T = part(mix_r, 9024, NBATCH * NS)
        yraw = part(hT_r, 2048, 2, P)
        Bm = part(mix_r, 11072, 2, NBATCH * NS)
        h_out = part(mix_r, 9024, 8, P)
        MTs = part(mix_r, 3072, H, TS)
        MT = part(hT_r, 0, 4, TP)

        cT = part(sb("c_features", KD * 32), 0, KD, 32)
        ada_s = part(sb("ada_sum", 512), 0, 512)
        mod = part(sb("modulation", 48 * NC), 0, 48, NC)
        amul = part(sb("norm_scale", KD * NC), 0, KD, NC)
        ident = sb("ident", P)
        ones = sb("ones", P)
        upper = sb("upper", P)
        strict = sb("strict", P)
        same_r = sb("same_sequence", TS)
        supper_r = sb("same_upper", TS)
        blk = sb("sequence_of", NBATCH)
        sel9 = sb("fold_rows", 32)
        par8 = sb("group_rows", 8)
        par2 = sb("group_parity", 2)
        iota = sb("slot_number", CAP)
        keyg = sb("group_key", NG)
        keye = sb("expert_key", NE)
        pc1 = sb("params1", 104)
        pc2 = sb("params2", 80)
        pc3 = sb("params3", 16)
        cs_r = sb("conv_state", XT * 24)
        csT = part(cs_r, 0, XT, 24)
        tails_r = sb("conv_tails", XT * 27)
        tails = part(tails_r, 0, XT, 27)
        w_dt = part(sb("w_dt", KD * H), 0, KD, H)
        w_rt = part(sb("w_router", KD * NE), 0, KD, NE)
        dtb = sb("dt_bias_row", H)
        alog = sb("a_log_row", H)
        brt = sb("b_router_row", NE)
        dt3 = part(sb("dt", 3 * H), 0, 3, H)
        da3 = part(sb("dta", 3 * H), 0, 3, H)
        dtt = part(sb("dt_tmp", 3 * H), 0, 3, H)
        dte = part(sb("decay_to_end", 3 * H), 0, 3, H)
        acs = part(sb("a_cumsum", 3 * 2 * H), 0, 3, 2 * H)
        eft = part(tails_r, 0, KD, TS)
        yoff = part(cs_r, 0, KD, TS)
        s5c = part(tok_r, 2048, 24, S5T)
        st5_flat = tok_r[:, 2432:2432 + 2 * P]
        st5 = part(tok_r, 2432, 2, NBATCH, S5T)
        fin5 = part(tok_r, 2688, 2, S5T)
        npf = sb("passes_f", 8)
        npi = sb("passes_i", 1, I32)

        ps = ctx.enter_context(nc.psum_tensor("psum", [P, 8, BANK], F32))

        nw1, nw2, ssdw = pc1[:, 0:8], pc1[:, 8:16], pc1[:, 16:24]
        convw = pc1[:, 24:72].rearrange("p (k j) -> p k j", j=XT)
        convb, s5d, fnw, dskip = pc1[:, 72:84], pc1[:, 84:88], pc1[:, 88:96], pc1[:, 96:104]
        b_ada, a_re, a_im = pc2[:, 0:48], pc2[:, 48:64], pc2[:, 64:80]

        ld_x, ld_c, ld_par, ld_exp, ld_state, ld_bc, ld_rows, ld_wsm = (
            sem(n) for n in ("ld_x", "ld_c", "ld_par", "ld_exp", "ld_state", "ld_bc", "ld_rows", "ld_w_small"))
        ld_h0 = [sem(f"ld_h0_{i}") for i in range(NH0)]
        landed = [sem(f"ring_landed{i}") for i in range(NR + 4)]
        unit_used = sem("unit_used")
        consts = sem("consts")
        vconsts = sem("vector_consts")
        dte_pre, q_msk, sm_in, sm_exp = sem("dte_pre"), sem("q_masked"), sem("softmax_in"), sem("softmax_exp")
        pos_dn = sem("positions_down")
        expd = sem("expanded")
        c_silu, cT_ps, cT_ok = sem("c_silu"), sem("cT_ps"), sem("cT_ok")
        par_ps, par_ok = sem("par_ps"), sem("par_ok")
        x_ps, x_ok = sem("x_ps"), sem("x_ok")
        sq_ok, sq_used = sem("sq_ok"), sem("sq_used")
        var_ok, rs_ok = sem("var_ok"), sem("rs_ok")
        ada_cp, adaT_ps, mod_ok = sem("ada_cp"), sem("adaT_ps"), sem("mod_ok")
        xn_ok, amul_ok = sem("x_normed"), sem("norm_scale_ok")
        h_ok, hp_ok = sem("h_sample_ok"), sem("h_prompt_ok")
        tile_ps, tile_ev = sem("tile_ps"), sem("tile_ev")
        conv_acc, conv_ok = sem("conv_acc"), sem("conv_ok")
        dt_ps, dt_pre, dt_exp, da_ok = sem("dt_ps"), sem("dt_pre"), sem("dt_exp"), sem("da_ok")
        tail_ps, tail_cp = sem("tail_ps"), sem("tail_cp")
        dsc, trig, rot_u, rot_ok = sem("s5_discrete"), sem("s5_trig"), sem("rot_u"), sem("rot_ok")
        blk5, s5w_ps, s5w_ok = sem("s5_blocks"), sem("s5w_ps"), sem("s5w_ok")
        s5_x, s5_xused, s5_g, s5_h, s5_hused = sem("s5_x"), sem("s5_x_used"), sem("s5_g"), sem("s5_h"), sem("s5_h_used")
        s5_y, s5_yev, s5_hs = sem("s5_y"), sem("s5_y_ev"), sem("s5_hs")
        gelu_ok = sem("gelu_ok")
        s5f_cp = sem("s5f_cp")
        glu_ps, glu_sig, glu_ev = sem("glu_ps"), sem("glu_sig"), sem("glu_ev")
        cb_ps, cb_ok, acs_ps, acs_ok, dte_ok = sem("cb_ps"), sem("cb_ok"), sem("acs_ps"), sem("acs_ok"), sem("dte_ok")
        xt_ps, xdt_ok, xs_ok, bt_ok = sem("xt_ps"), sem("xdt_ok"), sem("xs_ok"), sem("bt_ok")
        st_ps, h1_ok, hf_ok, hf_ps, hf_cp = sem("st_ps"), sem("h1_ok"), sem("hf_ok"), sem("hf_ps"), sem("hf_cp")
        h0_ps, h0_cp, yo_ps, ss_ps, ss_ok = sem("h0_ps"), sem("h0_cp"), sem("yo_ps"), sem("ss_ps"), sem("ss_ok")
        qs_ps, qs_diff, qs_msk, qs_exp, qs_ok = (sem(n) for n in ("qs_ps", "qs_diff", "qs_masked", "qs_exp", "qs_ok"))
        yo_cp, yoT_ps = sem("yo_copied"), sem("yoT_ps")
        yoff_ok, g0_ps = sem("yoff_ok"), sem("group0_ps")
        q_ps, q_diff, q_exp, q_mt, q_y, q_yev = sem("q_ps"), sem("q_diff"), sem("q_exp"), sem("q_mt"), sem("q_y"), sem("q_yev")
        bm_ok, yn_ok = sem("bm_ok"), sem("yn_ok")
        outa_ps, mrg_ok = sem("outa_ps"), sem("merged_ok")
        mix_ps, x1_ok = sem("mix_ps"), sem("x1_ok")
        h2t_ps, h2t_ok = sem("h2t_ps"), sem("h2t_ok")
        lg_ps, top_ok, pos_ps, route_ok = sem("logits_ps"), sem("top_ok"), sem("pos_ps"), sem("route_ok")
        selo_ok, selw_ok, xe_ok = sem("chosen"), sem("weights_chosen"), sem("xe_ok")
        xg_cp, xe_ps = sem("xg_copied"), sem("xe_ps")
        xg_ps = [sem("gathered_first_half"), sem("gathered_second_half")]
        act_s, act_ok = sem("act_silu"), sem("act_ok")
        aT_ps, aT_ok, pT_ps, pT_ok = sem("aT_ps"), sem("aT_ok"), sem("pT_ps"), sem("pT_ok")
        w2_ps, ye_ok, cmb_ps, cmb_ok = sem("w2_ps"), sem("ye_ok"), sem("combine_ps"), sem("combine_ok")
        x2_ok, fin_ok, fin_ps, fin_cp, fin_rs = sem("x2_ok"), sem("fin_ok"), sem("fin_ps"), sem("fin_cp"), sem("fin_rs")
        st_conv, st_s5, st_hp, st_y = sem("st_conv"), sem("st_s5"), sem("st_ssm_prompt"), sem("st_y")
        st_hs = [sem(f"st_ssm_{i}") for i in range(NH0)]
        dve_chain, act_chain, pool_chain = sem("dve_chain"), sem("act_chain"), sem("pool_chain")

        def linker(eng, chain):
            n = [0]

            def link(ins):
                n[0] += 1
                ins.then_inc(chain, 1)
                eng.wait_ge(chain, n[0])
            return link

        def ring_tile(slot, k):
            at = (0, SLOT + D, 2 * SLOT + D, 0)[slot - NR] if slot >= NR else slot * SLOT
            region = ring if slot < NR else mix_r if slot < NR + 3 else proj_r
            return region[:, at:at + SLOT].rearrange("p (k n) -> p k n", k=k)

        def unit_tile(n, k):
            return ring_tile(n % NR, k)

        def sums_bank(i):
            return (5, 3)[i % 2] if i < 4 else 6 if i < 11 else 5

        def turned(i, c0, c1):
            bank, at = (6, 0) if i < 4 else (7, 256)
            return ps[:, bank, at + c0 * NC:at + c1 * NC]

        def sample(v):
            return v.rearrange("p (b l) -> p b l", l=LSAMP)

        h2_tok = part(tok_r, 0, 3, D)
        y_tok = part(tok_r, 0, 3, D)
        yacc = part(xbc_r, 0, KD, T)
        selw = part(xbc_r, KD * T, 3, 2, CAP)
        selw2 = selw.rearrange("p c e s -> p c (e s)")
        selo = part(xbc_r, KD * T + 384, 3, 2, CAP)
        selo2 = selo.rearrange("p c e s -> p c (e s)")
        Xe = part(gate_r, 0, KD, P)
        Xg = part(mix_r, SLOT, D)
        hs_ = part(gate_r, 1024, FE)
        act_e = part(gate_r, 1536, FE)
        actT = part(gate_r, 2048, FT, P)
        y_e = part(gate_r, 2560, D)
        pT = part(gate_r, 3584, T)
        tok_v, tok_rs, tok_t = (part(z_r, 40 * 3 * NE + 4 * k, 3) for k in range(3))
        r_ = part(z_r, 0, 40, 3 * NE)
        sq_fin = part(ring, 0, KD, T)
        score, sel, comb, posm, s_all = (r_[:, k, :].rearrange("p (c e) -> p c e", e=NE) for k in range(5))

        tiles = ([("u", j) for j in range(UT)] + [("x", j) for j in range(XT)]
                 + [("z", j) for j in range(KD)] + [("g", j) for j in range(2 * KD)])
        T_XBC, T_Z, NT = UT, UT + XT, len(tiles)

        def s5_steps(n):
            return [i for i in range(S5T) if (4 * i) // 3 == n]

        block = ctx.enter_context(nc.Block())

        @block.sync
        def _(sp):
            def weights(n):
                if n < 4:
                    return a["w_ada"][0, :, n * 512:(n + 1) * 512], KD
                if n < U_XBC:
                    return a["w_in"][0, :, IN_U:IN_U + 512], KD
                if n < U_Z:
                    return a["w_in"][0, :, IN_XBC + (n - U_XBC) * 512:IN_XBC + (n - U_XBC + 1) * 512], KD
                if n < U_GATE:
                    return a["w_in"][0, :, (n - U_Z) * 512:(n - U_Z + 1) * 512], KD
                if n < U_GLU:
                    return a["w_in"][0, :, IN_GATE + (n - U_GATE) * 512:IN_GATE + (n - U_GATE + 1) * 512], KD
                if n < U_ADA2:
                    return a["w_glu"][0, :, (n - U_GLU) * D:(n - U_GLU + 1) * D], UT
                if n < U_OUTA:
                    i = n - U_ADA2 + 4
                    return a["w_ada"][0, :, i * 512:(i + 1) * 512], KD
                if n < U_OUT:
                    return a["w_out_a"][0, :, (n - U_OUTA) * 512:(n - U_OUTA + 1) * 512], KD
                if n < U_ADA3:
                    return a["w_out"][0, :, (n - U_OUT) * 512:(n - U_OUT + 1) * 512], KD
                return a["w_ada"][0, :, 11 * 512:12 * 512], KD

            for n in range(N_UNITS):
                if n >= NR:
                    sp.wait_ge(unit_used, n - NR + 1)
                if n == 0:
                    sp.wait_ge(ld_c, 32)
                elif n == 1:
                    sp.wait_ge(ld_par, 16 * 10)
                src, k = weights(n)
                sp.dma_start(unit_tile(n, k), src.rearrange("(k p) n -> p k n", p=P)).then_inc(landed[n % NR], 16)

            def expert_tile(pair, parity, r):
                w, k = (("w1", KD), ("w3", KD), ("w2", FT))[r // 2]
                s = MOE_SLOTS[parity][r]
                src = a[w][0, bass.ds(2 * pair + r % 2, 1), :, :].rearrange("e (k p) n -> p (e k) n", p=P)
                sp.dma_start(ring_tile(s, k), src).then_inc(landed[s], 16)

            def pair_tile(v, pair, parity, r):
                sp.wait_ge(unit_used, N_UNITS + 6 * (v - (2 if r < ALTERNATE else 1)) + r + 1)
                expert_tile(pair, parity, r)

            def later_tiles(v0):
                def stage(p, parity):
                    for step, r in ((1, 0), (1, 1), (0, 3), (1, 2), (0, 4), (0, 5)):
                        pair_tile(v0 + p + step, p + step, (parity + step) % 2, r)

                with sp.Fori(0, PAIRS // 2 - 1) as h:
                    stage(2 * h + 1, 1)
                    stage(2 * h + 2, 0)
                for r in range(ALTERNATE, 6):
                    pair_tile(v0 + PAIRS - 1, PAIRS - 1, 1, r)

            for r in range(5):
                sp.wait_ge(unit_used, max(n for n in range(N_UNITS) if n % NR == MOE_SLOTS[0][r]) + 1)
                expert_tile(0, 0, r)
            sp.wait_ge(unit_used, U_OUT)
            sp.wait_ge(st_hp, 16)
            for b in range(NH0):
                sp.wait_ge(st_hs[b], 16 * len(range(b, KD, NH0)))
            expert_tile(0, 0, 5)
            expert_tile(1, 1, 0)
            expert_tile(1, 1, 1)
            sp.wait_ge(h2t_ps, 6)
            expert_tile(1, 1, 2)
            later_tiles(0)
            sp.wait_ge(route_ok, 1)
            passes = sp.value_load(npi[0:1, 0:1], min_val=1, max_val=MAXPASS)
            with sp.If(passes > 1):
                with sp.Fori(1, passes) as n:
                    for r in range(6):
                        pair_tile(n * PAIRS, 0, 0, r)
                    for r in range(ALTERNATE):
                        pair_tile(n * PAIRS + 1, 1, 1, r)
                    later_tiles(n * PAIRS)

            sp.wait_ge(fin_cp, 6)
            for i, (t0, n) in enumerate(CHUNKS[:2]):
                sp.dma_start(o["y_prompt"][0, t0:t0 + n, :], y_tok[0:n, i, :]).then_inc(st_y, 16)
            sp.dma_start(o["y_sample"].rearrange("b l d -> (b l) d"), y_tok[0:TS, 2, :]).then_inc(st_y, 16)
            sp.wait_ge(st_y, 48)
            sp.wait_ge(st_conv, 32)
            sp.wait_ge(st_s5, 64)

        @block.gpsimd
        def _(pool):
            link = linker(pool, pool_chain)
            g = nc.gpsimd

            def keep(out, in_, pattern, mult, base, op=ALU.is_ge):
                return g.affine_select(out=out, in_=in_, compare_op=op, fill=0.0, base=base,
                                       pattern=pattern, channel_multiplier=mult)

            link(g.memset(par8[:], 1.0))
            link(g.memset(strict[:], 1.0))
            link(g.memset(same_r[0:TS, :], 1.0))
            link(g.memset(blk[0:TS, :], 1.0))
            link(g.memset(ident[:], 0.0))
            g.affine_select(out=ident[:], in_=ident[:], compare_op=ALU.not_equal, fill=1.0, base=0,
                            pattern=[[-1, P]], channel_multiplier=1).then_inc(consts, 1)
            link(g.memset(upper[:], 1.0))
            keep(upper[:], upper[:], [[1, P]], -1, 0).then_inc(consts, 1)
            keep(strict[:], strict[:], [[1, P]], -1, -1).then_inc(consts, 1)
            same3 = sample(same_r[0:TS, :])
            link(keep(same3, same3, [[-LSAMP, NBATCH], [0, LSAMP]], 1, 0))
            link(keep(same3, same3, [[LSAMP, NBATCH], [0, LSAMP]], -1, LSAMP - 1))
            keep(supper_r[0:TS, :], same_r[0:TS, :], [[1, TS]], -1, 0).then_inc(consts, 1)
            link(keep(blk[0:TS, :], blk[0:TS, :], [[-LSAMP, NBATCH]], 1, 0))
            keep(blk[0:TS, :], blk[0:TS, :], [[LSAMP, NBATCH]], -1, LSAMP - 1).then_inc(consts, 1)
            p8 = par8[:].rearrange("p (q h) -> p q h", q=2)
            link(keep(p8, p8, [[-S5C, 2], [-2 * S5C, 4]], 1, 0))
            keep(p8, p8, [[S5C, 2], [2 * S5C, 4]], -1, S5C - 1).then_inc(consts, 1)
            g.iota(iota[:], [[1, CAP]], base=0, channel_multiplier=0,
                   allow_small_or_imprecise_dtypes=True).then_inc(consts, 1)
            g.iota(keyg[:], [[-1, NG]], base=NG, channel_multiplier=0,
                   allow_small_or_imprecise_dtypes=True).then_inc(consts, 1)
            g.iota(keye[:], [[-1, NE]], base=NE, channel_multiplier=0,
                   allow_small_or_imprecise_dtypes=True).then_inc(consts, 1)

            pool.wait_ge(rot_u, 1)
            wc, ws = [s5c[:, 0, :], s5c[:, 2, :]], [s5c[:, 1, :], s5c[:, 3, :]]
            link(g.memset(rotc[:, :, 0:1], 1.0))
            link(g.memset(rots[:, :, 0:1], 0.0))
            k, lv = 1, 0
            J = 64
            ta, tb = part(mix_r, off + 2048, S5T, J), part(mix_r, off + 3072, S5T, J)
            while k < TP:
                wcb = wc[lv % 2].unsqueeze(2)
                wsb = ws[lv % 2].unsqueeze(2)
                for j0 in range(0, k, J):
                    kk = min(k, J)
                    lo, hi = slice(j0, j0 + kk), slice(k + j0, k + j0 + kk)
                    bc = [P, S5T, kk]
                    A, B = ta[:, :, 0:kk], tb[:, :, 0:kk]
                    link(g.tensor_tensor(A, rotc[:, :, lo], wcb.to_broadcast(bc), ALU.mult))
                    link(g.tensor_tensor(B, rots[:, :, lo], wsb.to_broadcast(bc), ALU.mult))
                    link(g.tensor_tensor(rotc[:, :, hi], A, B, ALU.subtract))
                    link(g.tensor_tensor(A, rotc[:, :, lo], wsb.to_broadcast(bc), ALU.mult))
                    link(g.tensor_tensor(B, rots[:, :, lo], wcb.to_broadcast(bc), ALU.mult))
                    link(g.tensor_tensor(rots[:, :, hi], A, B, ALU.add))
                if 2 * k < TP:
                    c0, s0, c1, s1 = wc[lv % 2], ws[lv % 2], wc[(lv + 1) % 2], ws[(lv + 1) % 2]
                    t4 = s5c[:, 4, :]
                    link(g.tensor_tensor(c1, c0, c0, ALU.mult))
                    link(g.tensor_tensor(t4, s0, s0, ALU.mult))
                    link(g.tensor_tensor(c1, c1, t4, ALU.subtract))
                    link(g.tensor_tensor(s1, c0, s0, ALU.mult))
                    link(g.tensor_tensor(s1, s1, s1, ALU.add))
                k, lv = 2 * k, lv + 1
            g.tensor_copy(rotc[:, 0, 0:1], rotc[:, 0, 0:1]).then_inc(rot_ok, 1)

            for i in range(S5T):
                q = i % 2
                gr, gi, hr, hi = g5[:, 2 * q, :], g5[:, 2 * q + 1, :], h5[:, 2 * q, :], h5[:, 2 * q + 1, :]
                c_, s_ = rotc[:, i, :], rots[:, i, :]
                pool.wait_ge(s5_g, i + 1)
                if i >= 2:
                    pool.wait_ge(s5_hused, i - 1)
                link(g.tensor_tensor(pt[:, 0, :], gr, c_, ALU.mult))
                link(g.tensor_tensor(pt[:, 1, :], gi, s_, ALU.mult))
                link(g.tensor_tensor(hr, pt[:, 0, :], pt[:, 1, :], ALU.subtract))
                link(g.tensor_tensor(pt[:, 0, :], gr, s_, ALU.mult))
                link(g.tensor_tensor(pt[:, 1, :], gi, c_, ALU.mult))
                link(g.tensor_tensor(hi, pt[:, 0, :], pt[:, 1, :], ALU.add))
                link(g.tensor_copy(fin5[:, 0, i:i + 1], hr[:, TP - 1:TP]))
                g.tensor_copy(fin5[:, 1, i:i + 1], hi[:, TP - 1:TP]).then_inc(s5_h, 1)

            pool.wait_ge(dte_ok, 1)
            for i, (t0, n) in enumerate(CHUNKS):
                pool.wait_ge(xdt_ok, 2 * i + 2)
                g.tensor_tensor(Xs[0:n, i, :].rearrange("p (h d) -> p h d", d=HD),
                                Xdt[0:n, i, :].rearrange("p (h d) -> p h d", d=HD),
                                dte[0:n, i, :].unsqueeze(2).to_broadcast([n, H, HD]), ALU.mult).then_inc(xs_ok, 1)
            pool.wait_ge(bt_ok, 3)
            for gr in range(G):
                g.tensor_tensor(Bm[0:TS, gr, :].rearrange("p (b n) -> p b n", n=NS),
                                B_tok[0:TS, 2, gr * NS:(gr + 1) * NS].unsqueeze(1).to_broadcast([TS, NBATCH, NS]),
                                blk[0:TS, :].unsqueeze(2).to_broadcast([TS, NBATCH, NS]), ALU.mult).then_inc(bm_ok, 1)
            pool.wait_ge(q_yev, 4)
            pool.wait_ge(bm_ok, 2)
            link(g.tensor_tensor(sq_acc, zT[:, 0, :], zT[:, 0, :], ALU.mult))
            for j in range(1, 4):
                link(g.tensor_tensor(nv, zT[:, j, :], zT[:, j, :], ALU.mult))
                last = g.tensor_tensor(sq_acc, sq_acc, nv, ALU.add)
                if j < 3:
                    link(last)
            last.then_inc(xs_ok, 1)

        @block.tensor
        def _(pe):
            def mm(out, lhsT, rhs, first, last):
                return nc.tensor.matmul(out, lhsT, rhs, start=first, stop=last, skip_group_check=True)

            def tr(out, in_):
                return nc.tensor.transpose(out, in_, ident[0:in_.shape[0], 0:in_.shape[0]])

            def wait_unit(n):
                pe.wait_ge(landed[n % NR], 16 * (n // NR + 1))

            pe.wait_ge(consts, 9)
            pe.wait_ge(vconsts, 3)
            pe.wait_ge(c_silu, 1)
            for j in range(KD):
                last = tr(ps[:, 6, j * NC:(j + 1) * NC], c_in[0:NC, j * P:(j + 1) * P])
            last.then_inc(cT_ps, 1)

            def square_sum(bank, n, first, last):
                pe.wait_ge(sq_ok, n + 1)
                mm(ps[:, bank, 0:T], ones[:], sq[:, n % 2, :], first, last).then_inc(sq_used, 1)

            def square_sums(bank, tiles_, base):
                for j in range(tiles_):
                    square_sum(bank, base + j, j == 0, j == tiles_ - 1)

            pe.wait_ge(ld_x, 32)
            for j in range(KD):
                if j >= 2:
                    pe.wait_ge(x_ok, j - 1)
                for i, (t0, n) in enumerate(CHUNKS):
                    last = tr(ps[:, j % 2, t0:t0 + n], x_tok[0:n, i, j * P:(j + 1) * P])
                last.then_inc(x_ps, 1)
                if j:
                    square_sum(4, j - 1, j == 1, False)
            square_sum(4, KD - 1, False, True)

            pe.wait_ge(ld_par, 16 * 10)
            pe.wait_ge(expd, 2)
            tr(ps[:, 7, 0:104], prow1[0:104, :])
            tr(ps[:, 7, 128:208], prow2[0:80, :])
            tr(ps[:, 7, 256:272], prow3[0:16, :]).then_inc(par_ps, 1)

            def ada(i):
                n = ada_unit(i)
                w = unit_tile(n, KD)
                wait_unit(n)
                pe.wait_ge(cT_ok, 1)
                if i >= 2:
                    pe.wait_ge(ada_cp, i if i >= 4 else i - 1)
                for r in range(2):
                    for c in range(4):
                        last = mm(ps[32 * c:32 * c + 32, sums_bank(i), :], cT[:, 4 * r + c, :], w[:, 4 * r + c, :], r == 0, r == 1)
                last.then_inc(unit_used, 1)

            def ada_turn(i):
                pe.wait_ge(ada_cp, i + 1)
                if i >= 1:
                    pe.wait_ge(mod_ok, i)
                if i >= 4:
                    pe.wait_ge(yoff_ok, {4: 1, 5: 2, 6: 3, 7: 4, 8: 5, 9: 7}.get(i, KD))
                for c in range(4):
                    last = mm(turned(i, c, c + 1), ada_s[:, c * P:(c + 1) * P], sel9[:, 0:NC], c == 0, c == 3)
                last.then_inc(adaT_ps, 1)

            for i in range(4):
                ada(i)
                if i:
                    ada_turn(i - 1)
            ada_turn(3)

            def state_columns():
                pe.wait_ge(ld_state, 48)
                for q in range(2):
                    tr(ps[:, 2, q * P:(q + 1) * P], st_rows[:, q, :])
                for j in range(XT):
                    last = tr(ps[:, 3, j * 24:(j + 1) * 24], conv_in[0:24, j * P:(j + 1) * P])
                last.then_inc(cT_ps, 1)

            def tile(t):
                n = U_U + t // 4
                w = unit_tile(n, KD)
                wait_unit(n)
                if t >= 2:
                    pe.wait_ge(tile_ev, t - 1)
                for k in range(KD):
                    if t == 0:
                        pe.wait_ge(hp_ok, k + 1)
                        pe.wait_ge(h_ok, 1)
                    last = mm(ps[:, t % 2, 0:T], w[:, k, (t % 4) * P:(t % 4 + 1) * P], hT[:, k, :], k == 0, k == KD - 1)
                last.then_inc(tile_ps, 1)
                if t % 4 == 3:
                    pe.wait_ge(tile_ps, t + 1)
                    pe.nop().then_inc(unit_used, 1)

            for t in range(T_Z):
                if t == T_XBC:
                    state_columns()
                tile(t)
            pe.wait_ge(ld_wsm, 32)
            pe.wait_ge(par_ok, 2)
            for i, (t0, n) in enumerate(CHUNKS):
                for k in range(KD):
                    last = mm(ps[0:n, 2, i * H:(i + 1) * H], hT[:, k, t0:t0 + n], w_dt[:, k, :], k == 0, k == KD - 1)
            last.then_inc(dt_ps, 1)

            pe.wait_ge(blk5, 2)
            for q in range(2):
                for j in range(UT):
                    last = tr(ps[:, 3 + q, j * P:(j + 1) * P],
                              bblk[:, q, 4 * j:4 * j + 4, :].rearrange("p i c -> p (i c)"))
                last.then_inc(s5w_ps, 1)
            for q in range(2):
                for j in range(UT):
                    last = tr(ps[:, 5 + q, j * P:(j + 1) * P], cblk[:, q, j, :])
                last.then_inc(s5w_ps, 1)
            pe.wait_ge(s5w_ok, 2)
            pe.wait_ge(da_ok, 1)
            pe.wait_ge(conv_acc, XT)
            for j in range(XT):
                last = tr(ps[0:27, 2 + j // 4, (j % 4) * P:(j % 4 + 1) * P], tails[:, j, :])
            last.then_inc(tail_ps, 1)

            def s5_in(i):
                a_, r = i // 4, 32 * (i % 4)
                if i < 2:
                    pe.wait_ge(s5w_ok, 4)
                    pe.wait_ge(tail_cp, 1)
                    pe.wait_ge(tile_ev, UT)
                else:
                    pe.wait_ge(s5_xused, i - 1)
                for q in range(2):
                    last = mm(ps[:, 2 + 2 * (i % 2) + q, 0:T], bT[r:r + 32, q, a_, :], uT[r:r + 32, a_, :], True, True)
                last.then_inc(s5_x, 1)

            def s5_out(i):
                a_, r = i // 4, 32 * (i % 4)
                pe.wait_ge(s5_h, i + 1)
                if r == 0 and a_ >= 2:
                    pe.wait_ge(s5_yev, a_ - 1)
                for q in range(2):
                    last = mm(ps[r:r + 32, 6 + a_ % 2, 0:TP], cTs5[:, q, a_, r:r + 32], h5[:, 2 * (i % 2) + q, :], q == 0, q == 1)
                last.then_inc(s5_hused, 1)

            for t in range(T_Z, NT):
                for i in s5_steps(t - T_Z):
                    if i >= 2:
                        s5_out(i - 2)
                    s5_in(i)
                tile(t)
                if NT - 4 <= t < NT - 2:
                    s5_out(S5T - 2 + t - (NT - 4))
            pe.wait_ge(s5_hs, 1)
            for i in range(S5T):
                a_, r = i // 4, 32 * (i % 4)
                for q in range(2):
                    last = mm(ps[r:r + 32, 2, a_ * TS:(a_ + 1) * TS], cTs5[:, q, a_, r:r + 32], s5h[:, q, i, :], q == 0, q == 1)
            last.then_inc(s5_y, 1)
            for q in range(2):
                tr(ps[:, 3, q * P:(q + 1) * P], st5[:, q].rearrange("p b i -> p (b i)"))
                last = tr(ps[0:S5T, 3, 256 + q * P:256 + (q + 1) * P], fin5[:, q, :])
            last.then_inc(s5_y, 1)

            wait_unit(U_GLU)
            wait_unit(U_GLU + 1)
            wa, wb = unit_tile(U_GLU, UT), unit_tile(U_GLU + 1, UT)
            pe.wait_ge(s5f_cp, 1)
            pe.wait_ge(s5_yev, 5)
            pe.wait_ge(tile_ev, NT)

            def glu(j):
                if j:
                    pe.wait_ge(glu_ev, 2 * j - 1)
                for w, q in ((wb, 1), (wa, 0)):
                    for k in range(UT):
                        if j == 0 and q:
                            pe.wait_ge(gelu_ok, k + 1)
                        last = mm(ps[:, q, 0:T], w[:, k, j * P:(j + 1) * P], uT[:, k, :], k == 0, k == UT - 1)
                    last.then_inc(glu_ps, 1)

            def cb_and_sums():
                for i, (t0, n) in enumerate(CHUNKS):
                    for gr in range(G):
                        o_ = (i % 2) * 256 + gr * n
                        last = mm(ps[0:n, 4 + i // 2, o_:o_ + n], xbcT[:, KD + gr, t0:t0 + n], xbcT[:, KD + G + gr, t0:t0 + n], True, True)
                last.then_inc(cb_ps, 1)
                for i, (t0, n) in enumerate(CHUNKS):
                    up, on = (upper, ones) if i < 2 else (supper_r, same_r)
                    mm(ps[0:n, 5, 128 + 32 * i:144 + 32 * i], up[0:n, 0:n], da3[0:n, i, :], True, True)
                    mm(ps[0:n, 5, 144 + 32 * i:160 + 32 * i], on[0:n, 0:n], da3[0:n, i, :], True, True)
                for hp in range(KD):
                    for q in range(2):
                        last = mm(ps[64 * q:64 * q + HD, 5, 256 + hp * TS:256 + (hp + 1) * TS],
                                  da3[0:TS, 2, 2 * hp + q:2 * hp + q + 1].to_broadcast([TS, HD]), supper_r[0:TS, :], True, True)
                last.then_inc(acs_ps, 1)

            def token_major(i):
                t0, n = CHUNKS[i]
                if i >= 1:
                    pe.wait_ge(xdt_ok, 2 * i)
                    pe.wait_ge(bt_ok, i)
                for j in range(KD):
                    last = tr(ps[0:n, 6 + j // 4, (j % 4) * P:(j % 4 + 1) * P], xbcT[:, j, t0:t0 + n])
                for gr in range(G):
                    last = tr(ps[0:n, 2, gr * P:(gr + 1) * P], xbcT[:, KD + gr, t0:t0 + n])
                last.then_inc(xt_ps, 1)

            def chunk_states(i):
                pe.wait_ge(bt_ok, 3)
                pe.wait_ge(xs_ok, i + 1)
                if i:
                    pe.wait_ge(h1_ok, G)
                for gr in range(G):
                    last = mm(ps[:, 2 + gr, :], B_tok[:, i, gr * NS:(gr + 1) * NS], Xs[:, i, gr * 512:(gr + 1) * 512], True, True)
                last.then_inc(st_ps, 1)

            def sample_sums():
                pe.wait_ge(cb_ok, 3)
                for h in range(H):
                    last = mm(ps[0:TS, 4, h * TS:(h + 1) * TS], da3[0:TS, 2, h:h + 1].to_broadcast([TS, TS]), supper_r[0:TS, :], True, True)
                last.then_inc(qs_ps, 1)

            pe.wait_ge(conv_ok, 2 * XT)
            for j, step in enumerate((cb_and_sums, lambda: token_major(0), lambda: token_major(1), lambda: token_major(2),
                                      lambda: chunk_states(0), lambda: chunk_states(1), sample_sums, None)):
                glu(j)
                if step is not None:
                    step()
            for _ in range(2):
                pe.wait_ge(glu_ps, 2 * KD)
                pe.nop().then_inc(unit_used, 1)

            def h0_turn(hp):
                pe.wait_ge(ld_h0[hp % NH0], 16 * (hp // NH0 + 1))
                if hp:
                    pe.wait_ge(h0_cp, 2 * hp)
                else:
                    pe.wait_ge(hf_ok, G)
                for b in range(NBATCH):
                    last = tr(ps[:, 2 + b // 4, (b % 4) * P:(b % 4 + 1) * P], h0[hp % NH0][:, b, :])
                    if b % 4 == 3:
                        last.then_inc(h0_ps, 1)

            def sample_states(hp):
                if hp:
                    pe.wait_ge(ss_ok, hp)
                else:
                    pe.wait_ge(qs_diff, 1)
                    pe.wait_ge(acs_ok, 3)
                    pe.wait_ge(bm_ok, 2)
                    pe.wait_ge(xs_ok, 3)
                gr = hp // (KD // G)
                for q in range(2):
                    last = mm(ps[:, 4 + q, :], Xs[0:TS, 2, hp * P:(hp + 1) * P], Bm[0:TS, gr, q * 512:(q + 1) * 512], True, True)
                last.then_inc(ss_ps, 1)

            def sample_off(hp):
                gr = hp // (KD // G)
                pe.wait_ge(h0_cp, 2 * hp + 2)
                if hp:
                    pe.wait_ge(yoff_ok, hp)
                    pe.wait_ge(mod_ok, (4, 5, 6, 7, 8, 9, 9, 10)[hp])
                for b in range(NBATCH):
                    c, r = b % 4, b // 4
                    last = mm(ps[32 * c:32 * c + TS, 7, r * P:(r + 1) * P], xbcT[:, KD + G + gr, TP:T],
                              h0T[:, b * NS:(b + 1) * NS], True, True)
                last.then_inc(yo_ps, 1)

            def off_turn(hp):
                pe.wait_ge(yo_cp, hp + 1)
                for r in range(2):
                    last = tr(ps[:, 7, r * P:(r + 1) * P], yraw[:, r, :])
                last.then_inc(yoT_ps, 1)

            pe.wait_ge(glu_ev, 2 * KD)
            for qd in range(4):
                h0_turn(2 * qd)
                if qd:
                    pe.wait_ge(q_yev, 2 * qd)
                for i in range(2):
                    for h4 in range(4):
                        h = 4 * qd + h4
                        last = mm(ps[:, i, h4 * CH:(h4 + 1) * CH], da3[:, i, h:h + 1].to_broadcast([P, P]), upper[:, :], True, True)
                last.then_inc(q_ps, 1)
                ada(UNITS_OF[qd][0])
                sample_off(2 * qd)
                sample_states(2 * qd)
                h0_turn(2 * qd + 1)
                off_turn(2 * qd)
                ada_turn(UNITS_OF[qd][0])
                sample_off(2 * qd + 1)
                for u in UNITS_OF[qd][1:]:
                    ada(u)
                if qd == 3:
                    pe.wait_ge(xs_ok, 4)
                    pe.wait_ge(ada_cp, 10)
                    mm(ps[:, 6, 0:T], ones[:], sq_acc, True, True).then_inc(g0_ps, 1)
                sample_states(2 * qd + 1)
                off_turn(2 * qd + 1)
                pe.wait_ge(q_mt, 2 * (qd + 1))
                if qd == 0:
                    pe.wait_ge(qs_ok, 2)
                for h4 in range(4):
                    h = 4 * qd + h4
                    gr, j = h // (H // G), h // 2
                    out = ps[64 * (h % 2):64 * (h % 2) + HD, j % 2, :]
                    xh = slice(h * HD, (h + 1) * HD)
                    mm(out[:, 0:CH], Xdt[:, 0, xh], MT[:, h4, 0:CH], True, True)
                    mm(out[:, CH:TP], Xdt[:, 1, xh], MT[:, h4, CH:TP], True, False)
                    mm(out[:, CH:TP], h1T[:, gr, (h % 8) * HD:(h % 8 + 1) * HD], CTs[:, h4, :], False, True)
                    last = mm(out[:, TP:T], Xdt[0:TS, 2, xh], MTs[0:TS, h, :], True, True)
                    if h4 % 2 == 1:
                        last.then_inc(q_y, 1)
                for u in UNITS_OF[qd][1:]:
                    ada_turn(u)
            pe.wait_ge(h0_cp, 2 * KD)
            for j in range(KD):
                last = tr(ps[:, 2 + j // 4, (j % 4) * P:(j % 4 + 1) * P], hfT[:, j // 4, (j % 4) * P:(j % 4 + 1) * P])
            last.then_inc(hf_ps, 1)
            pe.wait_ge(ss_ok, KD)
            square_sums(5, 4, 8)

            def project(unit0, bank, src, banks_ps, freed, src_ok, after=None):
                for j in range(KD):
                    n = unit0 + j // 4
                    wait_unit(n)
                    w = unit_tile(n, KD)
                    if j >= 2:
                        pe.wait_ge(freed, j - 1)
                    for k in range(KD):
                        if j == 0:
                            pe.wait_ge(src_ok, k + 1)
                        last = mm(ps[:, bank + j % 2, 0:T], w[:, k, (j % 4) * P:(j % 4 + 1) * P], src[:, k, :], k == 0, k == KD - 1)
                    last.then_inc(banks_ps, 1)
                    if j % 4 == 3:
                        pe.wait_ge(banks_ps, j + 1)
                        pe.nop().then_inc(unit_used, 1)
                    if after is not None:
                        after(j)

            def residual_square(j):
                if j >= 2:
                    square_sum(4, 12 + j - 2, j == 2, False)

            ada(10)
            project(U_OUTA, 0, zT, outa_ps, mrg_ok, yn_ok, lambda j: ada_turn(10) if j == 0 else None)
            pe.wait_ge(hf_cp, 1)
            project(U_OUT, 2, gates, mix_ps, x1_ok, mrg_ok, residual_square)
            square_sum(4, 18, False, False)
            square_sum(4, 19, False, True)
            ada(11)
            pe.wait_ge(ld_wsm, 32)

            def scores(k, i):
                t0, n = CHUNKS[i]
                return mm(ps[0:n, 6, i * NE:(i + 1) * NE], hT[:, k, t0:t0 + n], w_rt[:, k, :], k == i == 0, k == KD - 1)

            for k in range(KD):
                pe.wait_ge(hp_ok, KD + k + 1)
                scores(k, 0)
                scores(k, 1)
            pe.wait_ge(h_ok, 2)
            for k in range(KD):
                last = scores(k, 2)
            last.then_inc(lg_ps, 1)
            ada_turn(11)
            for q in range(2):
                for i, (t0, n) in enumerate(CHUNKS):
                    for j in range(4 * q, 4 * q + 4):
                        last = tr(ps[0:n, 3 * q + i, (j % 4) * P:(j % 4 + 1) * P], hT[:, j, t0:t0 + n])
                    last.then_inc(h2t_ps, 1)
            pe.wait_ge(top_ok, 1)
            pe.wait_ge(mod_ok, 12)
            for i, (t0, n) in enumerate(CHUNKS):
                for i2 in range(i + 1):
                    m = CHUNKS[i2][1]
                    mm(ps[0:n, 7, i * NE:(i + 1) * NE], (strict if i2 == i else ones)[0:m, 0:n], s_all[0:m, i2, :], i2 == 0, i2 == i)
            for i, (t0, n) in enumerate(CHUNKS):
                last = mm(ps[:, 7, 48:64], ones[0:n, :], s_all[0:n, i, :], i == 0, i == 2)
            last.then_inc(pos_ps, 1)

            def ring_wait(v, r, half):
                s = MOE_SLOTS[half[1]][r]
                base = uses(s) if s < NR else 0
                pe.wait_ge(landed[s], (half[0] + (base + 1)) * 16 if r < ALTERNATE else (v + (base + 1)) * 16)

            def gather(v, half):
                if half == 0:
                    pe.wait_ge(selo_ok, v + 1)
                for i, (t0, n) in enumerate(CHUNKS):
                    last = mm(ps[:, half, :], selo2[0:n, i, :], h2_tok[0:n, i, half * 512:(half + 1) * 512], i == 0, i == 2)
                last.then_inc(xg_ps[half], 1)

            def gathered_turn(v):
                pe.wait_ge(xg_cp, 2 * v + 2)
                for j in range(KD):
                    last = tr(ps[:, j // 4, (j % 4) * P:(j % 4 + 1) * P], Xg[:, j * P:(j + 1) * P])
                    if j % 4 == 3:
                        last.then_inc(xe_ps, 1)

            def combine(v):
                pe.wait_ge(ye_ok, 2 * v + 2)
                pe.wait_ge(pT_ok, v + 1)
                for j in range(KD):
                    if j >= 4:
                        pe.wait_ge(cmb_ok, 8 * v + 8 + j - 3)
                    mm(ps[:, CMB_BANKS[j % 4], 0:T], y_e[:, j * P:(j + 1) * P], pT[:, :], True, True).then_inc(cmb_ps, 1)

            def up(v, wi, half):
                ring_wait(v, 2 * wi, half)
                ring_wait(v, 2 * wi + 1, half)
                for k in range(KD):
                    for e in range(2):
                        w = ring_tile(MOE_SLOTS[half[1]][2 * wi + e], KD)
                        last = mm(ps[64 * e:64 * e + 64, 2 + wi, :], Xe[:, k, 64 * e:64 * e + 64], w[:, k, :], k == 0, k == KD - 1)
                        if k == KD - 1:
                            last.then_inc(unit_used, 1)

            def experts(v, half, prev, following):
                pe.wait_ge(xe_ok, 2 * v + 2)
                up(v, 0, half)
                if prev:
                    combine(v - 1)
                up(v, 1, half)
                if prev:
                    pe.wait_ge(cmb_ok, 8 * v + 8)
                if following:
                    gather(v + 1, 0)
                pe.wait_ge(selw_ok, v + 1)
                for i, (t0, n) in enumerate(CHUNKS):
                    last = tr(ps[:, 7, t0:t0 + n], selw2[0:n, i, :])
                last.then_inc(pT_ps, 1)
                pe.wait_ge(act_ok, v + 1)
                for f in range(FT):
                    last = tr(ps[:, 4, f * P:(f + 1) * P], act_e[:, f * P:(f + 1) * P])
                last.then_inc(aT_ps, 1)
                if following:
                    gather(v + 1, 1)
                pe.wait_ge(aT_ok, v + 1)
                ring_wait(v, 4, half)
                ring_wait(v, 5, half)
                for nh in range(2):
                    for f in range(FT):
                        for e in range(2):
                            w = ring_tile(MOE_SLOTS[half[1]][4 + e], FT)
                            last = mm(ps[64 * e:64 * e + 64, 5 + nh, :], actT[:, f, 64 * e:64 * e + 64], w[:, f, nh * 512:(nh + 1) * 512], f == 0, f == FT - 1)
                            if nh == 1 and f == FT - 1:
                                last.then_inc(unit_used, 1)
                    if nh == 0:
                        last.then_inc(w2_ps, 1)
                        if following:
                            gathered_turn(v + 1)

            pe.wait_ge(h2t_ok, 3)
            gather(0, 0)
            pe.wait_ge(h2t_ok, 6)
            gather(0, 1)
            gathered_turn(0)
            experts(0, (0, 0), False, True)
            with pe.Fori(0, PAIRS // 2 - 1) as h:
                experts(2 * h + 1, (h, 1), True, True)
                experts(2 * h + 2, (h + 1, 0), True, True)
            experts(PAIRS - 1, (PAIRS // 2 - 1, 1), True, False)
            combine(PAIRS - 1)
            pe.wait_ge(route_ok, 1)
            passes = pe.value_load(npi[0:1, 0:1], min_val=1, max_val=MAXPASS)
            with pe.If(passes > 1):
                with pe.Fori(1, passes) as n:
                    v0 = n * PAIRS
                    gather(v0, 0)
                    gather(v0, 1)
                    gathered_turn(v0)
                    half0 = n * (PAIRS // 2)
                    experts(v0, (half0, 0), False, True)
                    with pe.Fori(0, PAIRS // 2 - 1) as h:
                        v = n * PAIRS + 2 * h
                        hv = n * (PAIRS // 2) + h
                        experts(v + 1, (hv, 1), True, True)
                        experts(v + 2, (hv + 1, 0), True, True)
                    experts(v0 + (PAIRS - 1), (half0 + (PAIRS // 2 - 1), 1), True, False)
                    combine(v0 + (PAIRS - 1))

            for j in range(KD):
                pe.wait_ge(fin_ok, j + 1)
                for i, (t0, n) in enumerate(CHUNKS):
                    last = tr(ps[0:n, 2 * i + j // 4, (j % 4) * P:(j % 4 + 1) * P], hT[:, j, t0:t0 + n])
                if j % 4 == 3:
                    last.then_inc(fin_ps, 1)
            pe.wait_ge(sq_ok, 20 + KD + 1)
            for i, (t0, n) in enumerate(CHUNKS):
                last = mm(ps[0:n, 6, 2 * i:2 * i + 1], sq_fin[:, 0, t0:t0 + n], ones[:, 0:1], True, True)
            last.then_inc(sq_used, 1)

        @block.scalar
        def _(act):
            link = linker(act, act_chain)

            def f(out, in_, func=ACT.Copy, **kw):
                return nc.scalar.activation(out, in_, func, **kw)

            def load(out, in_, s):
                act.dma_start(out, in_).then_inc(s, 16)

            load(c_in[0:1, :], a["c_prompt"], ld_c)
            load(c_in[1:NC, :], a["c_sample"], ld_c)
            load(x_tok[:, 0:2, :], a["x_prompt"][0].rearrange("(i p) d -> p i d", p=P), ld_x)
            load(x_tok[0:TS, 2, :], a["x_sample"].rearrange("b l d -> (b l) d"), ld_x)
            with nc.allow_non_contiguous_dma(reason="a value or a short run per descriptor, a few KiB in all"):
                load(exp_in[96:104, 0:2], a["d_ssd"][0].rearrange("(j q) -> j q", q=2), ld_exp)
                load(exp_in[0:S5T, 2:4], a["s5_log_dt"][0].rearrange("(j q) -> j q", q=2), ld_exp)
            r0 = 0
            for name, n in (("norm1_w", 8), ("norm2_w", 8), ("ssd_norm_w", 8), ("conv_w", 48), ("conv_b", 12), ("s5_d", 4)):
                v = a[name][0]
                v = v.rearrange("k (j p) -> (k j) p", p=P) if name == "conv_w" else v.rearrange("(j p) -> j p", p=P)
                load(prow1[r0:r0 + n, :], v, ld_par)
                r0 += n
            load(prow1[r0:r0 + 8, :], a["final_norm_w"].rearrange("(j p) -> j p", p=P), ld_par)
            load(prow2[0:48, :], a["b_ada"][0].rearrange("(j p) -> j p", p=P), ld_par)
            load(prow2[48:64, :], a["s5_a_re"][0].rearrange("(i q) s -> i (q s)", q=2), ld_par)
            load(prow2[64:80, :], a["s5_a_im"][0].rearrange("(i q) s -> i (q s)", q=2), ld_par)
            act.wait_ge(ld_c, 32)
            f(c_in[0:NC, :], c_in[0:NC, :], ACT.Silu).then_inc(c_silu, 1)

            n_sq = [0]

            def square(src):
                q = n_sq[0]
                if q >= 2:
                    act.wait_ge(sq_used, q - 1)
                f(sq[:, q % 2, :], src, ACT.Square).then_inc(sq_ok, 1)
                n_sq[0] += 1

            for j in range(KD):
                act.wait_ge(x_ps, j + 1)
                f(xT[:, j, :], ps[:, j % 2, 0:T]).then_inc(x_ok, 1)
                act.wait_ge(x_ok, j + 1)
                square(xT[:, j, :])

            n_rs = [0]

            def rsqrt(v, y):
                n_rs[0] += 1
                act.wait_ge(var_ok, n_rs[0])
                link(f(y, v, ACT.Ln))
                f(y, y, ACT.Exp, scale=-0.5).then_inc(rs_ok, 1)

            rsqrt(n1v, n1y)
            for q, name in enumerate(("state_s5_re", "state_s5_im")):
                load(st_rows[:, q, :], a[name][0].rearrange("b (i q) s -> (b i) (q s)", q=2), ld_state)
            load(conv_in[0:24, :], a["state_conv"][0].rearrange("b k f -> (b k) f"), ld_state)
            for name, t_ in (("dt_bias", dtb), ("a_log", alog)):
                load(t_[:, :], a[name].to_broadcast([P, H]), ld_bc)
            load(brt[:, :], a["b_router"].unsqueeze(0).to_broadcast([P, NE]), ld_bc)
            for q, name in enumerate(("s5_b_re", "s5_b_im")):
                for gg in range(2):
                    load(b_raw[64 * gg:64 * gg + 64, q, :, :],
                         a[name][0].rearrange("(i q) s c -> q s i c", q=2)[gg], ld_rows)
            for q, name in enumerate(("s5_c_re", "s5_c_im")):
                load(c_raw[:, q, :, :], a[name][0].rearrange("(j g) c s -> (g c) j s", j=UT), ld_rows)
            load(w_dt[:, :, :], a["w_in"][0, :, IN_DT:IN_DT + H].rearrange("(k p) n -> p k n", p=P), ld_wsm)
            load(w_rt[:, :, :], a["w_router"].rearrange("(k p) n -> p k n", p=P), ld_wsm)

            n_mod = [0]

            def modulate(sh):
                n_mod[0] += 1
                act.wait_ge(amul_ok, n_mod[0])
                for j in range(KD):
                    act.wait_ge(xn_ok, (n_mod[0] - 1) * KD + j + 1)
                    f(hT[:, j, 0:TP], hT[:, j, 0:TP], ACT.Identity, scale=amul[:, j, 0:1], bias=mod[:, sh + j, 0:1]).then_inc(hp_ok, 1)

            modulate(0)
            act.wait_ge(par_ok, 1)
            f(s5c[:, 5, :], pc3[:, :], ACT.Exp).then_inc(trig, 1)
            act.wait_ge(dsc, 1)
            f(s5c[:, 6, :], s5c[:, 6, :], ACT.Exp).then_inc(trig, 1)
            f(s5c[:, 11, :], s5c[:, 8, :], ACT.Sin).then_inc(trig, 1)
            f(s5c[:, 10, :], s5c[:, 9, :], ACT.Sin).then_inc(trig, 1)

            def conv_silu(j):
                act.wait_ge(conv_acc, j + 1)
                acc = part(z_r, (j % 2) * 312, 312)
                f(xbcT[:, j, 0:TP], acc[:, 0:TP], ACT.Silu).then_inc(conv_ok, 1)
                f(sample(xbcT[:, j, TP:T]), rows_sample(acc)[:, :, 0:LSAMP], ACT.Silu).then_inc(conv_ok, 1)

            def rows_sample(v):
                n = v.shape[-1] - 259
                if n == 56:
                    return v[:, 259:315].rearrange("p (b l) -> p b l", l=7)
                return bass.AP(v.tensor, v.offset + 259, [list(v.ap[0]), [7, NBATCH], [1, LSAMP]])

            for t, (kind, j) in enumerate(tiles[:T_Z]):
                if kind == "x" and j >= 2:
                    conv_silu(j - 2)
                act.wait_ge(tile_ps, t + 1)
                if kind == "u":
                    f(uT[:, j, :], ps[:, t % 2, 0:T]).then_inc(tile_ev, 1)
                else:
                    if j == 0:
                        act.wait_ge(sq_used, KD)
                    row = rows[:, j % 2, :]
                    link(f(row[:, 3:3 + TP], ps[:, t % 2, 0:TP]))
                    f(rows_sample(row)[:, :, 3:7], sample(ps[:, t % 2, TP:T])).then_inc(tile_ev, 1)
            conv_silu(XT - 2)
            conv_silu(XT - 1)
            act.wait_ge(ld_bc, 48)
            link(f(alog[:, :], alog[:, :], ACT.Exp))
            act.wait_ge(dt_pre, 1)
            link(f(dtt[:, :, :], dt3[:, :, :], ACT.Abs))
            link(f(dtt[:, :, :], dtt[:, :, :], ACT.Exp, scale=-1.0))
            f(dtt[:, :, :], dtt[:, :, :], ACT.Ln, bias=1.0).then_inc(dt_exp, 1)
            act.wait_ge(tail_ps, 1)
            ctail = part(gate_r, 8 * T, XBC)
            f(ctail[0:27, :].rearrange("p (a b) -> p a b", b=512), ps[0:27, 2:5, :]).then_inc(tail_cp, 1)
            act.wait_ge(tail_cp, 1)
            act.dma_start(o["conv_prompt"][0, 0], ctail[0:3, :]).then_inc(st_conv, 16)
            act.dma_start(o["conv_sample"][0].rearrange("b k f -> (b k) f"), ctail[3:27, :]).then_inc(st_conv, 16)

            for t, (kind, j) in enumerate(tiles):
                if t < T_Z:
                    continue
                act.wait_ge(tile_ps, t + 1)
                if kind == "z":
                    f(zT[:, j, :], ps[:, t % 2, 0:T], ACT.Silu).then_inc(tile_ev, 1)
                else:
                    if j == KD:
                        act.wait_ge(st_conv, 32)
                    f(gates[:, j, :], ps[:, t % 2, 0:T], ACT.Sigmoid).then_inc(tile_ev, 1)

            act.wait_ge(s5_yev, 5)
            for j in range(UT):
                f(uT[:, j, :], uT[:, j, :], ACT.Gelu_apprx_tanh).then_inc(gelu_ok, 1)
            act.wait_ge(s5_y, 2)
            link(f(ada_s[:, 0:256], ps[:, 3, 0:256]))
            f(ada_s[0:S5T, 256:512], ps[0:S5T, 3, 256:512]).then_inc(s5f_cp, 1)
            act.wait_ge(s5f_cp, 1)
            for q, (ns, npr) in enumerate((("s5_re_sample", "s5_re_prompt"), ("s5_im_sample", "s5_im_prompt"))):
                act.dma_start(o[ns][0].rearrange("b (i q) s -> (b i) (q s)", q=2), ada_s[:, q * P:(q + 1) * P]).then_inc(st_s5, 16)
                act.dma_start(o[npr][0, 0].rearrange("(i q) s -> i (q s)", q=2),
                              ada_s[0:S5T, 256 + q * P:256 + (q + 1) * P]).then_inc(st_s5, 16)
            h0_src = a["state_ssm"][0].rearrange("b (j q) p n -> j (q p) b n", q=2)
            h0_dst = o["ssm_sample"][0].rearrange("b (j q) p n -> j (q p) b n", q=2)

            for hp in range(NH0):
                act.dma_start(h0[hp], h0_src[hp]).then_inc(ld_h0[hp], 16)

            def glu_gate(j):
                act.wait_ge(glu_ps, 2 * j + 1)
                if j >= 2:
                    act.wait_ge(glu_ev, 2 * j - 2)
                f(sq[:, j % 2, :], ps[:, 1, 0:T], ACT.Sigmoid).then_inc(glu_sig, 1)

            glu_gate(0)
            glu_gate(1)
            act.wait_ge(acs_ok, 2)
            f(eft[:, :, :].rearrange("p j t -> p (j t)"), ps[:, 5, 256:512], ACT.Exp).then_inc(acs_ok, 1)
            act.wait_ge(dte_pre, 1)
            link(f(dte[:, 0:2, :], dte[:, 0:2, :], ACT.Exp))
            link(f(dte[0:TS, 2, :], dte[0:TS, 2, :], ACT.Exp))
            f(acs[:, 1, H:2 * H], acs[:, 1, H:2 * H], ACT.Exp).then_inc(dte_ok, 1)
            for i, (t0, n) in enumerate(CHUNKS):
                act.wait_ge(xt_ps, i + 1)
                f(B_tok[0:n, i, :], ps[0:n, 2, 0:2 * NS]).then_inc(bt_ok, 1)
                glu_gate(2 + i)
            act.wait_ge(st_ps, 1)
            for gr in range(G):
                f(h1T[:, gr, :], ps[:, 2 + gr, :]).then_inc(h1_ok, 1)
            for j in range(5, KD):
                glu_gate(j)

            def h0_copies(hp):
                for q in range(2):
                    act.wait_ge(h0_ps, 2 * hp + q + 1)
                    if hp:
                        act.wait_ge(yo_ps, hp)
                    f(h0T[:, q * 512:(q + 1) * 512], ps[:, 2 + q, :]).then_inc(h0_cp, 1)

            def off_copy(hp):
                act.wait_ge(yo_ps, hp + 1)
                f(yraw[:, :, :], ps[:, 7, 0:2 * P].rearrange("p (r f) -> p r f", r=2)).then_inc(yo_cp, 1)
                if hp >= 1:
                    store_states(hp - 1)
                if 2 <= hp < KD - 2:
                    b = (hp + 2) % NH0
                    act.wait_ge(st_hs[b], 16 * ((hp + 2) // NH0))
                    act.dma_start(h0[b], h0_src[hp + 2]).then_inc(ld_h0[b], 16)

            def store_states(hp):
                act.wait_ge(ss_ok, hp + 1)
                act.dma_start(h0_dst[hp], h0[hp % NH0]).then_inc(st_hs[hp % NH0], 16)

            act.wait_ge(qs_msk, 1)
            f(MTs[0:TS], MTs[0:TS], ACT.Exp).then_inc(qs_exp, 1)
            for qd in range(4):
                h0_copies(2 * qd)
                act.wait_ge(q_diff, qd + 1)
                if qd:
                    act.wait_ge(q_y, 2 * qd)
                f(CTs[:, :, :].rearrange("p h q -> p (h q)"), ps[:, 1, :], ACT.Exp).then_inc(q_exp, 1)
                act.wait_ge(q_msk, qd + 1)
                f(MT, MT, ACT.Exp).then_inc(q_exp, 1)
                off_copy(2 * qd)
                h0_copies(2 * qd + 1)
                if qd == 3:
                    act.wait_ge(q_yev, 6)
                    square(zT[:, 4, :])
                    square(zT[:, 5, :])
                    rsqrt(nv, ny)
                off_copy(2 * qd + 1)
            store_states(KD - 1)
            for j in (6, 7):
                act.wait_ge(q_yev, j + 1)
                square(zT[:, j, :])
            rsqrt(nv, ny)
            act.wait_ge(hf_ps, 1)
            f(h_out[:, :, :].rearrange("p (a j) n -> p a (j n)", a=2), ps[:, 2:4, :]).then_inc(hf_cp, 1)
            act.wait_ge(hf_cp, 1)
            act.dma_start(o["ssm_prompt"][0, 0].rearrange("(j q) p n -> (q p) j n", q=2), h_out).then_inc(st_hp, 16)
            for j in range(KD):
                act.wait_ge(x1_ok, j + 1)
                square(xT[:, j, :])
            rsqrt(nv, ny)
            modulate(24)
            act.wait_ge(sm_in, 1)
            f(score, score, ACT.Exp).then_inc(sm_exp, 1)
            for q in range(2):
                for i, (t0, n) in enumerate(CHUNKS):
                    act.wait_ge(h2t_ps, 3 * q + i + 1)
                    f(h2_tok[0:n, i, q * 512:(q + 1) * 512], ps[0:n, 3 * q + i, :]).then_inc(h2t_ok, 1)

            def gathered_half(v):
                act.wait_ge(xg_ps[1], v + 1)
                f(Xg[:, 512:D], ps[:, 1, :]).then_inc(xg_cp, 1)

            def tokens_in(v):
                for half in range(2):
                    act.wait_ge(xe_ps, 2 * v + half + 1)
                    f(Xe[:, 4 * half:4 * half + 4, :].rearrange("p j s -> p (j s)"), ps[:, half, :]).then_inc(xe_ok, 1)

            def experts(v, prev, following):
                act.wait_ge(unit_used, N_UNITS + 6 * v + 2)
                if prev:
                    act.wait_ge(act_ok, v)
                f(hs_[:, :], ps[:, 2, :], ACT.Silu).then_inc(act_s, 1)
                act.wait_ge(aT_ps, v + 1)
                f(actT[:, :, :].rearrange("p f s -> p (f s)"), ps[:, 4, :]).then_inc(aT_ok, 1)
                if following:
                    gathered_half(v + 1)
                act.wait_ge(w2_ps, v + 1)
                f(y_e[:, 0:512], ps[:, 5, :]).then_inc(ye_ok, 1)
                if following:
                    tokens_in(v + 1)
                act.wait_ge(unit_used, N_UNITS + 6 * v + 6)
                f(y_e[:, 512:D], ps[:, 6, :]).then_inc(ye_ok, 1)

            gathered_half(0)
            tokens_in(0)
            experts(0, False, True)
            with act.Fori(1, PAIRS - 1) as q:
                experts(q, True, True)
            experts(PAIRS - 1, True, False)
            act.wait_ge(route_ok, 1)
            passes = act.value_load(npi[0:1, 0:1], min_val=1, max_val=MAXPASS)
            with act.If(passes > 1):
                with act.Fori(1, passes) as n:
                    v0 = n * PAIRS
                    gathered_half(v0)
                    tokens_in(v0)
                    experts(v0, True, True)
                    with act.Fori(1, PAIRS - 1) as q:
                        experts(n * PAIRS + q, True, True)
                    experts(v0 + (PAIRS - 1), True, False)
            for j in range(KD):
                act.wait_ge(x2_ok, j + 1)
                f(hT[:, j, :], xT[:, j, :], ACT.Copy, scale=fnw[:, j:j + 1]).then_inc(fin_ok, 1)
                f(sq_fin[:, j, :], xT[:, j, :], ACT.Square).then_inc(sq_ok, 1)
            rsqrt(tok_v, tok_rs)
            act.wait_ge(fin_rs, 1)
            act.wait_ge(fin_ps, 2)
            for i, (t0, n) in enumerate(CHUNKS):
                f(y_tok[0:n, i, 0:512], ps[0:n, 2 * i, :], ACT.Copy, scale=tok_rs[0:n, i:i + 1]).then_inc(fin_cp, 1)

        @block.vector
        def _(dve):
            link = linker(dve, dve_chain)
            v = nc.vector

            def tt(out, x, y, op):
                return v.tensor_tensor(out, x, y, op)

            def ts(out, x, s1, s2, op0, op1=None):
                return v.tensor_scalar(out, x, s1, s2, op0, op1) if op1 is not None else v.tensor_scalar(out, x, s1, s2, op0)

            def stt(out, x, s, y, op0, op1):
                return v.scalar_tensor_tensor(out=out, in0=x, scalar=s, in1=y, op0=op0, op1=op1)

            v.memset(ones[:], 1.0).then_inc(vconsts, 1)
            link(v.memset(cT, 0.0))
            link(v.memset(bblk, 0.0))
            dve.wait_ge(consts, 9)
            for c in range(4):
                last = v.tensor_copy(sel9[32 * c:32 * c + 32, :], ident[32 * c:32 * c + 32, 32 * c:32 * c + 32])
            last.then_inc(vconsts, 1)
            v.tensor_reduce(par2[:], par8[:].rearrange("p (q h) -> p q h", q=2), AX_X, ALU.add).then_inc(vconsts, 1)
            dve.wait_ge(vconsts, 3)
            dve.wait_ge(cT_ps, 1)
            v.tensor_copy(cT[:, :, 0:NC], ps[:, 6, 0:KD * NC].rearrange("p (k c) -> p k c", c=NC)).then_inc(cT_ok, 1)
            dve.wait_ge(ld_exp, 32)
            v.tensor_copy(prow1[96:104, :].rearrange("p (q s) -> p q s", q=2),
                          exp_in[96:104, 0:2].unsqueeze(2).to_broadcast([8, 2, 64])).then_inc(expd, 1)
            v.tensor_copy(prow3[0:S5T, :].rearrange("p (q s) -> p q s", q=2),
                          exp_in[0:S5T, 2:4].unsqueeze(2).to_broadcast([S5T, 2, 64])).then_inc(expd, 1)
            dve.wait_ge(par_ps, 1)
            link(v.tensor_copy(pc1[:, :], ps[:, 7, 0:104]))
            link(v.tensor_copy(pc2[:, :], ps[:, 7, 128:208]))
            v.tensor_copy(pc3[:, :], ps[:, 7, 256:272]).then_inc(par_ok, 1)

            def norm_var(bank, width, vv):
                ts(vv, ps[:, bank, 0:T], 1.0 / width, EPS, ALU.mult, ALU.add).then_inc(var_ok, 1)

            def norm_refine(vv, y, t, n):
                dve.wait_ge(rs_ok, n)
                link(tt(t, vv, y, ALU.mult))
                link(tt(t, t, y, ALU.mult))
                link(ts(t, t, -0.5, 1.5, ALU.mult, ALU.add))
                link(tt(y, y, t, ALU.mult))

            def norm_scale(bank, count, width, vv, y, t, n):
                dve.wait_ge(sq_used, count)
                norm_var(bank, width, vv)
                norm_refine(vv, y, t, n)

            def ada_copy(i):
                dve.wait_ge(unit_used, ada_unit(i) + 1)
                if i >= 1:
                    dve.wait_ge(adaT_ps, i)
                if i == 4:
                    dve.wait_ge(st_s5, 64)
                v.tensor_copy(ada_s[:, :], ps[:, sums_bank(i), :]).then_inc(ada_cp, 1)

            def ada_add(i):
                dve.wait_ge(adaT_ps, i + 1)
                tt(mod[:, 4 * i:4 * i + 4, :], turned(i, 0, 4).rearrange("p (k c) -> p k c", c=NC),
                   b_ada[:, 4 * i:4 * i + 4].unsqueeze(2).to_broadcast([P, 4, NC]), ALU.add).then_inc(mod_ok, 1)

            def per_sequence(col):
                return col.unsqueeze(2).to_broadcast([P, NBATCH, LSAMP])

            def normalize(y):
                for j in range(KD):
                    tt(hT[:, j, :], xT[:, j, :], y, ALU.mult).then_inc(xn_ok, 1)

            def scales(nw, sc):
                stt(amul, mod[:, sc:sc + KD, :], 1.0, nw.unsqueeze(2).to_broadcast([P, KD, NC]), ALU.add, ALU.mult).then_inc(amul_ok, 1)

            def modulate(sh, n):
                dve.wait_ge(amul_ok, n)
                dve.wait_ge(xn_ok, n * KD)
                hs = hT[:, :, TP:T].rearrange("p j (b l) -> p j b l", l=LSAMP)
                m4 = [P, KD, NBATCH, LSAMP]
                link(tt(hs, hs, amul[:, :, 1:NC].unsqueeze(3).to_broadcast(m4), ALU.mult))
                tt(hs, hs, mod[:, sh:sh + KD, 1:NC].unsqueeze(3).to_broadcast(m4), ALU.add).then_inc(h_ok, 1)

            norm_scale(4, KD, D, n1v, n1y, n1t, 1)
            ada_copy(0)
            normalize(n1y)
            for i in range(1, 4):
                ada_copy(i)
                ada_add(i - 1)
            ada_add(3)
            dve.wait_ge(mod_ok, 4)
            scales(nw1, 8)
            modulate(0, 1)

            C = [s5c[:, k, :] for k in range(24)]
            dt_, mag, th, r, r2, co, si, abr, abi, den, fre, fim = C[5], C[6], C[7], C[8], C[9], C[10], C[11], C[12], C[13], C[14], C[15], C[16]
            t0_, t1_, am1 = C[17], C[18], C[21]
            dve.wait_ge(trig, 1)
            link(tt(mag, dt_, a_re, ALU.mult))
            link(tt(th, dt_, a_im, ALU.mult))
            link(ts(t0_, th, 1.0 / TWO_PI, ROUND, ALU.mult, ALU.add))
            link(ts(t0_, t0_, -ROUND, None, ALU.add))
            link(stt(r, t0_, -TWO_PI_HI, th, ALU.mult, ALU.add))
            link(stt(r, t0_, -(TWO_PI - TWO_PI_HI), r, ALU.mult, ALU.add))
            link(ts(r, r, PI_IN, -PI_IN, ALU.min, ALU.max))
            link(ts(t1_, r, TWO_PI / 4, -TWO_PI, ALU.is_gt, ALU.mult))
            link(stt(r2, r, TWO_PI / 4, t1_, ALU.add, ALU.add))
            ts(r2, r2, PI_IN, -PI_IN, ALU.min, ALU.max).then_inc(dsc, 1)
            dve.wait_ge(trig, 4)
            link(v.tensor_copy(C[0], co))
            v.tensor_copy(C[1], si).then_inc(rot_u, 1)
            link(tt(abr, mag, co, ALU.mult))
            link(tt(abi, mag, si, ALU.mult))
            link(ts(am1, abr, -1.0, None, ALU.add))
            link(tt(den, a_re, a_re, ALU.mult))
            link(tt(t0_, a_im, a_im, ALU.mult))
            link(tt(den, den, t0_, ALU.add))
            link(v.reciprocal(den, den))
            link(tt(fre, am1, a_re, ALU.mult))
            link(tt(t0_, abi, a_im, ALU.mult))
            link(tt(fre, fre, t0_, ALU.add))
            link(tt(fre, fre, den, ALU.mult))
            link(tt(fim, abi, a_re, ALU.mult))
            link(tt(t0_, am1, a_im, ALU.mult))
            link(tt(fim, fim, t0_, ALU.subtract))
            link(tt(fim, fim, den, ALU.mult))
            dve.wait_ge(cT_ps, 2)
            link(v.tensor_copy(csT.rearrange("p j k -> p (j k)"), ps[:, 3, 0:XT * 24]))
            dve.wait_ge(x_ps, KD)
            v.tensor_copy(st5_flat, ps[:, 2, 0:256]).then_inc(par_ok, 1)

            dve.wait_ge(ld_rows, 16 * 6)
            b3 = [P // 2, S5T, S5C]
            btmp = part(gate_r, 4228, S5T, S5C)
            for gg in range(2):
                rr = slice(64 * gg, 64 * gg + 64)
                cc = slice(S5C * gg, S5C * gg + S5C)
                fr, fi = fre[rr].unsqueeze(2).to_broadcast(b3), fim[rr].unsqueeze(2).to_broadcast(b3)
                for q, (x, y, op) in enumerate(((0, 1, ALU.subtract), (1, 0, ALU.add))):
                    link(tt(btmp[rr], b_raw[rr, y], fi, ALU.mult))
                    link(tt(bblk[rr, q, :, cc], b_raw[rr, x], fr, ALU.mult))
                    link(tt(bblk[rr, q, :, cc], bblk[rr, q, :, cc], btmp[rr], op))
            dve.wait_ge(cT_ps, 1)
            for q, sign in enumerate((1.0, -1.0)):
                for hh in range(2):
                    link(ts(cblk[:, q, :, 64 * hh:64 * hh + 64], c_raw[:, q], par2[:, hh:hh + 1], sign, ALU.mult, ALU.mult))
            v.memset(npf[:, 0:1], 0.0).then_inc(blk5, 2)


            dve.wait_ge(sq_used, KD)
            link(v.memset(rows[:, :, 0:3], 0.0))
            for j in range(XT):
                row = rows[:, j % 2, :]
                acc = part(z_r, (j % 2) * 312, 312)
                srow = row[:, 259:315].rearrange("p (b l) -> p b l", l=7)
                link(v.tensor_copy(srow[:, :, 0:3], csT[:, j, :].rearrange("p (b k) -> p b k", k=3)))
                dve.wait_ge(tile_ev, T_XBC + j + 1)
                if j >= 2:
                    dve.wait_ge(conv_ok, 2 * (j - 1))
                elif j == 0:
                    dve.wait_ge(xn_ok, KD)
                link(ts(acc, row[:, 0:312], convw[:, 0, j:j + 1], convb[:, j:j + 1], ALU.mult, ALU.add))
                for k in range(1, CONV):
                    link(stt(acc, row[:, k:k + 312], convw[:, k, j:j + 1], acc, ALU.mult, ALU.add))
                link(v.tensor_copy(tails[:, j, 0:3], row[:, TP:TP + 3]))
                v.tensor_copy(tails[:, j, 3:27].rearrange("p (b k) -> p b k", k=3), srow[:, :, 4:7]).then_inc(conv_acc, 1)

            link(v.memset(dt3, 0.0))
            dve.wait_ge(dt_ps, 1)
            dve.wait_ge(ld_bc, 48)
            link(tt(dt3[:, 0:2, :], ps[:, 2, 0:2 * H].rearrange("p (i h) -> p i h", h=H),
                    dtb[:, :].unsqueeze(1).to_broadcast([P, 2, H]), ALU.add))
            tt(dt3[0:TS, 2, :], ps[0:TS, 2, 2 * H:3 * H], dtb[0:TS, :], ALU.add).then_inc(dt_pre, 1)
            dve.wait_ge(dt_exp, 1)
            link(stt(dt3, dt3, 0.0, dtt, ALU.max, ALU.add))
            stt(da3, dt3, -1.0, alog[:, :].unsqueeze(1).to_broadcast([P, 3, H]), ALU.mult, ALU.mult).then_inc(da_ok, 1)
            for q in range(4):
                dve.wait_ge(s5w_ps, q + 1)
                dst = (bT if q < 2 else cTs5)[:, q % 2]
                v.tensor_copy(dst.rearrange("p j m -> p (j m)"), ps[:, 3 + q, :]).then_inc(s5w_ok, 1)

            dve.wait_ge(rot_ok, 1)
            dve.wait_ge(conv_acc, XT)

            def s5_y_out(j):
                dve.wait_ge(s5_hused, 4 * j + 4)
                stt(uT[:, j, 0:TP], uT[:, j, 0:TP], s5d[:, j:j + 1], ps[:, 6 + j % 2, 0:TP], ALU.mult, ALU.add).then_inc(s5_yev, 1)

            for i in range(S5T):
                q = i % 2
                xr, xi = ps[:, 2 + 2 * q, :], ps[:, 3 + 2 * q, :]
                c_, s_ = rotc[:, i, :], rots[:, i, :]
                gr, gi = g5[:, 2 * q, :], g5[:, 2 * q + 1, :]
                dve.wait_ge(s5_x, i + 1)
                if i >= 2:
                    dve.wait_ge(s5_h, i - 1)
                link(tt(vt[:, 0, :], xr[:, 0:TP], c_, ALU.mult))
                link(tt(vt[:, 1, :], xi[:, 0:TP], s_, ALU.mult))
                link(tt(gr, vt[:, 0, :], vt[:, 1, :], ALU.add))
                link(tt(vt[:, 0, :], xi[:, 0:TP], c_, ALU.mult))
                link(tt(vt[:, 1, :], xr[:, 0:TP], s_, ALU.mult))
                link(tt(gi, vt[:, 0, :], vt[:, 1, :], ALU.subtract))
                link(v.tensor_copy(s5x[:, 0, i, :], xr[:, TP:T]))
                v.tensor_copy(s5x[:, 1, i, :], xi[:, TP:T]).then_inc(s5_xused, 1)
                m_ = mag[:, i:i + 1].to_broadcast([P, TP])
                link(v.tensor_tensor_scan(gr, m_, gr, 0.0, ALU.mult, ALU.add))
                v.tensor_tensor_scan(gi, m_, gi, 0.0, ALU.mult, ALU.add).then_inc(s5_g, 1)
                if i % 4 == 1 and i > 1:
                    s5_y_out(i // 4 - 1)
            dve.wait_ge(s5_xused, S5T)
            dve.wait_ge(s5_g, S5T)
            sh = [P, S5T, NBATCH]
            ar, ai = abr.unsqueeze(2).to_broadcast(sh), abi.unsqueeze(2).to_broadcast(sh)
            w0, w1_ = part(conv_r, 0, S5T, NBATCH), part(conv_r, P, S5T, NBATCH)
            xl = [s5x[:, q].rearrange("p i (b l) -> p i b l", l=LSAMP) for q in range(2)]
            hl = [s5h[:, q].rearrange("p i (b l) -> p i b l", l=LSAMP) for q in range(2)]
            prev = [st5[:, q].rearrange("p b i -> p i b") for q in range(2)]
            for l in range(LSAMP):
                for q, (x, y, op) in enumerate(((0, 1, ALU.subtract), (1, 0, ALU.add))):
                    link(tt(w0, prev[x], ar, ALU.mult))
                    link(tt(w1_, prev[y], ai, ALU.mult))
                    link(tt(w0, w0, w1_, op))
                    link(tt(hl[q][:, :, :, l], w0, xl[q][:, :, :, l], ALU.add))
                prev = [hl[q][:, :, :, l] for q in range(2)]
            link(v.tensor_copy(st5[:, 0].rearrange("p b i -> p i b"), prev[0]))
            dve.wait_ge(s5_h, S5T)
            v.tensor_copy(st5[:, 1].rearrange("p b i -> p i b"), prev[1]).then_inc(s5_hs, 1)
            s5_y_out(UT - 1)
            dve.wait_ge(s5_y, 1)
            for j in range(UT):
                last = stt(uT[:, j, TP:T], uT[:, j, TP:T], s5d[:, j:j + 1], ps[:, 2, j * TS:(j + 1) * TS], ALU.mult, ALU.add)
            last.then_inc(s5_yev, 1)

            def gated(j):
                dve.wait_ge(glu_sig, j + 1)
                dve.wait_ge(glu_ps, 2 * j + 2)
                tt(sq[:, j % 2, :], ps[:, 0, 0:T], sq[:, j % 2, :], ALU.mult).then_inc(glu_ev, 1)
                dve.wait_ge(glu_ev, 2 * j + 1)
                tt(gates[:, KD + j, :], gates[:, KD + j, :], sq[:, j % 2, :], ALU.mult).then_inc(glu_ev, 1)

            gated(0)
            dve.wait_ge(cb_ps, 1)
            for i, (c0, n) in enumerate(CHUNKS):
                if i == 2:
                    dve.wait_ge(acs_ps, 1)
                o_ = (i % 2) * 256
                mask = upper[:, :] if i < 2 else supper_r[0:TS, :]
                tt(CBm[0:n, :, c0:c0 + n], ps[0:n, 4 + i // 2, o_:o_ + 2 * n].rearrange("p (g q) -> p g q", g=G),
                   mask.unsqueeze(1).to_broadcast([n, G, n]), ALU.mult).then_inc(cb_ok, 1)
            dve.wait_ge(acs_ps, 1)
            p5 = ps[:, 5, 128:224].rearrange("p (i h) -> p i h", i=3)
            v.tensor_copy(acs[:, 0:2, :], p5[:, 0:2, :]).then_inc(acs_ok, 1)
            v.tensor_copy(acs[0:TS, 2, :], p5[0:TS, 2, :]).then_inc(acs_ok, 1)
            gated(1)
            dve.wait_ge(acs_ok, 3)
            link(tt(dte[:, 0:2, :], acs[:, 0:2, H:2 * H], acs[:, 0:2, 0:H], ALU.subtract))
            tt(dte[0:TS, 2, :], acs[0:TS, 2, H:2 * H], acs[0:TS, 2, 0:H], ALU.subtract).then_inc(dte_pre, 1)
            for i, (c0, n) in enumerate(CHUNKS):
                dve.wait_ge(xt_ps, i + 1)
                for q in range(2):
                    tt(Xdt[0:n, i, q * 512:(q + 1) * 512].rearrange("p (h d) -> p h d", d=HD),
                       ps[0:n, 6 + q, :].rearrange("p (h d) -> p h d", d=HD),
                       dt3[0:n, i, 8 * q:8 * q + 8].unsqueeze(2).to_broadcast([n, 8, HD]), ALU.mult).then_inc(xdt_ok, 1)
                gated(2 + i)
            gated(5)
            dve.wait_ge(st_ps, 2)
            dve.wait_ge(dte_ok, 1)
            for gr in range(G):
                hf3 = hfT[:, gr, :].rearrange("p (h d) -> p h d", d=HD)
                link(tt(hf3, h1T[:, gr, :].rearrange("p (h d) -> p h d", d=HD),
                        acs[:, 1, H + 8 * gr:H + 8 * gr + 8].unsqueeze(2).to_broadcast([P, 8, HD]), ALU.mult))
                tt(hfT[:, gr, :], hfT[:, gr, :], ps[:, 2 + gr, :], ALU.add).then_inc(hf_ok, 1)
            gated(6)
            dve.wait_ge(qs_ps, 1)
            dve.wait_ge(bm_ok, 2)
            tt(MTs[0:TS], ps[0:TS, 4, :].rearrange("p (h q) -> p h q", h=H),
               acs[0:TS, 2, 0:H].unsqueeze(2).to_broadcast([TS, H, TS]), ALU.subtract).then_inc(qs_diff, 1)
            dve.wait_ge(qs_diff, 1)
            tt(MTs[0:TS], MTs[0:TS], supper_r[0:TS, :].unsqueeze(1).to_broadcast([TS, H, TS]), ALU.mult).then_inc(qs_msk, 1)
            gated(7)
            dve.wait_ge(qs_exp, 1)
            for gr in range(G):
                ms = MTs[0:TS, gr * (H // G):(gr + 1) * (H // G), :]
                tt(ms, ms, CBm[0:TS, gr, TP:T].unsqueeze(1).to_broadcast([TS, H // G, TS]), ALU.mult).then_inc(qs_ok, 1)

            def decayed(hp):
                dve.wait_ge(h0_ps, 2 * hp + 2)
                hv = h0[hp % NH0]
                link(tt(hv, hv, sample(eft[:, hp, :])[:, :, LSAMP - 1:LSAMP].to_broadcast([P, NBATCH, NS]), ALU.mult))

            def renewed(hp):
                dve.wait_ge(ss_ps, hp + 1)
                h2v = h0[hp % NH0].rearrange("p (a b) n -> p a (b n)", a=2)
                tt(h2v, h2v, ps[:, 4:6, :], ALU.add).then_inc(ss_ok, 1)

            def y_out(j):
                dve.wait_ge(q_y, j + 1)
                if j:
                    dve.wait_ge(q_yev, j)
                link(stt(nt, xbcT[:, j, :], dskip[:, j:j + 1], ps[:, j % 2, 0:T], ALU.mult, ALU.add))
                link(tt(nt[:, TP:T], nt[:, TP:T], yoff[:, j, :], ALU.add))
                tt(zT[:, j, :], zT[:, j, :], nt, ALU.mult).then_inc(q_yev, 1)

            def group_normed(gr):
                norm_refine(nv, ny, nt, 2 + gr)
                for j in range(4 * gr, 4 * gr + 4):
                    stt(zT[:, j, :], zT[:, j, :], ssdw[:, j:j + 1], ny, ALU.mult, ALU.mult).then_inc(yn_ok, 1)
                dve.wait_ge(yn_ok, 4 * gr + 4)

            dve.wait_ge(tile_ev, NT)

            def off_decayed(hp):
                dve.wait_ge(yoT_ps, hp + 1)
                raw = ps[:, 7, 0:1]
                own = bass.AP(raw.tensor, raw.offset, [list(raw.ap[0]), [P + 4 * LSAMP, 2], [32 + LSAMP, 4], [1, LSAMP]])
                v4 = [t[:, hp, :].rearrange("p (r c l) -> p r c l", r=2, c=4) for t in (yoff, eft)]
                tt(v4[0], own, v4[1], ALU.mult).then_inc(yoff_ok, 1)

            for qd in range(4):
                dve.wait_ge(q_ps, qd + 1)
                if qd:
                    dve.wait_ge(q_y, 2 * qd)
                tt(MT.rearrange("p h (i q) -> p i h q", i=2), ps[:, 0:2, :].rearrange("p i (h q) -> p i h q", h=4),
                   acs[:, 0:2, 4 * qd:4 * qd + 4].unsqueeze(3).to_broadcast([P, 2, 4, CH]), ALU.subtract).then_inc(q_diff, 1)
                dve.wait_ge(q_diff, qd + 1)
                m3 = MT.rearrange("p h (i q) -> p h i q", i=2)
                tt(m3, m3, upper[:, :].unsqueeze(1).unsqueeze(1).to_broadcast([P, 4, 2, CH]), ALU.mult).then_inc(q_msk, 1)
                decayed(2 * qd)
                ada_copy(UNITS_OF[qd][0])
                gr = qd // 2
                dve.wait_ge(q_exp, 2 * qd + 1)
                tt(CTs, CTs, xbcT[:, KD + G + gr, CH:TP].unsqueeze(1).to_broadcast([P, 4, CH]), ALU.mult).then_inc(q_mt, 1)
                renewed(2 * qd)
                off_decayed(2 * qd)
                ada_add(UNITS_OF[qd][0])
                dve.wait_ge(q_exp, 2 * qd + 2)
                tt(MT, MT, CBm[:, gr, 0:TP].unsqueeze(1).to_broadcast([P, 4, TP]), ALU.mult).then_inc(q_mt, 1)
                decayed(2 * qd + 1)
                for u in UNITS_OF[qd][1:]:
                    ada_copy(u)
                if qd == 3:
                    dve.wait_ge(g0_ps, 1)
                    norm_var(6, D // G, nv)
                renewed(2 * qd + 1)
                off_decayed(2 * qd + 1)
                dve.wait_ge(yoff_ok, 2 * qd + 2)
                if qd == 3:
                    dve.wait_ge(q_yev, 6)
                    group_normed(0)
                y_out(2 * qd)
                y_out(2 * qd + 1)
                for u in UNITS_OF[qd][1:]:
                    ada_add(u)
            dve.wait_ge(q_yev, KD)
            dve.wait_ge(sq_used, 12)
            norm_var(5, D // G, nv)
            group_normed(1)
            ada_copy(10)
            dve.wait_ge(mod_ok, 10)
            scales(nw2, 32)
            for j in range(KD):
                dve.wait_ge(outa_ps, j + 1)
                link(tt(gates[:, j, :], gates[:, j, :], ps[:, j % 2, 0:T], ALU.mult))
                tt(gates[:, j, :], gates[:, j, :], gates[:, KD + j, :], ALU.add).then_inc(mrg_ok, 1)
                if j == 0:
                    ada_add(10)

            def residual(j, src, gate, done):
                link(stt(xT[:, j, 0:TP], src[:, 0:TP], mod[:, gate + j, 0:1], xT[:, j, 0:TP], ALU.mult, ALU.add))
                link(tt(sample(nt[:, 0:TS]), sample(src[:, TP:T]), per_sequence(mod[:, gate + j, 1:NC]), ALU.mult))
                tt(xT[:, j, TP:T], xT[:, j, TP:T], nt[:, 0:TS], ALU.add).then_inc(done, 1)

            dve.wait_ge(mix_ps, 1)
            link(v.memset(score, 0.0))
            link(v.memset(posm, -1.0))
            v.memset(yacc, 0.0).then_inc(cmb_ok, 8)
            for j in range(KD):
                dve.wait_ge(mix_ps, j + 1)
                residual(j, ps[:, 2 + j % 2, 0:T], 16, x1_ok)
            norm_scale(4, 20, D, nv, ny, nt, 4)
            dve.wait_ge(st_hp, 16)
            normalize(ny)
            modulate(24, 2)
            ada_copy(11)

            S = [r_[:, k, :].rearrange("p (c e) -> p c e", e=NE) for k in range(40)]
            m3_, g12 = [P, 3, NE], [P, 3 * NG, EPG]

            def col(k):
                return r_[:, k, 0:3]

            def wide(c3):
                return c3.unsqueeze(2).to_broadcast(m3_)

            dve.wait_ge(lg_ps, 1)
            link(v.tensor_copy(score[:, 0:2, :], ps[:, 6, 0:2 * NE].rearrange("p (c e) -> p c e", e=NE)))
            link(v.tensor_copy(score[0:TS, 2, :], ps[0:TS, 6, 2 * NE:3 * NE]))
            link(v.tensor_reduce(col(5), score, AX_X, ALU.max))
            tt(score, score, wide(col(5)), ALU.subtract).then_inc(sm_in, 1)
            ada_add(11)
            dve.wait_ge(sm_exp, 1)
            link(v.tensor_reduce(col(5), score, AX_X, ALU.add))
            link(v.reciprocal(col(5), col(5)))
            link(tt(score, score, wide(col(5)), ALU.mult))
            link(tt(sel, score, brt[:, :].unsqueeze(1).to_broadcast(m3_), ALU.add))
            s4 = r_[:, 1, :].rearrange("p (c e) -> p c e", e=EPG)
            e4 = [s4[:, :, k] for k in range(4)]
            q = [r_[:, 6 + k, 0:3 * NG] for k in range(8)]
            link(tt(q[0], e4[0], e4[1], ALU.max))
            link(tt(q[1], e4[0], e4[1], ALU.min))
            link(tt(q[2], e4[2], e4[3], ALU.max))
            link(tt(q[3], e4[2], e4[3], ALU.min))
            link(tt(q[4], q[0], q[2], ALU.max))
            link(tt(q[5], q[0], q[2], ALU.min))
            link(tt(q[6], q[1], q[3], ALU.max))
            link(tt(q[5], q[5], q[6], ALU.max))
            link(tt(q[4], q[4], q[5], ALU.add))

            def first_max(vals, key, m, one):
                n = vals.shape[-1]
                bc = [P, 3, n]
                link(v.tensor_reduce(m, vals, AX_X, ALU.max))
                link(tt(one, vals, m.unsqueeze(2).to_broadcast(bc), ALU.is_equal))
                link(tt(one, one, key.unsqueeze(1).to_broadcast(bc), ALU.mult))
                link(v.tensor_reduce(m, one, AX_X, ALU.max))
                link(tt(one, one, m.unsqueeze(2).to_broadcast(bc), ALU.is_equal))

            best = q[7]
            first_max(q[4].rearrange("p (c g) -> p c g", g=NG), keyg[:, :], col(5), best.rearrange("p (c g) -> p c g", g=NG))
            msk, one1, one2 = S[14], S[15], S[16]
            msk4 = r_[:, 14, :].rearrange("p (c e) -> p c e", e=EPG)
            link(tt(msk4, s4, best.unsqueeze(2).to_broadcast(g12), ALU.mult))
            link(ts(q[0], best, -1.0, BIG, ALU.add, ALU.mult))
            link(tt(msk4, msk4, q[0].unsqueeze(2).to_broadcast(g12), ALU.add))
            first_max(msk, keye[:, :], col(5), one1)
            link(stt(msk, one1, -BIG, msk, ALU.mult, ALU.add))
            first_max(msk, keye[:, :], col(5), one2)
            tt(s_all, one1, one2, ALU.add).then_inc(top_ok, 1)
            dve.wait_ge(top_ok, 1)
            link(tt(comb, score, s_all, ALU.mult))
            link(v.tensor_reduce(col(5), comb, AX_X, ALU.add))
            link(v.reciprocal(col(5), col(5)))
            link(tt(comb, comb, wide(col(5)), ALU.mult))
            b4 = [P, 3, 2, CAP]

            def choose(q, v_, first, after=None):
                if not first:
                    dve.wait_ge(xg_ps[1], v_)
                    dve.wait_ge(selw_ok, v_)
                if after is not None:
                    dve.wait_ge(pos_dn, after)
                tt(selo, iota[:, :].unsqueeze(1).unsqueeze(1).to_broadcast(b4),
                   posm[:, :, bass.ds(2 * q, 2)].unsqueeze(3).to_broadcast(b4), ALU.is_equal).then_inc(selo_ok, 1)

            dve.wait_ge(pos_ps, 1)
            for rr, cc in ((P, slice(0, 2)), (TS, slice(2, 3))):
                pp = ps[0:rr, 7, 0:3 * NE].rearrange("p (c e) -> p c e", e=NE)[:, cc, :]
                link(stt(posm[0:rr, cc, :], pp, 1.0, s_all[0:rr, cc, :], ALU.add, ALU.mult))
            link(ts(posm, posm, -1.0, None, ALU.add))
            choose(0, 0, True)
            link(v.tensor_reduce(npf[:, 1:2], ps[:, 7, 48:64], AX_X, ALU.max))
            link(v.memset(npf[:, 2:3], 1.0))
            for k in range(1, MAXPASS):
                link(stt(npf[:, 2:3], npf[:, 1:2], float(CAP * k), npf[:, 2:3], ALU.is_gt, ALU.add))
            v.tensor_copy(npi[:, :], npf[:, 2:3]).then_inc(route_ok, 1)
            dve.wait_ge(route_ok, 1)

            def gathered_half(v_):
                dve.wait_ge(xg_ps[0], v_ + 1)
                v.tensor_copy(Xg[:, 0:512], ps[:, 0, :]).then_inc(xg_cp, 1)

            def add_up(v_):
                dve.wait_ge(cmb_ok, 8 * v_ + 8)
                for j in range(KD):
                    dve.wait_ge(cmb_ps, 8 * v_ + j + 1)
                    tt(yacc[:, j, :], yacc[:, j, :], ps[:, CMB_BANKS[j % 4], 0:T], ALU.add).then_inc(cmb_ok, 1)

            def experts(q, v_, first, prev, following):
                dve.wait_ge(selo_ok, v_ + 1)
                if not first:
                    dve.wait_ge(pT_ps, v_)
                tt(selw, selo, comb[:, :, bass.ds(2 * q, 2)].unsqueeze(3).to_broadcast(b4), ALU.mult).then_inc(selw_ok, 1)
                if following:
                    choose(q + 1, v_ + 1, False)
                if prev:
                    add_up(v_ - 1)
                dve.wait_ge(act_s, v_ + 1)
                dve.wait_ge(unit_used, N_UNITS + 6 * v_ + 4)
                if not first:
                    dve.wait_ge(aT_ps, v_)
                tt(act_e[:, :], hs_[:, :], ps[:, 3, :], ALU.mult).then_inc(act_ok, 1)
                if following:
                    gathered_half(v_ + 1)
                dve.wait_ge(pT_ps, v_ + 1)
                v.tensor_copy(pT[:, :], ps[:, 7, 0:T]).then_inc(pT_ok, 1)

            gathered_half(0)
            experts(0, 0, True, False, True)
            with dve.Fori(1, PAIRS - 1) as q_:
                experts(q_, q_, False, True, True)
            experts(PAIRS - 1, PAIRS - 1, False, True, False)
            add_up(PAIRS - 1)
            passes = dve.value_load(npi[0:1, 0:1], min_val=1, max_val=MAXPASS)
            with dve.If(passes > 1):
                with dve.Fori(1, passes) as n_:
                    v0 = n_ * PAIRS
                    dve.wait_ge(selo_ok, v0)
                    ts(posm, posm, -float(CAP), None, ALU.add).then_inc(pos_dn, 1)
                    choose(0, v0, False, n_)
                    gathered_half(v0)
                    experts(0, v0, False, False, True)
                    with dve.Fori(1, PAIRS - 1) as q_:
                        experts(q_, n_ * PAIRS + q_, False, True, True)
                    experts(PAIRS - 1, v0 + (PAIRS - 1), False, True, False)
                    add_up(v0 + (PAIRS - 1))

            dve.wait_ge(cmb_ok, 8 * PAIRS * passes + 8)
            dve.wait_ge(mod_ok, 12)
            ys = yacc[:, :, TP:T].rearrange("p j (b l) -> p j b l", l=LSAMP)
            link(tt(ys, ys, mod[:, 40:48, 1:NC].unsqueeze(3).to_broadcast([P, KD, NBATCH, LSAMP]), ALU.mult))
            link(tt(xT[:, :, TP:T], xT[:, :, TP:T], yacc[:, :, TP:T], ALU.add))
            for j in range(KD):
                stt(xT[:, j, 0:TP], yacc[:, j, 0:TP], mod[:, 40 + j, 0:1], xT[:, j, 0:TP], ALU.mult, ALU.add).then_inc(x2_ok, 1)
            link(v.memset(tok_v, 1.0))
            for j in range(1, KD):
                dve.wait_ge(sq_ok, 20 + j + 1)
                last = tt(sq_fin[:, 0, :], sq_fin[:, 0, :], sq_fin[:, j, :], ALU.add)
                if j < KD - 1:
                    link(last)
            last.then_inc(sq_ok, 1)
            dve.wait_ge(sq_used, 21)
            for rr, cc in ((P, slice(0, 2)), (TS, slice(2, 3))):
                link(ts(tok_v[0:rr, cc], ps[0:rr, 6, 0:6].rearrange("p (i k) -> p i k", k=2)[:, cc, 0], 1.0 / D, EPS, ALU.mult, ALU.add))
            v.tensor_copy(tok_v, tok_v).then_inc(var_ok, 1)
            dve.wait_ge(rs_ok, 5)
            link(tt(tok_t, tok_v, tok_rs, ALU.mult))
            link(tt(tok_t, tok_t, tok_rs, ALU.mult))
            link(ts(tok_t, tok_t, -0.5, 1.5, ALU.mult, ALU.add))
            tt(tok_rs, tok_rs, tok_t, ALU.mult).then_inc(fin_rs, 1)
            dve.wait_ge(fin_rs, 1)
            dve.wait_ge(fin_ps, 2)
            for i, (t0, n) in enumerate(CHUNKS):
                ts(y_tok[0:n, i, 512:D], ps[0:n, 2 * i + 1, :], tok_rs[0:n, i:i + 1], None, ALU.mult).then_inc(fin_cp, 1)


_OUTS = [("y_prompt", (1, TP, D)), ("y_sample", (NBATCH, LSAMP, D)),
         ("ssm_prompt", (1, 1, H, HD, NS)), ("ssm_sample", (1, NBATCH, H, HD, NS)),
         ("conv_prompt", (1, 1, CONV - 1, XBC)), ("conv_sample", (1, NBATCH, CONV - 1, XBC)),
         ("s5_re_prompt", (1, 1, S5G, S5N)), ("s5_re_sample", (1, NBATCH, S5G, S5N)),
         ("s5_im_prompt", (1, 1, S5G, S5N)), ("s5_im_sample", (1, NBATCH, S5G, S5N))]


def kernel(**inputs):
    import numpy as _np
    import concourse.bacc as _bacc
    from concourse import mybir as _mybir
    from concourse.bass_utils import run_bass_kernel_spmd as _run

    nc = _bacc.Bacc("TRN2", target_bir_lowering=False, num_devices=1, dynamic_dma_scratch_size=1024)
    arrays, a, o = {}, {}, {}
    for name, x in inputs.items():
        x = _np.ascontiguousarray(x)
        arrays[f"in_{name}"] = x
        a[name] = nc.dram_tensor(f"in_{name}", x.shape, _mybir.dt.from_np(x.dtype), kind="ExternalInput").ap()
    for name, shape in _OUTS:
        o[name] = nc.dram_tensor(f"out_{name}", shape, _mybir.dt.float32, kind="ExternalOutput").ap()
    hybrid_decoder_step(nc, a, o)
    r = _run(nc, [arrays], core_ids=[0])
    return tuple(r.results[0][f"out_{name}"] for name, _ in _OUTS)
```
